# Optimizing a Trainium2 kernel written in Bass

```python
import math
import jax, jax.numpy as jnp
from jax import lax
import numpy as np

D_MODEL = 1024
BATCH = 1
SEQ = 512
DEPTH = 1
DEC_BATCH = 8
DEC_SEQ = 4
PAST_LEN = 4096
PAGE_SIZE = 128

MLSTM_WIDTH = D_MODEL // 2
MLSTM_HEADS = 4
MLSTM_DK = MLSTM_WIDTH // MLSTM_HEADS
MLSTM_DV = MLSTM_WIDTH // MLSTM_HEADS
CONV_WIDTH = D_MODEL - MLSTM_WIDTH
CONV_KERNEL = 31
CONV_GROUPS = 8
MIX_WIDTH = MLSTM_WIDTH + CONV_WIDTH
CHUNK = 64
IN_COLS = 4 * MLSTM_WIDTH + 2 * MLSTM_HEADS + 2 * CONV_WIDTH
PEER_HEADS = 8
N_KEYS = 128
N_EXPERTS = N_KEYS * N_KEYS
PEER_TOPK = 16
PEER_KEY_DIM = 256
PEER_HALF = PEER_KEY_DIM // 2
PEER_BLOCK = 256
EPS = 1e-6

kernel_name = 'hymba_mlstm_conformer_peer_step'

def rmsnorm(x, gain):
    x32 = x.astype(jnp.float32)
    y = x32 * lax.rsqrt(jnp.mean(x32 * x32, axis=-1, keepdims=True) + EPS)
    return (y * gain.astype(jnp.float32)).astype(x.dtype)

def group_norm(x, gain, bias):
    B, T, C = x.shape
    x32 = x.astype(jnp.float32).reshape(B, T, CONV_GROUPS, C // CONV_GROUPS)
    mu = jnp.mean(x32, axis=-1, keepdims=True)
    var = jnp.mean(jnp.square(x32 - mu), axis=-1, keepdims=True)
    y = ((x32 - mu) * lax.rsqrt(var + EPS)).reshape(B, T, C)
    return (y * gain.astype(jnp.float32) + bias.astype(jnp.float32)).astype(x.dtype)

def _chunk_len(T):
    for L in range(min(CHUNK, T), 0, -1):
        if T % L == 0:
            return L

def mlstm_chunkwise(q, k, v, i_pre, f_pre, C0, n0, m0):
    B, H, T, DK = q.shape
    DV = v.shape[-1]
    L = _chunk_len(T)
    NC = T // L
    k = k * (DK ** -0.5)
    log_f = jax.nn.log_sigmoid(f_pre)

    def to_chunks(a):
        return jnp.moveaxis(a.reshape(B, H, NC, L, *a.shape[3:]), 2, 0)

    causal = jnp.tril(jnp.ones((L, L), dtype=bool))

    def step(carry, inp):
        C, n, m = carry
        qc, kc, vc, ic, fc = inp
        b = jnp.cumsum(fc, axis=-1)
        D = b[..., :, None] - b[..., None, :] + ic[..., None, :]
        D = jnp.where(causal, D, -jnp.inf)
        inter = b + m[..., None]
        m_t = jnp.maximum(inter, jnp.max(D, axis=-1))
        w_intra = jnp.exp(D - m_t[..., None])
        w_inter = jnp.exp(inter - m_t)
        S = jnp.einsum('bhtd,bhsd->bhts', qc, kc) * w_intra
        num = w_inter[..., None] * jnp.einsum('bhtd,bhde->bhte', qc, C) + jnp.einsum('bhts,bhse->bhte', S, vc)
        den = w_inter * jnp.einsum('bhtd,bhd->bht', qc, n) + jnp.sum(S, axis=-1)
        h = num / jnp.maximum(jnp.abs(den), jnp.exp(-m_t))[..., None]
        m_new = m_t[..., -1]
        w_state = jnp.exp(b[..., -1:] - b + ic - m_new[..., None])
        decay = jnp.exp(b[..., -1] + m - m_new)
        C_new = decay[..., None, None] * C + jnp.einsum('bhs,bhsd,bhse->bhde', w_state, kc, vc)
        n_new = decay[..., None] * n + jnp.einsum('bhs,bhsd->bhd', w_state, kc)
        return (C_new, n_new, m_new), h

    (C1, n1, m1), h = lax.scan(step, (C0, n0, m0),
                               (to_chunks(q), to_chunks(k), to_chunks(v), to_chunks(i_pre), to_chunks(log_f)))
    h = jnp.moveaxis(h, 0, 2).reshape(B, H, T, DV)
    return h, C1, n1, m1

def hybrid_mixer(xn, w_in, b_gates, w_dw, b_dw, gn_gain, gn_bias, w_out, C0, n0, m0, buf0):
    B, T, _ = xn.shape
    H, W = MLSTM_HEADS, MLSTM_WIDTH
    p = xn @ w_in
    q = p[..., 0:W]
    k = p[..., W:2 * W]
    v = p[..., 2 * W:3 * W]
    o = p[..., 3 * W:4 * W]
    gates = p[..., 4 * W:4 * W + 2 * H].astype(jnp.float32) + b_gates.astype(jnp.float32)
    a = p[..., 4 * W + 2 * H:4 * W + 2 * H + CONV_WIDTH]
    g = p[..., 4 * W + 2 * H + CONV_WIDTH:]

    def heads(t):
        return t.reshape(B, T, H, -1).transpose(0, 2, 1, 3).astype(jnp.float32)

    h, C1, n1, m1 = mlstm_chunkwise(heads(q), heads(k), heads(v),
                                    gates[..., :H].transpose(0, 2, 1), gates[..., H:].transpose(0, 2, 1),
                                    C0.astype(jnp.float32), n0.astype(jnp.float32), m0.astype(jnp.float32))
    h = h.transpose(0, 2, 1, 3).reshape(B, T, W).astype(xn.dtype) * jax.nn.sigmoid(o)

    u = a * jax.nn.sigmoid(g)
    full = jnp.concatenate([buf0.astype(u.dtype), u], axis=1)
    c = lax.conv_general_dilated(full, w_dw[:, None, :].astype(u.dtype), window_strides=(1,), padding='VALID',
                                 dimension_numbers=('NWC', 'WIO', 'NWC'), feature_group_count=CONV_WIDTH) + b_dw
    c = jax.nn.silu(group_norm(c, gn_gain, gn_bias))
    out = jnp.concatenate([h, c], axis=-1) @ w_out
    new_buf = full[:, T:]
    return out, C1, n1, m1, new_buf

def peer_ffn(xn, w_query, keys1, keys2, u_tab, v_tab):
    B, T, D = xn.shape
    n = B * T
    blk = min(PEER_BLOCK, n)
    pad = (-n) % blk
    xb = jnp.pad(xn.reshape(n, D), ((0, pad), (0, 0))).reshape(-1, blk, D)
    k1 = keys1.astype(jnp.float32)
    k2 = keys2.astype(jnp.float32)

    def one_block(xt):
        q = (xt @ w_query).reshape(blk, PEER_HEADS, PEER_KEY_DIM).astype(jnp.float32)
        s1 = jnp.einsum('nhd,hkd->nhk', q[..., :PEER_HALF], k1)
        s2 = jnp.einsum('nhd,hkd->nhk', q[..., PEER_HALF:], k2)
        sc1, i1 = lax.top_k(s1, PEER_TOPK)
        sc2, i2 = lax.top_k(s2, PEER_TOPK)
        cand = (sc1[..., :, None] + sc2[..., None, :]).reshape(blk, PEER_HEADS, PEER_TOPK * PEER_TOPK)
        top_sc, top_c = lax.top_k(cand, PEER_TOPK)
        e1 = jnp.take_along_axis(i1, top_c // PEER_TOPK, axis=-1)
        e2 = jnp.take_along_axis(i2, top_c % PEER_TOPK, axis=-1)
        experts = e1 * N_KEYS + e2
        gate = jax.nn.softmax(top_sc, axis=-1)
        u_sel = u_tab[experts]
        act = jax.nn.gelu(jnp.einsum('nd,nhkd->nhk', xt, u_sel).astype(jnp.float32), approximate=False)
        z = (gate * act).astype(xt.dtype)
        return jnp.einsum('nhk,nhkd->nd', z, v_tab[experts])

    out = lax.map(one_block, xb).reshape(-1, D)[:n]
    return out.reshape(B, T, D)

def setup_inputs(seed: int = 0) -> dict:
    key = jax.random.key(seed)
    ks = jax.random.split(key, 24)
    f32 = jnp.float32
    nrm = lambda k, s: jax.random.normal(k, s, dtype=f32)
    x_prompt = nrm(ks[0], (BATCH, SEQ, D_MODEL))
    x_sample = nrm(ks[1], (DEC_BATCH, DEC_SEQ, D_MODEL))
    state_C = 0.1 * nrm(ks[2], (DEPTH, DEC_BATCH, MLSTM_HEADS, MLSTM_DK, MLSTM_DV))
    state_n = 0.5 * nrm(ks[3], (DEPTH, DEC_BATCH, MLSTM_HEADS, MLSTM_DK))
    state_m = nrm(ks[4], (DEPTH, DEC_BATCH, MLSTM_HEADS))
    state_conv = 0.5 * nrm(ks[5], (DEPTH, DEC_BATCH, CONV_KERNEL - 1, CONV_WIDTH))
    norm_mix = 1.0 + 0.02 * nrm(ks[6], (DEPTH, D_MODEL))
    w_in = nrm(ks[7], (DEPTH, D_MODEL, IN_COLS)) * D_MODEL ** -0.5
    b_i = 0.1 * nrm(ks[8], (DEPTH, MLSTM_HEADS))
    b_f = 3.0 + 0.5 * nrm(ks[9], (DEPTH, MLSTM_HEADS))
    b_gates = jnp.concatenate([b_i, b_f], axis=-1)
    w_dw = nrm(ks[10], (DEPTH, CONV_KERNEL, CONV_WIDTH)) * CONV_KERNEL ** -0.5
    b_dw = 0.02 * nrm(ks[11], (DEPTH, CONV_WIDTH))
    gn_gain = 1.0 + 0.02 * nrm(ks[12], (DEPTH, CONV_WIDTH))
    gn_bias = 0.02 * nrm(ks[13], (DEPTH, CONV_WIDTH))
    w_out = nrm(ks[14], (DEPTH, MIX_WIDTH, D_MODEL)) * MIX_WIDTH ** -0.5
    norm_ffn = 1.0 + 0.02 * nrm(ks[15], (DEPTH, D_MODEL))
    w_query = nrm(ks[16], (DEPTH, D_MODEL, PEER_HEADS * PEER_KEY_DIM)) * D_MODEL ** -0.5
    keys1 = nrm(ks[17], (DEPTH, PEER_HEADS, N_KEYS, PEER_HALF)) * PEER_HALF ** -0.5
    keys2 = nrm(ks[18], (DEPTH, PEER_HEADS, N_KEYS, PEER_HALF)) * PEER_HALF ** -0.5
    u_experts = nrm(ks[19], (DEPTH, N_EXPERTS, D_MODEL)) * D_MODEL ** -0.5
    v_experts = 0.1 * nrm(ks[20], (DEPTH, N_EXPERTS, D_MODEL))
    norm_final = 1.0 + 0.02 * nrm(ks[21], (D_MODEL,))
    return {'x_prompt': x_prompt, 'x_sample': x_sample,
            'state_C': state_C, 'state_n': state_n, 'state_m': state_m, 'state_conv': state_conv,
            'norm_mix': norm_mix, 'w_in': w_in, 'b_gates': b_gates, 'w_dw': w_dw, 'b_dw': b_dw,
            'gn_gain': gn_gain, 'gn_bias': gn_bias, 'w_out': w_out, 'norm_ffn': norm_ffn,
            'w_query': w_query, 'keys1': keys1, 'keys2': keys2, 'u_experts': u_experts,
            'v_experts': v_experts, 'norm_final': norm_final}

def reference(x_prompt, x_sample, state_C, state_n, state_m, state_conv, norm_mix, w_in, b_gates, w_dw, b_dw,
              gn_gain, gn_bias, w_out, norm_ffn, w_query, keys1, keys2, u_experts, v_experts, norm_final):
    xp, xs = x_prompt, x_sample
    Bp = xp.shape[0]
    pC, pn, pm, pcv, sC, sn, sm, scv = [], [], [], [], [], [], [], []
    for l in range(DEPTH):
        mix_w = (w_in[l], b_gates[l], w_dw[l], b_dw[l], gn_gain[l], gn_bias[l], w_out[l])
        C0 = jnp.zeros((Bp, MLSTM_HEADS, MLSTM_DK, MLSTM_DV), state_C.dtype)
        n0 = jnp.zeros((Bp, MLSTM_HEADS, MLSTM_DK), state_n.dtype)
        m0 = jnp.zeros((Bp, MLSTM_HEADS), state_m.dtype)
        b0 = jnp.zeros((Bp, CONV_KERNEL - 1, CONV_WIDTH), state_conv.dtype)
        mo, C1, n1, m1, bf1 = hybrid_mixer(rmsnorm(xp, norm_mix[l]), *mix_w, C0, n0, m0, b0)
        xp = xp + mo
        xp = xp + peer_ffn(rmsnorm(xp, norm_ffn[l]), w_query[l], keys1[l], keys2[l], u_experts[l], v_experts[l])
        pC.append(C1.astype(state_C.dtype)); pn.append(n1.astype(state_n.dtype))
        pm.append(m1.astype(state_m.dtype)); pcv.append(bf1.astype(state_conv.dtype))
        mo, C2, n2, m2, bf2 = hybrid_mixer(rmsnorm(xs, norm_mix[l]), *mix_w,
                                           state_C[l], state_n[l], state_m[l], state_conv[l])
        xs = xs + mo
        xs = xs + peer_ffn(rmsnorm(xs, norm_ffn[l]), w_query[l], keys1[l], keys2[l], u_experts[l], v_experts[l])
        sC.append(C2.astype(state_C.dtype)); sn.append(n2.astype(state_n.dtype))
        sm.append(m2.astype(state_m.dtype)); scv.append(bf2.astype(state_conv.dtype))
    y_prompt = rmsnorm(xp, norm_final)
    y_sample = rmsnorm(xs, norm_final)
    prompt_C, prompt_n, prompt_m, prompt_conv = jnp.stack(pC), jnp.stack(pn), jnp.stack(pm), jnp.stack(pcv)
    sample_C, sample_n, sample_m, sample_conv = jnp.stack(sC), jnp.stack(sn), jnp.stack(sm), jnp.stack(scv)
    return (y_prompt, y_sample, prompt_C, prompt_n, prompt_m, prompt_conv, sample_C, sample_n, sample_m, sample_conv)


_drawn_inputs = setup_inputs


def setup_inputs(seed=0):
    import zlib

    import numpy as np

    out = dict(_drawn_inputs(seed))
    spreads = {}
    factors = {'b_dw': 3.539, 'gn_gain': 5.921, 'gn_bias': 7.27, 'norm_ffn': 8.0, 'norm_final': 2.741}
    for name, (base, spread) in spreads.items():
        noise = np.random.default_rng([zlib.crc32(name.encode()), seed]).standard_normal(out[name].shape)
        drawn = base * np.exp(spread * noise) if base else spread * noise
        out[name] = __import__('jax').numpy.asarray(drawn.astype(out[name].dtype))
    for name, factor in factors.items():
        out[name] = (out[name] * factor).astype(out[name].dtype)
    return out
```

```python
import concourse.bass as bass
from concourse import mybir
from contextlib import ExitStack

D = 1024
KC = D // 128
SEQ, NB, NT = 512, 8, 4
NS = NB * NT
H = 4
CC = 4
TAPS = 31
HIST = TAPS - 1
QC = 16
PH = 8
TOPK = 16
PICKS = PH * TOPK
EPS = 1e-6
NEG = -1e30
LOW = -3e38

PAIRS = [(0, 1, 16, 0), (1, 1, 8, 16), (2, 1, 5, 24), (3, 1, 4, 29), (4, 1, 3, 33), (5, 3, 2, 36), (8, 8, 1, 42)]
CAND = 50
HITS = 8

TILES = [(NS, 0, 0), (128, NS, 0), (128, 0, 1), (128, 128, 1), (128, 256, 1)]
GROUPS = [(0, 1), (2, 3, 4)]
WIDTH = [NS + 128, 384]
GMAX = 384
XN_SLOT = [0, 1, 2, 3, 0]

N_IN, N_OUT = 24, 8
N_W = N_IN + N_OUT + QC
W_SLOTS = 4
KINDS_IN = [("g", c) if h == 0 else ("a", c) for c in range(CC) for h in range(2)] + \
           [("o", c) for c in range(H)] + [("k", c) for c in range(H)] + \
           [("q", c) for c in range(H)] + [("v", c) for c in range(H)]

U_SLOTS, V_SLOTS = 8, 4
N_PICK = [PICKS * NS // 128] + [PICKS] * 4
FIRST_PICK = [sum(N_PICK[:t]) for t in range(5)]
BLOCK = 8


def pp_jobs():
    jobs = []
    for g, tiles in enumerate(GROUPS):
        jobs += [("xT", t, half) for t in tiles for half in range(2)]
        jobs += [("gate_i", g), ("gate_f", g)]
        jobs += [("in", g, i) for i in range(N_IN)]
        jobs += [("mean", g, c) for c in range(CC)] + [("var", g, c) for c in range(CC)]
        for t in tiles:
            jobs += [("kTr", t), ("hT", t)]
        jobs += [("out", g, j) for j in range(N_OUT)]
        jobs += [("x2T", t, half) for t in tiles for half in range(2)]
        for c in range(QC):
            jobs += [("query", g, c), ("score", g, c)]
    return {name: n for n, name in enumerate(jobs)}


class Steps:

    def __init__(self, engine, sem):
        self.engine, self.sem, self.n = engine, sem, 0

    def __call__(self, ins):
        self.n += 1
        ins.then_inc(self.sem, 1)

    def done(self, but=0):
        if self.n - but > 0:
            self.engine.wait_ge(self.sem, self.n - but)


def build(nc, a, o):
    f32, u32 = mybir.dt.float32, mybir.dt.uint32
    ALU, ACT, AX = mybir.AluOpType, mybir.ActivationFunctionType, mybir.AxisListType
    ds = bass.ds
    J = pp_jobs()

    with ExitStack() as ctx:
        def sb(name, shape, dt=f32):
            return ctx.enter_context(nc.sbuf_tensor(name, shape, dt))

        def sem(name):
            return ctx.enter_context(nc.semaphore(name))

        def view(region_, at, **dims):
            n = 1
            for d in dims.values():
                n *= d
            flat = region_[:, at:at + n]
            if len(dims) == 1:
                return flat
            names = " ".join(dims)
            return flat.rearrange(f"p ({names}) -> p {names}", **dims)

        W = sb("w_ring", [128, W_SLOTS, KC, 128])
        x = sb("x_res", [128, 5, D])
        xn = sb("x_normed", [128, 4, D])
        xnT = sb("x_normed_T", [128, KC, GMAX])
        v = sb("v_rows", [128, 3, H, 128])
        sigo = sb("sig_o", [128, 3, H, 128])
        up = sb("u_prompt", [128, CC, HIST + GMAX])
        mixT = sb("mix_T", [128, KC, GMAX])
        region = sb("region", [128, 3 * QC * 128])
        qT = view(region, 0, h=H, n=GMAX)
        kT = view(region, H * GMAX, h=H, n=GMAX)
        cv = view(region, 2 * H * GMAX, c=CC, n=GMAX)
        ct = view(region, 3 * H * GMAX, c=CC, n=GMAX)
        score = view(region, 0, t=3, c=QC, k=128)
        qry = mixT[:, 0:2, :]
        u_ring = sb("u_ring", [128, U_SLOTS * D])
        v_ring = sb("v_ring", [128, V_SLOTS * D])
        U = [u_ring[:, s * D:(s + 1) * D] for s in range(U_SLOTS)]
        V = [v_ring[:, s * D:(s + 1) * D] for s in range(V_SLOTS)]
        Cs = view(u_ring, 0, h=H, b=NB, e=128)
        us = view(v_ring, 0, c=CC, b=NB, w=HIST + NT)
        vm = [view(v_ring, 1088 + 1024 * i, b=NB, e=128) for i in range(2)]
        BT = view(v_ring, 3136, h=H, n=NS)
        Cp = sb("C_prompt", [128, H, 128])
        keys = sb("keys_T", [128, QC, 128])
        gain = sb("gain", [128, D])
        rowsIF = sb("rows_if", [4, 2, GMAX])
        scratch = sb("scratch", [128, 2480])
        att = view(scratch, 0, h=H, n=128)
        num = view(scratch, 512, h=H, e=128)
        kw = view(scratch, 1024, h=H, e=128)
        R = view(scratch, 1536, k=7, n=128)[0:4]
        lf = scratch[0:4, 1536:1536 + GMAX]
        topv = view(scratch, 0, c=QC, k=TOPK)
        topi = view(scratch, 256, c=QC, k=TOPK)
        topf = view(scratch, 512, c=QC, k=TOPK)
        cand = view(scratch, 768, h=PH, c=CAND)
        ceid = view(scratch, 1168, h=PH, c=CAND)
        best = view(scratch, 1568, h=PH, k=TOPK)
        pos = view(scratch, 1696, h=PH, k=TOPK)
        posf = view(scratch, 1824, h=PH, k=TOPK)
        hit = view(scratch, 1952, k=HITS, c=CAND)
        eid = scratch[:, 2352:2480]
        idx = sb("expert_idx", [128, 2, PICKS], u32)
        sub = sb("score_minus_max", [128, 2, PICKS])
        dots = sb("dots", [128, 2, PICKS])
        z = sb("z", [128, 2, PICKS])
        idxS = sb("expert_idx_spread", [128, N_PICK[0]], u32)
        subS = sb("score_spread", [128, N_PICK[0]])
        u_idx = sb("u_idx_now", [128, 2, BLOCK], u32)
        v_idx = sb("v_idx_now", [128, 2, BLOCK], u32)
        diag = sb("diag", [128, V_SLOTS, 128])
        ident = sb("ident", [128, 128])
        fold = sb("fold", [128, NS])
        halves = sb("halves", [128, 128])
        negP = sb("neg_prompt", [128, 128])
        negS = sb("neg_sample", [NS, NS])
        sel = sb("sel", [4, H, 128])
        bmask = sb("batch_mask", [NS, NB])
        ones = sb("ones", [128, 1])
        iota_i = sb("iota_i", [128, CAND], mybir.dt.int32)
        iota = sb("iota", [128, CAND])
        zero = sb("zero", [4, 1])
        keepS = sb("keep_sample", [4, NS])
        dropS = sb("drop_sample", [4, NS])
        eps = sb("eps", [128, 1])
        gmix = sb("gain_mix", [128, KC])
        wg = sb("w_gates", [128, KC, 2 * H])
        bi = sb("b_i", [4, 1])
        bf = sb("b_f", [4, 1])
        wdw = sb("w_dw", [128, CC, TAPS])
        bdw = sb("b_dw", [128, CC])
        gng = sb("gn_gain", [128, CC])
        gnb = sb("gn_bias", [128, CC])
        npr = sb("n_prompt", [128, H])
        nsm = sb("n_sample", [128, H, NB])
        m0 = sb("m_sample", [4, NB])
        mprev = sb("m_prompt", [4, 1])
        mlast = sb("M_last", [4, NB])
        decR = sb("decay_rows", [4, NB])
        cols = sb("cols", [128, 4, H])
        dec = sb("decay", [128, H * NB])
        dtmp = sb("den_tmp", [128, H, NB])
        den = sb("den", [128, H])
        ss = sb("sum_squares", [128, 3, 5])
        rstd = sb("rstd", [128, 3, 5])
        zsum = sb("z_sum", [128, PH])
        credit = sb("credit", [128, 2])

        pp = [ctx.enter_context(nc.psum_tensor(f"pp{i}", [128, 512], f32)) for i in range(2)]
        pa = [ctx.enter_context(nc.psum_tensor(f"pa{i}", [128, 512], f32)) for i in range(4)]
        yps = ctx.enter_context(nc.psum_tensor("y", [128, D], f32))
        pM, pA = pa[0], pa[0]
        pK, pC = pa[1], pa[1]
        pB, pS = pa[2], pa[3]
        DEC, DA, DB, DN = 16, 48, 52, 84

        ld_x = [sem(f"ld_x{t}") for t in range(5)]
        ld_small, ld_keys, ld_state, ld_gains = sem("ld_small"), sem("ld_keys"), sem("ld_state"), sem("ld_gains")
        w_land = [sem(f"w_land{s}") for s in range(W_SLOTS)]
        consts = sem("consts")
        pp_full, pp_free = sem("pp_full"), [sem(f"pp_free{i}") for i in range(2)]
        sumsq1, rstd1, xs_ready = sem("sumsq1"), sem("rstd1"), sem("xs_ready")
        neg_f, log_f = sem("neg_f"), sem("log_f")
        u_ready, centred, squared, normed = sem("u_ready"), sem("centred"), sem("squared"), sem("normed")
        mix_c, conv_done, hist_ready = sem("mix_c"), sem("conv_done"), sem("hist_ready")
        rows_set, rows_exp = sem("rows_set"), sem("rows_exp")
        att_in, att_e, att_w, att_p = sem("att_in"), sem("att_e"), sem("att_w"), sem("att_p")
        att_b, att_a, att_c, att_done = sem("att_b"), sem("att_a"), sem("att_c"), sem("att_done")
        bt_copied, bt_back, vm_ready, cs_new, cs_added = (
            sem("bt_copied"), sem("bt_back"), sem("vm_ready"), sem("cs_new"), sem("cs_added"))
        hs_ready, den_read = sem("hs_ready"), sem("den_read")
        sumsq2, xn_ready = sem("sumsq2"), sem("xn_ready")
        spread_x, spread_i = sem("spread_x"), sem("spread_i")
        scores_read, picked = sem("scores_read"), sem("picked")
        u_land = [sem(f"u_land{s}") for s in range(U_SLOTS)]
        v_land = [sem(f"v_land{s}") for s in range(V_SLOTS)]
        u_free, v_done, diag_ready = sem("u_free"), sem("v_done"), sem("diag_ready")
        staged = sem("staged")
        z_act, z_ready = sem("z_act"), sem("z_ready")
        sumsq3, y_ready = sem("sumsq3"), sem("y_ready")
        out_s, out_p, out_y = sem("out_s"), sem("out_p"), sem("out_y")
        s_act, s_dve, s_pool = sem("s_act"), sem("s_dve"), sem("s_pool")
        N_CONST = 21

        def filled(eng, job):
            eng.wait_ge(pp_full, J[job] + 1)

        def evacuated(eng, job):
            eng.wait_ge(pp_free[J[job] % 2], J[job] // 2 + 1)

        def bank(job):
            return pp[J[job] % 2]

        def free(job):
            return pp_free[J[job] % 2]

        def weight_job(n):
            g, i = divmod(n, N_W)
            if i < N_IN:
                return "in", g, i
            return ("out", g, i - N_IN) if i < N_IN + N_OUT else ("query", g, i - N_IN - N_OUT)

        block = ctx.enter_context(nc.Block())

        @block.sync
        def _(sp):
            def load_x(t):
                rows = TILES[t][0]
                src = a["x_sample"] if t == 0 else a["x_prompt"][(t - 1) * 128:t * 128, :]
                sp.dma_start(x[0:rows, t, :], src).then_inc(ld_x[t], 16)

            def load_w(n):
                if n >= W_SLOTS:
                    sp.wait_ge(pp_full, J[weight_job(n - W_SLOTS)] + 1)
                sp.dma_start(W[:, n % W_SLOTS, :, :], a["w_all"][n % N_W]).then_inc(w_land[n % W_SLOTS], 16)

            load_x(0)
            load_x(1)
            sp.dma_start(gmix[:, :], a["gain_mix"]).then_inc(ld_small, 16)
            sp.dma_start(wg[:, :, :], a["w_gates"]).then_inc(ld_small, 16)
            sp.dma_start(bi[:, :], a["b_gates"][0:H, :]).then_inc(ld_small, 16)
            sp.dma_start(bf[:, :], a["b_gates"][H:2 * H, :]).then_inc(ld_small, 16)
            for n in range(W_SLOTS):
                load_w(n)
            for dst, name in ((wdw[:, :, :], "w_dw"), (bdw[:, :], "b_dw"), (gng[:, :], "gn_gain"),
                              (gnb[:, :], "gn_bias"), (m0[:, :], "state_m"), (nsm[:, :, :], "state_n"),
                              (us[:, :, :, 0:HIST], "conv_hist")):
                sp.dma_start(dst, a[name]).then_inc(ld_small, 16)
            for t in (2, 3, 4):
                load_x(t)
            sp.dma_start(Cs, a["state_C"]).then_inc(ld_state, 16)
            sp.dma_start(keys[:, :, :], a["keys_T"]).then_inc(ld_keys, 16)
            sp.dma_start(gain[:, :], a["norm_ffn"].broadcast_to([128, D])).then_inc(ld_gains, 16)
            for n in range(W_SLOTS, N_W):
                load_w(n)
            sp.wait_ge(u_ready, 1)
            sp.dma_start(o["conv_s"], us[:, :, :, NT:NT + HIST]).then_inc(out_s, 16)
            sp.wait_ge(att_done, 1)
            sp.dma_start(o["C_s"], Cs).then_inc(out_s, 16)
            sp.dma_start(o["n_s"], nsm[:, :, :]).then_inc(out_s, 16)
            sp.dma_start(o["m_s"], m0[:, :]).then_inc(out_s, 16)
            sp.wait_ge(xn_ready, 1)
            for s in range(1, 4):
                sp.dma_start(xn[NS * s:NS * (s + 1), 0, :], xn[0:NS, 0, :]).then_inc(spread_x, 16)
            sp.wait_ge(picked, 1)
            for s in range(4):
                part = slice(N_PICK[0] * s, N_PICK[0] * (s + 1))
                sp.dma_start(idxS[NS * s:NS * (s + 1), :], idx[0:NS, 0, part]).then_inc(spread_i, 16)
                sp.dma_start(subS[NS * s:NS * (s + 1), :], sub[0:NS, 0, part]).then_inc(spread_i, 16)
            for n in range(N_W, 2 * N_W):
                load_w(n)
            sp.wait_ge(u_ready, 2)
            sp.dma_start(o["conv_p"], up[:, :, GMAX:GMAX + HIST]).then_inc(out_p, 16)
            sp.wait_ge(att_done, 5)
            sp.dma_start(o["C_p"], Cp[:, :, :]).then_inc(out_p, 16)
            sp.dma_start(o["n_p"], npr[:, :]).then_inc(out_p, 16)
            sp.dma_start(o["m_p"], mprev[:, :]).then_inc(out_p, 16)
            sp.wait_ge(xn_ready, 5)
            sp.dma_start(gain[:, :], a["norm_final"].broadcast_to([128, D])).then_inc(ld_gains, 16)
            for t in range(5):
                sp.wait_ge(y_ready, t + 1)
                dst = o["y_s"] if t == 0 else o["y_p"][(t - 1) * 128:t * 128, :]
                sp.dma_start(dst, x[0:TILES[t][0], t, :]).then_inc(out_y, 16)
            sp.wait_ge(out_y, 16 * 5)
            sp.wait_ge(out_s, 16 * 4)
            sp.wait_ge(out_p, 16 * 4)

        @block.gpsimd
        def _(pool):
            step = Steps(pool, s_pool)
            for t, value in ((ident, 0.0), (fold, 0.0), (halves, 1.0 / 64), (negP, 0.0), (negS, 0.0),
                             (bmask, 1.0), (dropS, 0.0), (keepS, 1.0)):
                step(pool.memset(t[:, :], value))
            step(pool.memset(sel[:, :, :], 0.0))
            step.done()
            n_const = [0]

            def const(ins):
                n_const[0] += 1
                ins.then_inc(consts, 1)

            const(pool.affine_select(out=ident[:, :], in_=ident[:, :], compare_op=ALU.not_equal, fill=1.0,
                                     base=0, pattern=[[-1, 128]], channel_multiplier=1))
            step(pool.affine_select(out=negS[:, :], in_=negS[:, :], compare_op=ALU.is_ge, fill=NEG,
                                    base=0, pattern=[[-4, NB], [0, NT]], channel_multiplier=1))
            step(pool.affine_select(out=bmask[:, :], in_=bmask[:, :], compare_op=ALU.is_ge, fill=0.0,
                                    base=0, pattern=[[-4, NB]], channel_multiplier=1))
            step(pool.iota(iota_i[:, :], [[1, CAND]], base=0, channel_multiplier=0))
            const(pool.affine_select(out=negP[:, :], in_=negP[:, :], compare_op=ALU.is_ge, fill=NEG,
                                     base=0, pattern=[[1, 128]], channel_multiplier=-1))
            const(pool.affine_select(out=sel[:, :, :], in_=sel[:, :, :], compare_op=ALU.not_equal, fill=1.0,
                                     base=0, pattern=[[-1, H], [0, 128]], channel_multiplier=1))
            for at, base, mul in ((0, 63, -1), (64, -64, 1)):
                const(pool.affine_select(out=halves[:, at:at + 64], in_=halves[:, at:at + 64], compare_op=ALU.is_ge,
                                         fill=0.0, base=base, pattern=[[0, 64]], channel_multiplier=mul))
            const(pool.memset(keepS[:, :].rearrange("p (b t) -> p b t", t=NT)[:, :, 0:1], 0.0))
            const(pool.memset(dropS[:, :].rearrange("p (b t) -> p b t", t=NT)[:, :, 0:1], NEG))
            const(pool.memset(ones[:, :], 1.0))
            const(pool.memset(eps[:, :], EPS))
            const(pool.memset(up[:, :, 0:HIST], 0.0))
            const(pool.memset(zero[:, :], 0.0))
            const(pool.memset(npr[:, :], 0.0))
            const(pool.memset(mprev[:, :], 0.0))
            const(pool.memset(Cp[:, :, :], 0.0))
            for i in range(3):
                const(pool.memset(ss[:, i, :], 1.0))
            step.done()
            const(pool.affine_select(out=negS[:, :], in_=negS[:, :], compare_op=ALU.is_ge, fill=NEG,
                                     base=0, pattern=[[4, NB], [1, NT]], channel_multiplier=-1))
            const(pool.affine_select(out=bmask[:, :], in_=bmask[:, :], compare_op=ALU.is_ge, fill=0.0,
                                     base=NT - 1, pattern=[[4, NB]], channel_multiplier=-1))
            const(pool.tensor_copy(iota[:, :], iota_i[:, :]))
            for s in range(4):
                ins = pool.affine_select(out=fold[:, :], in_=fold[:, :], compare_op=ALU.not_equal, fill=1.0,
                                         base=-NS * s, pattern=[[-1, NS]], channel_multiplier=1)
                if s < 3:
                    step(ins)
                    step.done()
                else:
                    const(ins)
            assert n_const[0] == N_CONST
            pool.wait_ge(consts, N_CONST)

            turns = [0]

            def gathers(t, table, now, ring, slots, land, freed):
                src = idxS if t == 0 else idx[:, t % 2, :]
                first, base = FIRST_PICK[t], turns[0]
                with pool.Fori(0, N_PICK[t] // (2 * BLOCK)) as i:
                    for h in range(2):
                        pool.tensor_copy(now[:, h, :], src[:, ds(i * 2 * BLOCK + h * BLOCK, BLOCK)]).then_inc(staged, 1)
                        pool.wait_ge(staged, i * 2 + (base + h + 1))
                        for r in range(BLOCK):
                            s = r % slots
                            pool.wait_ge(freed, i * 2 * BLOCK + (h * BLOCK + r + first + 1))
                            pool.nop(nofuse=True)
                            pool.indirect_dma_start(
                                out=ring[s], out_offset=None, in_=table,
                                in_offset=bass.IndirectOffsetOnAxis(ap=now[:, h, r:r + 1], axis=0)
                            ).then_inc(land[s], 16)
                turns[0] += N_PICK[t] // BLOCK

            pool.wait_ge(out_s, 16 * 4)
            for t in range(5):
                if t == 0:
                    pool.wait_ge(spread_i, 16 * 8)
                else:
                    pool.wait_ge(picked, t + 1)
                gathers(t, a["u_experts"], u_idx, U, U_SLOTS, u_land, u_free)
                gathers(t, a["v_experts"], v_idx, V, V_SLOTS, v_land, v_done)

        @block.tensor
        def _(pe):
            def job(name):
                n = J[name]
                if n >= 2:
                    pe.wait_ge(pp_free[n % 2], n // 2)
                return pp[n % 2]

            def transposes(name, src, rows, cols_of, count):
                p = job(name)
                for i in range(count):
                    ins = pe.transpose(p[:, i * 128:i * 128 + rows], cols_of(src, i), ident[0:rows, 0:rows])
                ins.then_inc(pp_full, 1)

            def weights(n):
                pe.wait_ge(w_land[n % W_SLOTS], 16 * (n // W_SLOTS + 1))
                return W[:, n % W_SLOTS, :, :]

            def project(name, g, n, actT, rows_out):
                w = weights(n)
                p = job(name)
                if rows_out:
                    parts = [(i, TILES[t][0], TILES[t][1]) for i, t in enumerate(GROUPS[g])]
                else:
                    parts = [(0, 128, 0)]
                for i, rows, col in parts:
                    for k in range(KC):
                        if rows_out:
                            ins = pe.matmul(p[0:rows, i * 128:(i + 1) * 128], actT[:, k, col:col + rows], w[:, k, :],
                                            start=(k == 0), stop=(k == KC - 1))
                        else:
                            ins = pe.matmul(p[:, 0:WIDTH[g]], w[:, k, :], actT[:, k, 0:WIDTH[g]],
                                            start=(k == 0), stop=(k == KC - 1))
                ins.then_inc(pp_full, 1)

            def inputs(g):
                for t in GROUPS[g]:
                    rows = TILES[t][0]
                    pe.wait_ge(xs_ready, t + 1)
                    for half in range(2):
                        transposes(("xT", t, half), xn, rows,
                                   lambda s, i, t=t, half=half, rows=rows:
                                   s[0:rows, XN_SLOT[t], (4 * half + i) * 128:(4 * half + i + 1) * 128], 4)
                for t in GROUPS[g]:
                    for half in range(2):
                        evacuated(pe, ("xT", t, half))
                if g == 0:
                    pe.wait_ge(ld_small, 16 * 11)
                for kind, at in (("gate_i", 0), ("gate_f", H)):
                    p = job((kind, g))
                    for k in range(KC):
                        ins = pe.matmul(p[0:H, 0:WIDTH[g]], wg[:, k, at:at + H], xnT[:, k, 0:WIDTH[g]],
                                        start=(k == 0), stop=(k == KC - 1))
                    ins.then_inc(pp_full, 1)
                for i, (kind, _) in enumerate(KINDS_IN):
                    project(("in", g, i), g, g * N_W + i, xnT, kind in "ov")

            def conv_stats(g):
                n = WIDTH[g]
                pe.wait_ge(conv_done, g + 1)
                for c in range(CC):
                    p = job(("mean", g, c))
                    pe.matmul(p[:, 0:n], halves[:, :], cv[:, c, 0:n], start=True, stop=True).then_inc(pp_full, 1)
                for c in range(CC):
                    pe.wait_ge(squared, CC * g + c + 1)
                    p = job(("var", g, c))
                    pe.matmul(p[:, 0:n], halves[:, :], ct[:, c, 0:n], start=True, stop=True).then_inc(pp_full, 1)

            def attention(t):
                rows, col, g = TILES[t]
                nb = NB if t == 0 else 1
                slot = t - GROUPS[g][0]
                span = slice(col, col + rows)
                pe.wait_ge(rows_exp, t + 1)
                if t >= 1:
                    pe.wait_ge(att_done, t)
                for kind, k in enumerate((1, 3, 4, 5)):
                    pe.transpose(pS[0:rows, 4 * kind:4 * kind + 4], R[:, k, 0:rows], ident[0:4, 0:4])
                for h in range(H):
                    pe.matmul(pS[:, DEC + h * nb:DEC + (h + 1) * nb], sel[:, h, :], decR[:, 0:nb], start=True, stop=True)
                for h in range(H):
                    pe.matmul(pM[0:rows, h * 128:h * 128 + rows], sel[:, h, 0:rows], R[:, 2, 0:rows], start=True, stop=True)
                for h in range(H):
                    ins = pe.matmul(pK[0:rows, h * 128:h * 128 + rows], kT[:, h, span], qT[:, h, span], start=True, stop=True)
                ins.then_inc(att_in, 1)
                if t == 0:
                    pe.wait_ge(ld_state, 16)
                    for h in range(H):
                        for b in range(NB):
                            pe.matmul(pB[:, h * NS + NT * b:h * NS + NT * (b + 1)], Cs[:, h, b, :],
                                      qT[:, h, NT * b:NT * (b + 1)], start=True, stop=True)
                    pe.wait_ge(att_e, t + 1)
                    for h in range(H):
                        ins = pe.matmul(pS[0:rows, DB + h * NB:DB + (h + 1) * NB], qT[:, h, 0:NS], nsm[:, h, :],
                                        start=True, stop=True)
                    ins.then_inc(att_b, 1)
                    pe.wait_ge(bt_copied, 1)
                    for h in range(H):
                        ins = pe.transpose(pB[0:NS, h * 128:(h + 1) * 128], BT[:, h, :], ident[:, :])
                    ins.then_inc(bt_back, 1)
                else:
                    for h in range(H):
                        pe.matmul(pB[:, h * 128:(h + 1) * 128], qT[:, h, span], Cp[:, h, :], start=True, stop=True)
                    pe.wait_ge(att_e, t + 1)
                    for h in range(H):
                        ins = pe.matmul(pS[:, DB + h:DB + h + 1], qT[:, h, span], npr[:, h:h + 1], start=True, stop=True)
                    ins.then_inc(att_b, 1)
                p = job(("kTr", t))
                for h in range(H):
                    ins = pe.transpose(p[0:rows, h * 128:(h + 1) * 128], kT[:, h, span], ident[:, :])
                ins.then_inc(pp_full, 1)
                pe.wait_ge(att_p, t + 1)
                for h in range(H):
                    pe.matmul(pA[0:rows, h * 128:(h + 1) * 128], att[0:rows, h, 0:rows], v[0:rows, slot, h, :],
                              start=True, stop=True)
                for h in range(H):
                    ins = pe.matmul(pS[0:rows, DA + h:DA + h + 1], att[0:rows, h, 0:rows], ones[0:rows, :],
                                    start=True, stop=True)
                ins.then_inc(att_a, 1)
                evacuated(pe, ("kTr", t))
                pe.wait_ge(den_read, t + 1)
                if t == 0:
                    for h in range(H):
                        pe.wait_ge(vm_ready, h + 1)
                        if h:
                            pe.wait_ge(cs_added, h)
                        for half in range(2):
                            pe.matmul(yps[:, half * 512:(half + 1) * 512], kw[0:NS, h, :],
                                      vm[h % 2][0:NS, 4 * half:4 * half + 4, :].rearrange("p b e -> p (b e)"),
                                      start=True, stop=True)
                        pe.matmul(pS[:, DN + h * NB:DN + (h + 1) * NB], kw[0:NS, h, :], bmask[:, :],
                                  start=True, stop=True).then_inc(cs_new, 1)
                else:
                    for h in range(H):
                        pe.matmul(pC[:, h * 128:(h + 1) * 128], kw[:, h, :], v[:, slot, h, :], start=True, stop=True)
                    for h in range(H):
                        ins = pe.matmul(pS[:, DN + h:DN + h + 1], kw[:, h, :], ones[:, :], start=True, stop=True)
                    ins.then_inc(att_c, 1)
                pe.wait_ge(hs_ready, t + 1)
                transposes(("hT", t), num, rows, lambda s, h, rows=rows: s[0:rows, h, :], H)

            def outputs(g):
                pe.wait_ge(mix_c, CC * (g + 1))
                for t in GROUPS[g]:
                    evacuated(pe, ("hT", t))
                for j in range(N_OUT):
                    project(("out", g, j), g, g * N_W + N_IN + j, mixT, True)

            def queries(g):
                for t in GROUPS[g]:
                    rows = TILES[t][0]
                    pe.wait_ge(xn_ready, t + 1)
                    for half in range(2):
                        transposes(("x2T", t, half), xn, rows,
                                   lambda s, i, t=t, half=half, rows=rows:
                                   s[0:rows, XN_SLOT[t], (4 * half + i) * 128:(4 * half + i + 1) * 128], 4)
                for t in GROUPS[g]:
                    for half in range(2):
                        evacuated(pe, ("x2T", t, half))
                if g == 0:
                    pe.wait_ge(ld_keys, 16)
                for c in range(QC):
                    project(("query", g, c), g, g * N_W + N_IN + N_OUT + c, xnT, False)
                    p = job(("score", g, c))
                    evacuated(pe, ("query", g, c))
                    for i, t in enumerate(GROUPS[g]):
                        rows, col, _ = TILES[t]
                        ins = pe.matmul(p[0:rows, i * 128:(i + 1) * 128], qry[:, c % 2, col:col + rows], keys[:, c, :],
                                        start=True, stop=True)
                    ins.then_inc(pp_full, 1)

            def experts(t):
                rows, _, g = TILES[t]
                if t:
                    pe.wait_ge(y_ready, t)
                for half in range(2):
                    pe.matmul(yps[0:rows, half * 512:(half + 1) * 512], ident[0:rows, 0:rows],
                              x[0:rows, t, half * 512:(half + 1) * 512], start=True, stop=True, skip_group_check=True)
                first = FIRST_PICK[t]
                with pe.Fori(0, N_PICK[t] // BLOCK) as i:
                    for r in range(BLOCK):
                        s = r % V_SLOTS
                        pe.wait_ge(v_land[s], i * (16 * BLOCK // V_SLOTS) + 16 * (first // V_SLOTS + r // V_SLOTS + 1))
                        pe.wait_ge(diag_ready, i * BLOCK + (first + r + 1))
                        for half in range(2):
                            ins = pe.matmul(yps[0:rows, half * 512:(half + 1) * 512], diag[:, s, 0:rows],
                                            V[s][:, half * 512:(half + 1) * 512], start=False, stop=True,
                                            skip_group_check=True)
                        ins.then_inc(v_done, 1)

            pe.wait_ge(consts, N_CONST)
            inputs(0)
            evacuated(pe, ("in", 0, N_IN - 1))
            evacuated(pe, ("in", 0, N_IN - 2))
            conv_stats(0)
            attention(0)
            attention(1)
            outputs(0)
            queries(0)
            inputs(1)
            experts(0)
            evacuated(pe, ("in", 1, N_IN - 1))
            evacuated(pe, ("in", 1, N_IN - 2))
            conv_stats(1)
            for t in GROUPS[1]:
                attention(t)
            outputs(1)
            queries(1)
            for t in range(1, 5):
                experts(t)

        @block.scalar
        def _(act):
            step = Steps(act, s_act)
            A = act.activation

            def norm1(g):
                for t in GROUPS[g]:
                    rows = TILES[t][0]
                    act.wait_ge(ld_x[t], 16)
                    step.done()
                    step(A(xn[0:rows, XN_SLOT[t] if g == 0 else 2, :], x[0:rows, t, :], ACT.Square, accum_out=ss[0:rows, 0, t:t + 1]))
                step.done()
                lo, hi = GROUPS[g][0], GROUPS[g][-1] + 1
                A(ss[:, 0, lo:hi], ss[:, 0, lo:hi], ACT.Sqrt, bias=eps[:, :], scale=1.0 / D).then_inc(sumsq1, 1)

            def scale_x(g):
                act.wait_ge(rstd1, g + 1)
                for t in GROUPS[g]:
                    rows = TILES[t][0]
                    if t == 4:
                        act.wait_ge(u_free, U_SLOTS + N_PICK[0])
                    A(xn[0:rows, XN_SLOT[t], :], x[0:rows, t, :], ACT.Copy, scale=rstd[0:rows, 0, t:t + 1]).then_inc(xs_ready, 1)

            def spread_T(name, t, half, gain):
                rows, col, _ = TILES[t]
                job = (name, t, half)
                filled(act, job)
                if gain:
                    for i in range(4):
                        k = 4 * half + i
                        ins = A(xnT[:, k, col:col + rows], bank(job)[:, i * 128:i * 128 + rows], ACT.Copy, scale=gmix[:, k:k + 1])
                else:
                    ins = A(xnT[:, 4 * half:4 * half + 4, col:col + rows],
                            bank(job)[:, :].rearrange("p (i n) -> p i n", i=4)[:, :, 0:rows], ACT.Copy)
                ins.then_inc(free(job), 1)

            def inputs(g):
                n = WIDTH[g]
                scale_x(g)
                if g == 0:
                    act.wait_ge(ld_small, 16 * 11)
                for t in GROUPS[g]:
                    for half in range(2):
                        spread_T("xT", t, half, True)
                for at, (kind, bias) in enumerate((("gate_i", bi), ("gate_f", bf))):
                    job = (kind, g)
                    filled(act, job)
                    A(rowsIF[:, at, 0:n], bank(job)[0:H, 0:n], ACT.Identity, bias=bias[:, :]).then_inc(free(job), 1)
                if g == 1:
                    act.wait_ge(scores_read, 2)
                    act.wait_ge(hist_ready, 1)
                for i, (kind, c) in enumerate(KINDS_IN):
                    job = ("in", g, i)
                    p = bank(job)
                    filled(act, job)
                    if kind == "g":
                        ins = A(ct[:, c, 0:n], p[:, 0:n], ACT.Sigmoid)
                    elif kind == "a" and g == 0:
                        step(A(us[:, c, :, HIST:], p[:, 0:NS].rearrange("p (b t) -> p b t", t=NT), ACT.Copy))
                        ins = A(up[:, c, HIST:HIST + 128], p[:, NS:n], ACT.Copy)
                    elif kind == "a":
                        ins = A(up[:, c, HIST:HIST + n], p[:, 0:n], ACT.Copy)
                    elif kind == "k":
                        ins = A(kT[:, c, 0:n], p[:, 0:n], ACT.Copy, scale=128 ** -0.5)
                    elif kind == "q":
                        ins = A(qT[:, c, 0:n], p[:, 0:n], ACT.Copy)
                    else:
                        dst, f = (v, ACT.Copy) if kind == "v" else (sigo, ACT.Sigmoid)
                        if g == 0:
                            step(A(dst[0:NS, 0, c, :], p[0:NS, 0:128], f))
                            ins = A(dst[:, 1, c, :], p[:, 128:256], f)
                        else:
                            ins = A(dst[:, 0:3, c, :], p[:, 0:384].rearrange("p (t e) -> p t e", t=3), f)
                    ins.then_inc(free(job), 1)
                if g == 0:
                    norm1(1)

            def mixer(g):
                n = WIDTH[g]
                act.wait_ge(neg_f, g + 1)
                step(A(lf[:, 0:n], lf[:, 0:n], ACT.Exp))
                step.done()
                A(lf[:, 0:n], lf[:, 0:n], ACT.Ln, bias=1.0).then_inc(log_f, 1)
                for c in range(CC):
                    act.wait_ge(centred, CC * g + c + 1)
                    A(ct[:, c, 0:n], cv[:, c, 0:n], ACT.Square).then_inc(squared, 1)
                for c in range(CC):
                    job = ("var", g, c)
                    filled(act, job)
                    A(ct[:, c, 0:n], bank(job)[:, 0:n], ACT.Sqrt, bias=eps[:, :]).then_inc(free(job), 1)
                for c in range(CC):
                    act.wait_ge(normed, CC * g + c + 1)
                    A(mixT[:, CC + c, 0:n], cv[:, c, 0:n], ACT.Silu, bias=gnb[:, c:c + 1], scale=gng[:, c:c + 1]).then_inc(mix_c, 1)
                for t in GROUPS[g]:
                    rows, col, _ = TILES[t]
                    nb = NB if t == 0 else 1
                    act.wait_ge(rows_set, t + 1)
                    step(A(R[:, 3:6, 0:rows], R[:, 3:6, 0:rows], ACT.Exp))
                    A(decR[:, 0:nb], decR[:, 0:nb], ACT.Exp).then_inc(rows_exp, 1)
                    if t == 0:
                        act.wait_ge(att_b, 1)
                        A(BT, pB[:, 0:H * NS].rearrange("p (h n) -> p h n", h=H), ACT.Copy).then_inc(bt_copied, 1)
                    act.wait_ge(att_e, t + 1)
                    for h in range(H):
                        ins = A(att[0:rows, h, 0:rows], att[0:rows, h, 0:rows], ACT.Exp, bias=cols[0:rows, 0, h:h + 1])
                    ins.then_inc(att_w, 1)
                    job = ("hT", t)
                    filled(act, job)
                    A(mixT[:, 0:H, col:col + rows], bank(job)[:, :].rearrange("p (h n) -> p h n", h=H)[:, :, 0:rows],
                      ACT.Copy).then_inc(free(job), 1)
                for t in GROUPS[g]:
                    rows = TILES[t][0]
                    evacuated(act, ("out", g, N_OUT - 1))
                    evacuated(act, ("out", g, N_OUT - 2))
                    if t == 4:
                        act.wait_ge(u_free, U_SLOTS + N_PICK[0])
                    step(A(xn[0:rows, XN_SLOT[t], :], x[0:rows, t, :], ACT.Square, accum_out=ss[0:rows, 1, t:t + 1]))
                    step.done()
                    A(ss[0:rows, 1, t:t + 1], ss[0:rows, 1, t:t + 1], ACT.Sqrt, bias=eps[0:rows, :], scale=1.0 / D).then_inc(sumsq2, 1)

            def queries(g):
                n = WIDTH[g]
                for t in GROUPS[g]:
                    for half in range(2):
                        spread_T("x2T", t, half, False)
                for c in range(QC):
                    job = ("query", g, c)
                    filled(act, job)
                    A(qry[:, c % 2, 0:n], bank(job)[:, 0:n], ACT.Copy).then_inc(free(job), 1)
                    job = ("score", g, c)
                    filled(act, job)
                    if g == 0:
                        step(A(score[0:NS, 0, c, :], bank(job)[0:NS, 0:128], ACT.Copy))
                        ins = A(score[:, 1, c, :], bank(job)[:, 128:256], ACT.Copy)
                    else:
                        ins = A(score[:, 0:3, c, :], bank(job)[:, 0:384].rearrange("p (t k) -> p t k", t=3), ACT.Copy)
                    ins.then_inc(free(job), 1)

            def gates(t):
                n = N_PICK[t]
                s = subS[:, :] if t == 0 else sub[:, t % 2, :]
                act.wait_ge(u_free, U_SLOTS + FIRST_PICK[t] + n)
                if t == 0:
                    act.wait_ge(spread_i, 16 * 8)
                step(A(s, s, ACT.Exp))
                A(dots[:, t % 2, 0:n], dots[:, t % 2, 0:n], ACT.Gelu).then_inc(z_act, 1)

            def diagonals(t):
                src = fold if t == 0 else ident
                w = NS if t == 0 else 128
                first = FIRST_PICK[t]
                act.wait_ge(z_ready, t + 1)
                with act.Fori(0, N_PICK[t] // BLOCK) as i:
                    for r in range(BLOCK):
                        act.wait_ge(v_done, i * BLOCK + (first + r + 1))
                        A(diag[:, r % V_SLOTS, 0:w], src[:, 0:w], ACT.Copy,
                          scale=z[:, t % 2, ds(i * BLOCK + r, 1)]).then_inc(diag_ready, 1)

            def final(t):
                rows = TILES[t][0]
                act.wait_ge(v_done, V_SLOTS + FIRST_PICK[t] + N_PICK[t])
                step(A(x[0:rows, t, :], yps[0:rows, :], ACT.Square, accum_out=ss[0:rows, 2, t:t + 1]))
                step.done()
                A(ss[0:rows, 2, t:t + 1], ss[0:rows, 2, t:t + 1], ACT.Sqrt, bias=eps[0:rows, :], scale=1.0 / D).then_inc(sumsq3, 1)

            act.wait_ge(consts, N_CONST)
            norm1(0)
            inputs(0)
            mixer(0)
            queries(0)
            inputs(1)
            gates(0)
            diagonals(0)
            final(0)
            mixer(1)
            queries(1)
            for t in range(1, 5):
                gates(t)
                diagonals(t)
                final(t)

        @block.vector
        def _(dve):
            step = Steps(dve, s_dve)

            def bc(ap, axis, shape):
                return ap.unsqueeze(axis).broadcast_to(shape)

            def conv(g):
                if g == 0:
                    parts = [(us, slice(0, NS), True), (up, slice(NS, WIDTH[0]), False)]
                else:
                    parts = [(up, slice(0, GMAX), False)]
                for j in range(TAPS):
                    for c in range(CC):
                        for src, span, sample in parts:
                            out = cv[:, c, span]
                            if sample:
                                win = src[:, c, :, j:j + NT]
                                out = out.rearrange("p (b t) -> p b t", t=NT)
                            else:
                                win = src[:, c, j:j + span.stop - span.start]
                            if j == 0:
                                step(dve.tensor_scalar(out, win, wdw[:, c, 0:1], bdw[:, c:c + 1], ALU.mult, ALU.add))
                            else:
                                step.done(but=len(parts) * CC - 1)
                                step(dve.scalar_tensor_tensor(out=out, in0=win, scalar=wdw[:, c, j:j + 1], in1=out,
                                                              op0=ALU.mult, op1=ALU.add))
                step.done()
                dve.nop(nofuse=True).then_inc(conv_done, 1)

            def root1(g):
                dve.wait_ge(sumsq1, g + 1)
                lo, hi = GROUPS[g][0], GROUPS[g][-1] + 1
                dve.reciprocal(rstd[:, 0, lo:hi], ss[:, 0, lo:hi]).then_inc(rstd1, 1)

            def mixer_first(g):
                n = WIDTH[g]
                evacuated(dve, ("gate_f", g))
                evacuated(dve, ("gate_i", g))
                dve.scalar_tensor_tensor(out=lf[:, 0:n], in0=rowsIF[:, 1, 0:n], scalar=-1.0, in1=rowsIF[:, 1, 0:n],
                                         op0=ALU.mult, op1=ALU.min).then_inc(neg_f, 1)
                last = ("in", g, 2 * CC - 1)
                evacuated(dve, last)
                evacuated(dve, ("in", g, 2 * CC - 2))
                if g == 0:
                    step(dve.tensor_tensor(us[:, :, :, HIST:], us[:, :, :, HIST:],
                                           ct[:, :, 0:NS].rearrange("p c (b t) -> p c b t", t=NT), ALU.mult))
                    dve.tensor_tensor(up[:, :, HIST:HIST + 128], up[:, :, HIST:HIST + 128], ct[:, :, NS:n],
                                      ALU.mult).then_inc(u_ready, 1)
                else:
                    dve.tensor_tensor(up[:, :, HIST:HIST + n], up[:, :, HIST:HIST + n], ct[:, :, 0:n],
                                      ALU.mult).then_inc(u_ready, 1)
                dve.wait_ge(u_ready, g + 1)
                step.done()
                conv(g)
                dve.wait_ge(log_f, g + 1)
                step(dve.scalar_tensor_tensor(out=rowsIF[:, 1, 0:n], in0=rowsIF[:, 1, 0:n], scalar=0.0, in1=lf[:, 0:n],
                                              op0=ALU.min, op1=ALU.subtract))
                step.done()
                if g == 0:
                    root1(1)
                    dve.tensor_copy(up[:, :, 0:HIST], up[:, :, 128:128 + HIST]).then_inc(hist_ready, 1)
                for c in range(CC):
                    job = ("mean", g, c)
                    filled(dve, job)
                    step(dve.tensor_tensor(cv[:, c, 0:n], cv[:, c, 0:n], bank(job)[:, 0:n], ALU.subtract))
                    step.done()
                    dve.nop(nofuse=True).then_inc(centred, 1)
                    dve.nop(nofuse=True).then_inc(free(job), 1)
                for c in range(CC):
                    evacuated(dve, ("var", g, c))
                    step(dve.reciprocal(ct[:, c, 0:n], ct[:, c, 0:n]))
                    step.done()
                    dve.tensor_tensor(cv[:, c, 0:n], cv[:, c, 0:n], ct[:, c, 0:n], ALU.mult).then_inc(normed, 1)

            def rows_of(t):
                rows, col, g = TILES[t]
                b, gg, M, gx = (R[:, i, 0:rows] for i in (0, 1, 2, 6))
                span = slice(col, col + rows)
                sample = t == 0
                bt = (lambda ap: ap.rearrange("p (b t) -> p b t", t=NT))
                step(dve.tensor_tensor_scan(b, keepS[:, :] if sample else ones[0:4, :].broadcast_to([4, rows]), rowsIF[:, 1, span], 0.0,
                                            ALU.mult, ALU.add))
                step.done()
                step(dve.tensor_tensor(gg, rowsIF[:, 0, span], b, ALU.subtract))
                step.done()
                if sample:
                    step(dve.tensor_copy(gx, gg))
                    step.done()
                    first = bt(gx)[:, :, 0:1]
                    step(dve.tensor_tensor(first, first, m0[:, :].unsqueeze(2), ALU.max))
                    step.done()
                    step(dve.tensor_tensor_scan(M, dropS[:, :], gx, NEG, ALU.add, ALU.max))
                    step.done()
                    last = bt(M)[:, :, NT - 1:NT]
                    lastb = bt(b)[:, :, NT - 1:NT]
                    step(dve.tensor_copy(mlast[:, :].unsqueeze(2), last))
                    step.done()
                    carried = bc(m0[:, :], 2, [4, NB, NT])
                    step(dve.tensor_tensor(bt(R[:, 3, 0:rows]), carried, bt(M), ALU.subtract))
                    step(dve.tensor_tensor(bt(R[:, 5, 0:rows]), bt(gg), bc(mlast[:, :], 2, [4, NB, NT]), ALU.subtract))
                    step(dve.tensor_tensor(decR[:, :], m0[:, :], mlast[:, :], ALU.subtract))
                    step.done()
                    step(dve.tensor_tensor(m0[:, :].unsqueeze(2), last, lastb, ALU.add))
                else:
                    step(dve.tensor_tensor_scan(M, zero[:, :].broadcast_to([4, rows]), gg, mprev[:, :], ALU.add, ALU.max))
                    step.done()
                    step(dve.tensor_scalar(R[:, 3, 0:rows], M, -1.0, mprev[:, :], ALU.mult, ALU.add))
                    step(dve.tensor_scalar(R[:, 5, 0:rows], gg, M[:, rows - 1:rows], None, ALU.subtract))
                    step(dve.tensor_tensor(decR[:, 0:1], mprev[:, :], M[:, rows - 1:rows], ALU.subtract))
                    step.done()
                    step(dve.tensor_tensor(mprev[:, :], M[:, rows - 1:rows], b[:, rows - 1:rows], ALU.add))
                dve.scalar_tensor_tensor(out=R[:, 4, 0:rows], in0=M, scalar=-1.0, in1=b, op0=ALU.mult,
                                         op1=ALU.subtract).then_inc(rows_set, 1)

            def attention(t):
                rows, col, g = TILES[t]
                nb = NB if t == 0 else 1
                slot = t - GROUPS[g][0]
                full = [rows, H, 128]
                if t >= 1:
                    evacuated(dve, ("hT", t - 1))
                dve.wait_ge(att_in, t + 1)
                step(dve.tensor_copy(cols[0:rows, :, :], pS[0:rows, 0:16].rearrange("p (k h) -> p k h", h=H)))
                step(dve.tensor_copy(dec[:, 0:H * nb], pS[:, DEC:DEC + H * nb]))
                step.done()
                neg = negS if t == 0 else negP
                dve.tensor_tensor(att[0:rows, :, 0:rows], bc(neg[:, :], 1, [rows, H, rows]),
                                  pM[:, :].rearrange("p (h n) -> p h n", h=H)[0:rows, :, 0:rows], ALU.subtract).then_inc(att_e, 1)
                job = ("kTr", t)
                filled(dve, job)
                dve.tensor_tensor(kw[0:rows, :, :], bank(job)[0:rows, :].rearrange("p (h e) -> p h e", h=H),
                                  bc(cols[0:rows, 3, :], 2, full), ALU.mult).then_inc(free(job), 1)
                dve.wait_ge(att_w, t + 1)
                dve.tensor_tensor(att[0:rows, :, 0:rows], att[0:rows, :, 0:rows],
                                  pK[:, :].rearrange("p (h n) -> p h n", h=H)[0:rows, :, 0:rows], ALU.mult).then_inc(att_p, 1)
                dve.wait_ge(att_b, t + 1)
                if t == 0:
                    dve.wait_ge(bt_back, 1)
                wi = cols[0:rows, 1, :]
                step(dve.tensor_tensor(num[0:rows, :, :], pB[0:rows, :].rearrange("p (h e) -> p h e", h=H),
                                       bc(wi, 2, full), ALU.mult))
                dve.wait_ge(att_a, t + 1)
                if t == 0:
                    step(dve.tensor_tensor(dtmp[0:rows, :, :], pS[0:rows, DB:DB + H * NB].rearrange("p (h b) -> p h b", h=H),
                                           bc(bmask[:, :], 1, [rows, H, NB]), ALU.mult))
                    step.done()
                    step(dve.tensor_reduce(den[0:rows, :], dtmp[0:rows, :, :], AX.X, ALU.add))
                    step.done()
                    step(dve.tensor_tensor(den[0:rows, :], den[0:rows, :], wi, ALU.mult))
                else:
                    step(dve.tensor_tensor(den[:, :], pS[:, DB:DB + H], wi, ALU.mult))
                step.done()
                dve.tensor_tensor(den[0:rows, :], den[0:rows, :], pS[0:rows, DA:DA + H], ALU.add).then_inc(den_read, 1)
                step(dve.tensor_tensor(num[0:rows, :, :], num[0:rows, :, :],
                                       pA[0:rows, :].rearrange("p (h e) -> p h e", h=H), ALU.add))
                dve.wait_ge(den_read, t + 1)
                step.done()
                step(dve.scalar_tensor_tensor(out=den[0:rows, :], in0=den[0:rows, :], scalar=-1.0, in1=den[0:rows, :],
                                              op0=ALU.mult, op1=ALU.max))
                step.done()
                step(dve.tensor_tensor(den[0:rows, :], den[0:rows, :], cols[0:rows, 2, :], ALU.max))
                step.done()
                step(dve.reciprocal(den[0:rows, :], den[0:rows, :]))
                step.done()
                step(dve.tensor_tensor(num[0:rows, :, :], num[0:rows, :, :], bc(den[0:rows, :], 2, full), ALU.mult))
                step.done()
                dve.tensor_tensor(num[0:rows, :, :], num[0:rows, :, :], sigo[0:rows, slot, :, :], ALU.mult).then_inc(hs_ready, 1)
                if t == 0:
                    def masked(h):
                        dve.tensor_tensor(vm[h % 2][0:NS], bc(v[0:NS, 0, h, :], 1, [NS, NB, 128]),
                                          bc(bmask[:, :], 2, [NS, NB, 128]), ALU.mult).then_inc(vm_ready, 1)
                    masked(0)
                    for h in range(H):
                        if h + 1 < H:
                            if h >= 1:
                                dve.wait_ge(cs_new, h)
                            masked(h + 1)
                        dh = dec[:, h * NB:(h + 1) * NB]
                        step(dve.tensor_tensor(Cs[:, h, :, :], Cs[:, h, :, :], bc(dh, 2, [128, NB, 128]), ALU.mult))
                        step(dve.tensor_tensor(nsm[:, h, :], nsm[:, h, :], dh, ALU.mult))
                        step.done()
                        dve.wait_ge(cs_new, h + 1)
                        step(dve.tensor_tensor(nsm[:, h, :], nsm[:, h, :], pS[:, DN + h * NB:DN + (h + 1) * NB], ALU.add))
                        ins = dve.tensor_tensor(Cs[:, h, :, :].rearrange("p b e -> p (b e)"),
                                                Cs[:, h, :, :].rearrange("p b e -> p (b e)"), yps[:, :], ALU.add)
                        ins.then_inc(cs_added, 1)
                    dve.wait_ge(cs_added, H)
                    step.done()
                    dve.nop(nofuse=True).then_inc(att_done, 1)
                else:
                    step(dve.tensor_tensor(npr[:, :], npr[:, :], dec[:, 0:H], ALU.mult))
                    step.done()
                    dve.wait_ge(att_c, t)
                    step(dve.tensor_tensor(npr[:, :], npr[:, :], pS[:, DN:DN + H], ALU.add))
                    for h in range(H):
                        step(dve.scalar_tensor_tensor(out=Cp[:, h, :], in0=Cp[:, h, :], scalar=dec[:, h:h + 1],
                                                      in1=pC[:, h * 128:(h + 1) * 128], op0=ALU.mult, op1=ALU.add))
                    step.done()
                    dve.nop(nofuse=True).then_inc(att_done, 1)

            def residual(g, j):
                job = ("out", g, j)
                filled(dve, job)
                span = slice(j * 128, (j + 1) * 128)
                if g == 0:
                    step(dve.tensor_tensor(x[0:NS, 0, span], x[0:NS, 0, span], bank(job)[0:NS, 0:128], ALU.add))
                    ins = dve.tensor_tensor(x[:, 1, span], x[:, 1, span], bank(job)[:, 128:256], ALU.add)
                else:
                    ins = dve.tensor_tensor(x[:, 2:5, span], x[:, 2:5, span],
                                            bank(job)[:, 0:384].rearrange("p (t e) -> p t e", t=3), ALU.add)
                ins.then_inc(free(job), 1)

            def norm2(t):
                rows = TILES[t][0]
                dve.wait_ge(sumsq2, t + 1)
                step(dve.reciprocal(rstd[0:rows, 1, t:t + 1], ss[0:rows, 1, t:t + 1]))
                step.done()
                if t == 0:
                    dve.wait_ge(ld_gains, 16)
                dve.scalar_tensor_tensor(out=xn[0:rows, XN_SLOT[t], :], in0=x[0:rows, t, :], scalar=rstd[0:rows, 1, t:t + 1],
                                         in1=gain[0:rows, :], op0=ALU.mult, op1=ALU.mult).then_inc(xn_ready, 1)

            def top_lists(t):
                rows, _, g = TILES[t]
                s = score[0:rows, t - GROUPS[g][0]]
                evacuated(dve, ("score", g, QC - 1))
                evacuated(dve, ("score", g, QC - 2))
                topu = topi[0:rows].bitcast(u32)
                for half in range(2):
                    k = slice(8 * half, 8 * half + 8)
                    for c in range(QC):
                        step(dve.max(topv[0:rows, c, k], s[:, c, :]))
                    step.done()
                    for c in range(QC):
                        step(dve.max_index(topu[:, c, k], topv[0:rows, c, k], s[:, c, :]))
                    if half == 0:
                        step.done()
                        for c in range(QC):
                            step(dve.match_replace(s[:, c, :], topv[0:rows, c, k], s[:, c, :], LOW))
                        step.done()
                step.done()
                dve.tensor_copy(topf[0:rows], topu).then_inc(scores_read, 1)
                dve.wait_ge(scores_read, t + 1)

            def pick(t):
                rows = TILES[t][0]
                first = topf[0:rows].rearrange("p (h s) k -> p h s k", s=2)
                vals = topv[0:rows].rearrange("p (h s) k -> p h s k", s=2)
                step(dve.tensor_single_scalar(first[:, :, 0, :], first[:, :, 0, :], 128.0, ALU.mult))
                step.done()
                for out, src in ((cand, vals), (ceid, first)):
                    for i, ni, nj, at in PAIRS:
                        shape = [rows, PH, ni, nj]
                        dst = out[0:rows, :, at:at + ni * nj]
                        if ni == 1:
                            step(dve.tensor_tensor(dst, src[:, :, 0, i:i + 1].broadcast_to([rows, PH, nj]), src[:, :, 1, 0:nj], ALU.add))
                        elif nj == 1:
                            step(dve.tensor_tensor(dst, src[:, :, 0, i:i + ni], src[:, :, 1, 0:1].broadcast_to([rows, PH, ni]), ALU.add))
                        else:
                            step(dve.tensor_tensor(dst.rearrange("p h (i j) -> p h i j", i=ni),
                                                   src[:, :, 0, i:i + ni].unsqueeze(3).broadcast_to(shape),
                                                   src[:, :, 1, 0:nj].unsqueeze(2).broadcast_to(shape), ALU.add))
                step.done()
                posu = pos[0:rows].bitcast(u32)
                for half in range(2):
                    k = slice(8 * half, 8 * half + 8)
                    for h in range(PH):
                        step(dve.max(best[0:rows, h, k], cand[0:rows, h, :]))
                    step.done()
                    for h in range(PH):
                        step(dve.max_index(posu[:, h, k], best[0:rows, h, k], cand[0:rows, h, :]))
                    if half == 0:
                        step.done()
                        for h in range(PH):
                            step(dve.match_replace(cand[0:rows, h, :], best[0:rows, h, k], cand[0:rows, h, :], LOW))
                        step.done()
                step.done()
                step(dve.tensor_copy(posf[0:rows], posu))
                step(dve.tensor_tensor(sub[0:rows, t % 2, :].rearrange("p (h k) -> p h k", h=PH), best[0:rows],
                                       best[0:rows, :, 0:1].broadcast_to([rows, PH, TOPK]), ALU.subtract))
                step.done()
                for h in range(PH):
                    for k in range(TOPK):
                        if h or k >= HITS:
                            step.done(but=HITS - 1)
                        step(dve.scalar_tensor_tensor(out=hit[0:rows, k % HITS, :], in0=iota[0:rows, :], scalar=posf[0:rows, h, k:k + 1],
                                                      in1=ceid[0:rows, h, :], op0=ALU.is_equal, op1=ALU.mult,
                                                      accum_out=eid[0:rows, h * TOPK + k:h * TOPK + k + 1]))
                step.done()
                dve.tensor_copy(idx[0:rows, t % 2, :], eid[0:rows, :]).then_inc(picked, 1)
                dve.wait_ge(picked, t + 1)

            def dot_products(t, lo, hi):
                first = FIRST_PICK[t]
                if t == 0:
                    dve.wait_ge(spread_x, 48)
                    dve.wait_ge(xn_ready, 1)
                with dve.Fori(lo, hi) as i:
                    for r in range(BLOCK):
                        dve.wait_ge(u_land[r], i * 16 + 16 * (first // BLOCK + 1))
                        dve.scalar_tensor_tensor(out=U[r], in0=U[r], scalar=1.0, in1=xn[:, XN_SLOT[t], :],
                                                 op0=ALU.mult, op1=ALU.mult,
                                                 accum_out=dots[:, t % 2, ds(i * BLOCK + r, 1)]).then_inc(u_free, 1)

            def gates(t):
                n = N_PICK[t]
                nh = n // TOPK
                s = (subS[:, :] if t == 0 else sub[:, t % 2, :]).rearrange("p (h k) -> p h k", k=TOPK)
                zt = z[:, t % 2, 0:n]
                dve.wait_ge(z_act, t + 1)
                if t >= 2:
                    dve.wait_ge(diag_ready, FIRST_PICK[t - 1])
                step(dve.tensor_reduce(zsum[:, 0:nh], s, AX.X, ALU.add))
                step.done()
                step(dve.reciprocal(zsum[:, 0:nh], zsum[:, 0:nh]))
                step.done()
                step(dve.tensor_tensor(zt.rearrange("p (h k) -> p h k", k=TOPK), s, bc(zsum[:, 0:nh], 2, [128, nh, TOPK]), ALU.mult))
                step.done()
                dve.tensor_tensor(zt, zt, dots[:, t % 2, 0:n], ALU.mult).then_inc(z_ready, 1)

            def final(t):
                rows = TILES[t][0]
                dve.wait_ge(sumsq3, t + 1)
                if t == 0:
                    dve.wait_ge(ld_gains, 32)
                step(dve.reciprocal(rstd[0:rows, 2, t:t + 1], ss[0:rows, 2, t:t + 1]))
                step.done()
                dve.scalar_tensor_tensor(out=x[0:rows, t, :], in0=yps[0:rows, :], scalar=rstd[0:rows, 2, t:t + 1],
                                         in1=gain[0:rows, :], op0=ALU.mult, op1=ALU.mult).then_inc(y_ready, 1)

            dve.wait_ge(consts, N_CONST)
            dve.memset(credit[:, 0:1], 0.0).then_inc(u_free, U_SLOTS)
            dve.memset(credit[:, 1:2], 0.0).then_inc(v_done, V_SLOTS)
            root1(0)
            dve.wait_ge(ld_small, 16 * 11)
            mixer_first(0)
            for t in GROUPS[0]:
                rows_of(t)
                attention(t)
            for j in range(N_OUT):
                residual(0, j)
            for t in GROUPS[0]:
                norm2(t)
            top_lists(0)
            pick(0)
            top_lists(1)
            dot_products(0, 0, N_PICK[0] // BLOCK)
            pick(1)
            gates(0)
            mixer_first(1)
            per = N_PICK[1] // BLOCK // 4
            for i, t in enumerate(GROUPS[1]):
                rows_of(t)
                attention(t)
                dot_products(1, i * per, (i + 1) * per)
            for j in range(N_OUT):
                residual(1, j)
            for t in GROUPS[1]:
                norm2(t)
            final(0)
            dot_products(1, 3 * per, 4 * per)
            gates(1)
            for t in range(2, 5):
                top_lists(t)
                pick(t)
                half = N_PICK[t] // BLOCK // 2
                dot_products(t, 0, half)
                final(t - 1)
                dot_products(t, half, 2 * half)
                gates(t)
            final(4)


def kernel(x_prompt, x_sample, state_C, state_n, state_m, state_conv, norm_mix, w_in, b_gates, w_dw, b_dw,
           gn_gain, gn_bias, w_out, norm_ffn, w_query, keys1, keys2, u_experts, v_experts, norm_final):
    import numpy as np
    import concourse.bacc as bacc
    from concourse.bass_utils import run_bass_kernel_spmd

    def chunks(w):
        k, n = w.shape
        return w.reshape(k // 128, 128, n // 128, 128).transpose(2, 1, 0, 3)

    w = H * 128
    wi = w_in[0]
    part = {"q": wi[:, 0:w], "k": wi[:, w:2 * w], "v": wi[:, 2 * w:3 * w], "o": wi[:, 3 * w:4 * w],
            "a": wi[:, 4 * w + 2 * H:4 * w + 2 * H + w], "g": wi[:, 4 * w + 2 * H + w:]}
    part = {name: chunks(p) for name, p in part.items()}
    w_all = np.concatenate([np.stack([part[kind][c] for kind, c in KINDS_IN]), chunks(w_out[0]), chunks(w_query[0])])
    chan = lambda p: p.reshape(CC, 128).T
    ins = {
        "x_sample": x_sample.reshape(NS, D), "x_prompt": x_prompt[0],
        "w_all": w_all,
        "w_gates": wi[:, 4 * w:4 * w + 2 * H].reshape(KC, 128, 2 * H).transpose(1, 0, 2),
        "b_gates": b_gates[0].reshape(2 * H, 1),
        "gain_mix": norm_mix[0].reshape(KC, 128).T,
        "w_dw": w_dw[0].reshape(TAPS, CC, 128).transpose(2, 1, 0),
        "b_dw": chan(b_dw[0]), "gn_gain": chan(gn_gain[0]), "gn_bias": chan(gn_bias[0]),
        "state_C": state_C[0].transpose(2, 1, 0, 3), "state_n": state_n[0].transpose(2, 1, 0), "state_m": state_m[0].T,
        "conv_hist": state_conv[0].reshape(NB, HIST, CC, 128).transpose(3, 2, 0, 1),
        "keys_T": np.stack([keys1[0], keys2[0]], axis=1).reshape(QC, 128, 128).transpose(2, 0, 1),
        "norm_ffn": norm_ffn[0:1], "norm_final": norm_final.reshape(1, D),
        "u_experts": u_experts[0], "v_experts": v_experts[0],
    }
    outs = {"y_p": (SEQ, D), "y_s": (NS, D), "C_p": (128, H, 128), "n_p": (128, H), "m_p": (H, 1),
            "conv_p": (128, CC, HIST), "C_s": (128, H, NB, 128), "n_s": (128, H, NB), "m_s": (H, NB),
            "conv_s": (128, CC, NB, HIST)}
    nc = bacc.Bacc("TRN2", target_bir_lowering=False, num_devices=1)
    ins = {name: np.ascontiguousarray(p) for name, p in ins.items()}
    a = {name: nc.dram_tensor(f"in_{name}", p.shape, mybir.dt.from_np(p.dtype), kind="ExternalInput").ap()
         for name, p in ins.items()}
    o = {name: nc.dram_tensor(f"out_{name}", shape, mybir.dt.float32, kind="ExternalOutput").ap()
         for name, shape in outs.items()}
    build(nc, a, o)
    res = run_bass_kernel_spmd(nc, [{f"in_{name}": p for name, p in ins.items()}], core_ids=[0]).results[0]
    r = {name: np.asarray(res[f"out_{name}"]) for name in outs}
    return (r["y_p"].reshape(1, SEQ, D), r["y_s"].reshape(NB, NT, D),
            np.ascontiguousarray(r["C_p"].transpose(1, 0, 2))[None, None],
            np.ascontiguousarray(r["n_p"].T)[None, None],
            r["m_p"].reshape(1, 1, H),
            np.ascontiguousarray(r["conv_p"].transpose(2, 1, 0)).reshape(1, 1, HIST, CC * 128),
            np.ascontiguousarray(r["C_s"].transpose(2, 1, 0, 3))[None],
            np.ascontiguousarray(r["n_s"].transpose(2, 1, 0))[None],
            np.ascontiguousarray(r["m_s"].T)[None],
            np.ascontiguousarray(r["conv_s"].transpose(2, 3, 1, 0)).reshape(1, NB, HIST, CC * 128))
```

```python
import concourse.bass as bass
from concourse import mybir
from contextlib import ExitStack

D = 1024
KC = D // 128
SEQ, NB, NT = 512, 8, 4
NS = NB * NT
H = 4
CC = 4
TAPS = 31
HIST = TAPS - 1
QC = 16
PH = 8
TOPK = 16
PICKS = PH * TOPK
EPS = 1e-6
NEG = -1e30
LOW = -3e38

PAIRS = [(0, 1, 16, 0), (1, 1, 8, 16), (2, 1, 5, 24), (3, 1, 4, 29), (4, 1, 3, 33), (5, 3, 2, 36), (8, 8, 1, 42)]
CAND = 50
HITS = 8

TILES = [(NS, 0, 0), (128, NS, 0), (128, 0, 1), (128, 128, 1), (128, 256, 1)]
GROUPS = [(0, 1), (2, 3, 4)]
WIDTH = [NS + 128, 384]
GMAX = 384
XN_SLOT = [0, 1, 2, 3, 0]

N_IN, N_OUT = 24, 8
N_W = N_IN + N_OUT + QC
W_SLOTS = 4
KINDS_IN = [("g", c) if h == 0 else ("a", c) for c in range(CC) for h in range(2)] + \
           [(kind, c) for kind in "kqvo" for c in range(H)]
PAUSE = 20

U_SLOTS, V_SLOTS = 8, 4
N_PICK = [PICKS * NS // 128] + [PICKS] * 4
FIRST_PICK = [sum(N_PICK[:t]) for t in range(5)]
BLOCK = 8
LEAD = 4


def pp_jobs():
    jobs = []
    for g, tiles in enumerate(GROUPS):
        jobs += [("xT", t, half) for t in tiles for half in range(2)]
        jobs += [("gate_i", g), ("gate_f", g)]
        jobs += [("in", g, i) for i in range(N_IN)]
        jobs += [("mean", g, c) for c in range(CC)] + [("var", g, c) for c in range(CC)]
        for t in tiles:
            jobs += [("kTr", t), ("hT", t)]
        jobs += [("out", g, j) for j in range(N_OUT)]
        jobs += [("x2T", t, half) for t in tiles for half in range(2)]
        for c in range(QC):
            jobs += [("query", g, c), ("score", g, c)]
    return {name: n for n, name in enumerate(jobs)}


class Steps:

    def __init__(self, engine, sem):
        self.engine, self.sem, self.n = engine, sem, 0

    def __call__(self, ins):
        self.n += 1
        ins.then_inc(self.sem, 1)

    def done(self, but=0):
        if self.n - but > 0:
            self.engine.wait_ge(self.sem, self.n - but)


def build(nc, a, o):
    f32, u32 = mybir.dt.float32, mybir.dt.uint32
    ALU, ACT, AX = mybir.AluOpType, mybir.ActivationFunctionType, mybir.AxisListType
    ds = bass.ds
    J = pp_jobs()

    with ExitStack() as ctx:
        def sb(name, shape, dt=f32):
            return ctx.enter_context(nc.sbuf_tensor(name, shape, dt))

        def sem(name):
            return ctx.enter_context(nc.semaphore(name))

        def view(region_, at, **dims):
            n = 1
            for d in dims.values():
                n *= d
            flat = region_[:, at:at + n]
            if len(dims) == 1:
                return flat
            names = " ".join(dims)
            return flat.rearrange(f"p ({names}) -> p {names}", **dims)

        W = sb("w_ring", [128, W_SLOTS, KC, 128])
        x = sb("x_res", [128, 5, D])
        xn = sb("x_normed", [128, 4, D])
        xnT = sb("x_normed_T", [128, KC, GMAX])
        v = sb("v_rows", [128, 3, H, 128])
        x4n = v[:, 0:2, :, :].rearrange("p t h e -> p (t h e)")
        sigo = sb("sig_o", [128, 3, H, 128])
        up = sb("u_prompt", [128, CC, HIST + GMAX])
        mixT = sb("mix_T", [128, KC, GMAX])
        region = sb("region", [128, 3 * QC * 128])
        qT = view(region, 0, h=H, n=GMAX)
        kT = view(region, H * GMAX, h=H, n=GMAX)
        cv = view(region, 2 * H * GMAX, c=CC, n=GMAX)
        ct = view(region, 3 * H * GMAX, c=CC, n=GMAX)
        score = view(region, 0, t=3, c=QC, k=128)
        qry = mixT[:, 0:2, :]
        u_ring = sb("u_ring", [128, U_SLOTS * D])
        v_ring = sb("v_ring", [128, V_SLOTS * D])
        U = [u_ring[:, s * D:(s + 1) * D] for s in range(U_SLOTS)]
        V = [v_ring[:, s * D:(s + 1) * D] for s in range(V_SLOTS)]
        Cs = view(u_ring, 0, h=H, b=NB, e=128)
        us = view(v_ring, 0, c=CC, b=NB, w=HIST + NT)
        vm = [view(v_ring, 1088 + 1024 * i, b=NB, e=128) for i in range(2)]
        BT = view(v_ring, 3136, h=H, n=NS)
        Cp = sb("C_prompt", [128, H, 128])
        keys = sb("keys_T", [128, QC, 128])
        gain = sb("gain", [128, D])
        rowsIF = sb("rows_if", [4, 2, GMAX])
        scratch = sb("scratch", [128, 2480])
        att = view(scratch, 0, h=H, n=128)
        num = view(scratch, 512, h=H, e=128)
        kw = view(scratch, 1024, h=H, e=128)
        kwS = sigo[0:NS, 2, :, :]
        R = view(scratch, 1536, k=7, n=128)[0:4]
        lf = scratch[0:4, 1536:1536 + GMAX]
        topv = view(scratch, 0, c=QC, k=TOPK)
        topi = view(scratch, 256, c=QC, k=TOPK)
        topf = view(scratch, 512, c=QC, k=TOPK)
        cand = view(scratch, 768, h=PH, c=CAND)
        ceid = view(scratch, 1168, h=PH, c=CAND)
        best = view(scratch, 1568, h=PH, k=TOPK)
        pos = view(scratch, 1696, h=PH, k=TOPK)
        posf = view(scratch, 1824, h=PH, k=TOPK)
        hit = view(scratch, 1952, k=HITS, c=CAND)
        eid = scratch[:, 2352:2480]
        idx = sb("expert_idx", [128, 3, PICKS], u32)
        sub = sb("score_minus_max", [128, 2, PICKS])
        dots = sb("dots", [128, 2, PICKS])
        z = sb("z", [128, 2, PICKS])
        u_idx = sb("u_idx_now", [128, 2, BLOCK], u32)
        v_idx = sb("v_idx_now", [128, 2, BLOCK], u32)
        diag = sb("diag", [128, V_SLOTS, 128])
        ident = sb("ident", [128, 128])
        fold = sb("fold", [128, NS])
        halves = sb("halves", [128, 128])
        negP = sb("neg_prompt", [128, 128])
        negS = sb("neg_sample", [NS, NS])
        sel = sb("sel", [4, H, 128])
        bmask = sb("batch_mask", [NS, NB])
        ones = sb("ones", [128, 1])
        iota_i = sb("iota_i", [128, CAND], mybir.dt.int32)
        iota = sb("iota", [128, CAND])
        zero = sb("zero", [4, 1])
        keepS = sb("keep_sample", [4, NS])
        dropS = sb("drop_sample", [4, NS])
        eps = sb("eps", [128, 1])
        gmix = sb("gain_mix", [128, KC])
        wg = sb("w_gates", [128, KC, 2 * H])
        bi = sb("b_i", [4, 1])
        bf = sb("b_f", [4, 1])
        wdw = sb("w_dw", [128, CC, TAPS])
        bdw = sb("b_dw", [128, CC])
        gng = sb("gn_gain", [128, CC])
        gnb = sb("gn_bias", [128, CC])
        npr = sb("n_prompt", [128, H])
        nsm = sb("n_sample", [128, H, NB])
        m0 = sb("m_sample", [4, NB])
        mprev = sb("m_prompt", [4, 1])
        mlast = sb("M_last", [4, NB])
        decR = sb("decay_rows", [4, NB])
        cols = sb("cols", [128, 4, H])
        dec = sb("decay", [128, H])
        decS = sb("decay_sample", [128, H * NB])
        dtmp = sb("den_tmp", [128, H, NB])
        den = sb("den", [128, H])
        ss = sb("sum_squares", [128, 3, 5])
        rstd = sb("rstd", [128, 3, 5])
        zsum = sb("z_sum", [128, PH])
        credit = sb("credit", [128, 2])

        pp = [ctx.enter_context(nc.psum_tensor(f"pp{i}", [128, 512], f32)) for i in range(2)]
        pa = [ctx.enter_context(nc.psum_tensor(f"pa{i}", [128, 512], f32)) for i in range(4)]
        yps = ctx.enter_context(nc.psum_tensor("y", [128, D], f32))
        pM, pA = pa[0], pa[0]
        pK, pC = pa[1], pa[1]
        pB, pS = pa[2], pa[3]
        DEC, DA, DB, DN = 16, 48, 52, 84

        ld_x = [sem(f"ld_x{t}") for t in range(5)]
        ld_small, ld_keys, ld_state, ld_gains = sem("ld_small"), sem("ld_keys"), sem("ld_state"), sem("ld_gains")
        w_land = [sem(f"w_land{s}") for s in range(W_SLOTS)]
        consts = sem("consts")
        pp_full, pp_free = sem("pp_full"), [sem(f"pp_free{i}") for i in range(2)]
        sumsq1, rstd1, xs_ready = sem("sumsq1"), sem("rstd1"), sem("xs_ready")
        neg_f, log_f = sem("neg_f"), sem("log_f")
        u_ready, centred, squared, normed = sem("u_ready"), sem("centred"), sem("squared"), sem("normed")
        mix_c, conv_done, hist_ready = sem("mix_c"), sem("conv_done"), sem("hist_ready")
        rows_set, rows_exp = sem("rows_set"), sem("rows_exp")
        att_in, att_e, att_w, att_p = sem("att_in"), sem("att_e"), sem("att_w"), sem("att_p")
        att_b, att_a, att_c, att_done = sem("att_b"), sem("att_a"), sem("att_c"), sem("att_done")
        bt_copied, bt_back, vm_ready, cs_new, cs_added = (
            sem("bt_copied"), sem("bt_back"), sem("vm_ready"), sem("cs_new"), sem("cs_added"))
        hs_ready, den_read = sem("hs_ready"), sem("den_read")
        sumsq2, xn_ready = sem("sumsq2"), sem("xn_ready")
        spread_x = sem("spread_x")
        scores_read, picked = sem("scores_read"), sem("picked")
        u_land = [sem(f"u_land{s}") for s in range(U_SLOTS)]
        v_land = [sem(f"v_land{s}") for s in range(V_SLOTS)]
        u_free, v_done, diag_ready = sem("u_free"), sem("v_done"), sem("diag_ready")
        staged = sem("staged")
        z_act, z_ready = sem("z_act"), sem("z_ready")
        sumsq3, y_ready = sem("sumsq3"), sem("y_ready")
        out_s, out_p, out_y = sem("out_s"), sem("out_p"), sem("out_y")
        s_act, s_dve, s_pool = sem("s_act"), sem("s_dve"), sem("s_pool")
        N_CONST = 21

        def filled(eng, job):
            eng.wait_ge(pp_full, J[job] + 1)

        def evacuated(eng, job):
            eng.wait_ge(pp_free[J[job] % 2], J[job] // 2 + 1)

        def bank(job):
            return pp[J[job] % 2]

        def free(job):
            return pp_free[J[job] % 2]

        def weight_job(n):
            g, i = divmod(n, N_W)
            if i < N_IN:
                return "in", g, i
            return ("out", g, i - N_IN) if i < N_IN + N_OUT else ("query", g, i - N_IN - N_OUT)

        block = ctx.enter_context(nc.Block())

        @block.sync
        def _(sp):
            def load_x(t):
                rows = TILES[t][0]
                src = a["x_sample"] if t == 0 else a["x_prompt"][(t - 1) * 128:t * 128, :]
                sp.dma_start(x[0:rows, t, :], src).then_inc(ld_x[t], 16)

            def load_w(n):
                if n >= W_SLOTS:
                    sp.wait_ge(pp_full, J[weight_job(n - W_SLOTS)] + 1)
                sp.dma_start(W[:, n % W_SLOTS, :, :], a["w_all"][n % N_W]).then_inc(w_land[n % W_SLOTS], 16)

            load_x(0)
            load_x(1)
            sp.dma_start(gmix[:, :], a["gain_mix"]).then_inc(ld_small, 16)
            sp.dma_start(wg[:, :, :], a["w_gates"]).then_inc(ld_small, 16)
            sp.dma_start(bi[:, :], a["b_gates"][0:H, :]).then_inc(ld_small, 16)
            sp.dma_start(bf[:, :], a["b_gates"][H:2 * H, :]).then_inc(ld_small, 16)
            for n in range(W_SLOTS):
                load_w(n)
            for dst, name in ((wdw[:, :, :], "w_dw"), (bdw[:, :], "b_dw"), (gng[:, :], "gn_gain"),
                              (gnb[:, :], "gn_bias"), (m0[:, :], "state_m"), (nsm[:, :, :], "state_n"),
                              (us[:, :, :, 0:HIST], "conv_hist")):
                sp.dma_start(dst, a[name]).then_inc(ld_small, 16)
            for t in (2, 3, 4):
                load_x(t)
            sp.dma_start(Cs, a["state_C"]).then_inc(ld_state, 16)
            sp.dma_start(keys[:, :, :], a["keys_T"]).then_inc(ld_keys, 16)
            sp.dma_start(gain[:, :], a["norm_ffn"].broadcast_to([128, D])).then_inc(ld_gains, 16)
            for n in range(W_SLOTS, N_W):
                load_w(n)
            sp.wait_ge(u_ready, 2)
            sp.dma_start(o["conv_s"], us[:, :, :, NT:NT + HIST]).then_inc(out_s, 16)
            sp.wait_ge(cs_added, H)
            sp.dma_start(o["C_s"], Cs).then_inc(out_s, 16)
            sp.dma_start(o["n_s"], nsm[:, :, :]).then_inc(out_s, 16)
            sp.dma_start(o["m_s"], m0[:, :]).then_inc(out_s, 16)
            sp.wait_ge(xn_ready, 1)
            for s in range(1, 4):
                sp.dma_start(xn[NS * s:NS * (s + 1), 0, :], xn[0:NS, 0, :]).then_inc(spread_x, 16)
            for n in range(N_W, 2 * N_W - QC + W_SLOTS):
                load_w(n)
            sp.wait_ge(u_ready, 4)
            sp.dma_start(o["conv_p"], up[:, :, GMAX:GMAX + HIST]).then_inc(out_p, 16)
            sp.wait_ge(att_done, 5)
            sp.dma_start(o["C_p"], Cp[:, :, :]).then_inc(out_p, 16)
            sp.dma_start(o["n_p"], npr[:, :]).then_inc(out_p, 16)
            sp.dma_start(o["m_p"], mprev[:, :]).then_inc(out_p, 16)
            sp.wait_ge(xn_ready, 5)
            sp.dma_start(gain[:, :], a["norm_final"].broadcast_to([128, D])).then_inc(ld_gains, 16)
            for n in range(2 * N_W - QC + W_SLOTS, 2 * N_W):
                load_w(n)
            for t in range(5):
                sp.wait_ge(y_ready, t + 1)
                dst = o["y_s"] if t == 0 else o["y_p"][(t - 1) * 128:t * 128, :]
                sp.dma_start(dst, x[0:TILES[t][0], t, :]).then_inc(out_y, 16)
            sp.wait_ge(out_y, 16 * 5)
            sp.wait_ge(out_s, 16 * 4)
            sp.wait_ge(out_p, 16 * 4)

        @block.gpsimd
        def _(pool):
            step = Steps(pool, s_pool)
            for t, value in ((ident, 0.0), (fold, 0.0), (halves, 1.0 / 64), (negP, 0.0), (negS, 0.0),
                             (bmask, 1.0), (dropS, 0.0), (keepS, 1.0)):
                step(pool.memset(t[:, :], value))
            step(pool.memset(sel[:, :, :], 0.0))
            step.done()
            n_const = [0]

            def const(ins):
                n_const[0] += 1
                ins.then_inc(consts, 1)

            const(pool.affine_select(out=ident[:, :], in_=ident[:, :], compare_op=ALU.not_equal, fill=1.0,
                                     base=0, pattern=[[-1, 128]], channel_multiplier=1))
            step(pool.affine_select(out=negS[:, :], in_=negS[:, :], compare_op=ALU.is_ge, fill=NEG,
                                    base=0, pattern=[[-4, NB], [0, NT]], channel_multiplier=1))
            step(pool.affine_select(out=bmask[:, :], in_=bmask[:, :], compare_op=ALU.is_ge, fill=0.0,
                                    base=0, pattern=[[-4, NB]], channel_multiplier=1))
            step(pool.iota(iota_i[:, :], [[1, CAND]], base=0, channel_multiplier=0))
            const(pool.affine_select(out=negP[:, :], in_=negP[:, :], compare_op=ALU.is_ge, fill=NEG,
                                     base=0, pattern=[[1, 128]], channel_multiplier=-1))
            const(pool.affine_select(out=sel[:, :, :], in_=sel[:, :, :], compare_op=ALU.not_equal, fill=1.0,
                                     base=0, pattern=[[-1, H], [0, 128]], channel_multiplier=1))
            for at, base, mul in ((0, 63, -1), (64, -64, 1)):
                const(pool.affine_select(out=halves[:, at:at + 64], in_=halves[:, at:at + 64], compare_op=ALU.is_ge,
                                         fill=0.0, base=base, pattern=[[0, 64]], channel_multiplier=mul))
            const(pool.memset(keepS[:, :].rearrange("p (b t) -> p b t", t=NT)[:, :, 0:1], 0.0))
            const(pool.memset(dropS[:, :].rearrange("p (b t) -> p b t", t=NT)[:, :, 0:1], NEG))
            const(pool.memset(ones[:, :], 1.0))
            const(pool.memset(eps[:, :], EPS))
            const(pool.memset(up[:, :, 0:HIST], 0.0))
            const(pool.memset(zero[:, :], 0.0))
            const(pool.memset(npr[:, :], 0.0))
            const(pool.memset(mprev[:, :], 0.0))
            const(pool.memset(Cp[:, :, :], 0.0))
            for i in range(3):
                const(pool.memset(ss[:, i, :], 1.0))
            step.done()
            const(pool.affine_select(out=negS[:, :], in_=negS[:, :], compare_op=ALU.is_ge, fill=NEG,
                                     base=0, pattern=[[4, NB], [1, NT]], channel_multiplier=-1))
            const(pool.affine_select(out=bmask[:, :], in_=bmask[:, :], compare_op=ALU.is_ge, fill=0.0,
                                     base=NT - 1, pattern=[[4, NB]], channel_multiplier=-1))
            const(pool.tensor_copy(iota[:, :], iota_i[:, :]))
            for s in range(4):
                ins = pool.affine_select(out=fold[:, :], in_=fold[:, :], compare_op=ALU.not_equal, fill=1.0,
                                         base=-NS * s, pattern=[[-1, NS]], channel_multiplier=1)
                if s < 3:
                    step(ins)
                    step.done()
                else:
                    const(ins)
            assert n_const[0] == N_CONST
            pool.wait_ge(consts, N_CONST)

            turns = [0]
            rings = {"u": (a["u_experts"], u_idx, U, U_SLOTS, u_land, u_free),
                     "v": (a["v_experts"], v_idx, V, V_SLOTS, v_land, v_done)}

            def gathers(*streams):
                n = len(streams)
                base = turns[0]
                blocks = streams[0][3] - streams[0][2]
                with pool.Fori(0, blocks // 2) as i:
                    for h in range(2):
                        for kind, t, lo, _ in streams:
                            src = idx[:, t % 3, :]
                            pool.tensor_copy(rings[kind][1][:, h, :],
                                             src[:, ds(i * 2 * BLOCK + (lo + h) * BLOCK, BLOCK)]).then_inc(staged, 1)
                        pool.wait_ge(staged, i * 2 * n + (base + (h + 1) * n))
                        for r in range(BLOCK):
                            for kind, t, lo, _ in streams:
                                table, now, ring, slots, land, freed = rings[kind]
                                s = r % slots
                                pool.wait_ge(freed, i * 2 * BLOCK + ((lo + h) * BLOCK + r + FIRST_PICK[t] + 1))
                                pool.nop(nofuse=True)
                                pool.indirect_dma_start(
                                    out=ring[s], out_offset=None, in_=table,
                                    in_offset=bass.IndirectOffsetOnAxis(ap=now[:, h, r:r + 1], axis=0)
                                ).then_inc(land[s], 16)
                turns[0] += n * blocks

            pool.wait_ge(out_s, 16 * 4)
            pool.wait_ge(picked, 1)
            gathers(("u", 0, 0, 4))
            gathers(("v", 0, 0, 4))
            pool.wait_ge(picked, 2)
            gathers(("u", 1, 0, 16))
            gathers(("v", 1, 0, LEAD))
            pool.wait_ge(picked, 3)
            gathers(("u", 2, 0, 16 - LEAD), ("v", 1, LEAD, 16))
            gathers(("u", 2, 16 - LEAD, 16))
            for t in range(2, 4):
                pool.wait_ge(picked, t + 2)
                gathers(("u", t + 1, 0, 16), ("v", t, 0, 16))
            gathers(("v", 4, 0, 16))

        @block.tensor
        def _(pe):
            def job(name):
                n = J[name]
                if n >= 2:
                    pe.wait_ge(pp_free[n % 2], n // 2)
                return pp[n % 2]

            def transposes(name, src, rows, cols_of, count):
                p = job(name)
                for i in range(count):
                    ins = pe.transpose(p[:, i * 128:i * 128 + rows], cols_of(src, i), ident[0:rows, 0:rows])
                ins.then_inc(pp_full, 1)

            def weights(n):
                pe.wait_ge(w_land[n % W_SLOTS], 16 * (n // W_SLOTS + 1))
                return W[:, n % W_SLOTS, :, :]

            def project(name, g, n, actT, rows_out):
                w = weights(n)
                p = job(name)
                if rows_out:
                    parts = [(i, TILES[t][0], TILES[t][1]) for i, t in enumerate(GROUPS[g])]
                else:
                    parts = [(0, 128, 0)]
                for i, rows, col in parts:
                    for k in range(KC):
                        if rows_out:
                            ins = pe.matmul(p[0:rows, i * 128:(i + 1) * 128], actT[:, k, col:col + rows], w[:, k, :],
                                            start=(k == 0), stop=(k == KC - 1))
                        else:
                            ins = pe.matmul(p[:, 0:WIDTH[g]], w[:, k, :], actT[:, k, 0:WIDTH[g]],
                                            start=(k == 0), stop=(k == KC - 1))
                ins.then_inc(pp_full, 1)

            def inputs(g):
                for t in GROUPS[g]:
                    rows = TILES[t][0]
                    pe.wait_ge(xs_ready, t + 1)
                    for half in range(2):
                        transposes(("xT", t, half), x4n if t == 4 else xn[0:rows, XN_SLOT[t], :], rows,
                                   lambda s, i, half=half: s[:, (4 * half + i) * 128:(4 * half + i + 1) * 128], 4)
                for t in GROUPS[g]:
                    for half in range(2):
                        evacuated(pe, ("xT", t, half))
                if g == 0:
                    pe.wait_ge(ld_small, 16 * 11)
                for kind, at in (("gate_i", 0), ("gate_f", H)):
                    p = job((kind, g))
                    for k in range(KC):
                        ins = pe.matmul(p[0:H, 0:WIDTH[g]], wg[:, k, at:at + H], xnT[:, k, 0:WIDTH[g]],
                                        start=(k == 0), stop=(k == KC - 1))
                    ins.then_inc(pp_full, 1)
                project_inputs(g, range(PAUSE))

            def project_inputs(g, chunks):
                for i in chunks:
                    project(("in", g, i), g, g * N_W + i, xnT, KINDS_IN[i][0] in "ov")

            def conv_stats(g):
                n = WIDTH[g]
                pe.wait_ge(conv_done, g + 1)
                for c in range(CC):
                    p = job(("mean", g, c))
                    pe.matmul(p[:, 0:n], halves[:, :], cv[:, c, 0:n], start=True, stop=True).then_inc(pp_full, 1)
                for c in range(CC):
                    pe.wait_ge(squared, CC * g + c + 1)
                    p = job(("var", g, c))
                    pe.matmul(p[:, 0:n], halves[:, :], ct[:, c, 0:n], start=True, stop=True).then_inc(pp_full, 1)

            def attention(t):
                rows, col, g = TILES[t]
                nb = NB if t == 0 else 1
                slot = t - GROUPS[g][0]
                span = slice(col, col + rows)
                pe.wait_ge(rows_exp, t + 1)
                if t >= 1:
                    pe.wait_ge(att_done, t)
                for kind, k in enumerate((1, 3, 4, 5)):
                    pe.transpose(pS[0:rows, 4 * kind:4 * kind + 4], R[:, k, 0:rows], ident[0:4, 0:4])
                for h in range(H):
                    pe.matmul(pS[:, DEC + h * nb:DEC + (h + 1) * nb], sel[:, h, :], decR[:, 0:nb], start=True, stop=True)
                for h in range(H):
                    pe.matmul(pM[0:rows, h * 128:h * 128 + rows], sel[:, h, 0:rows], R[:, 2, 0:rows], start=True, stop=True)
                for h in range(H):
                    ins = pe.matmul(pK[0:rows, h * 128:h * 128 + rows], kT[:, h, span], qT[:, h, span], start=True, stop=True)
                ins.then_inc(att_in, 1)
                if t == 0:
                    pe.wait_ge(ld_state, 16)
                    for h in range(H):
                        for b in range(NB):
                            pe.matmul(pB[:, h * NS + NT * b:h * NS + NT * (b + 1)], Cs[:, h, b, :],
                                      qT[:, h, NT * b:NT * (b + 1)], start=True, stop=True)
                    pe.wait_ge(att_e, t + 1)
                    for h in range(H):
                        ins = pe.matmul(pS[0:rows, DB + h * NB:DB + (h + 1) * NB], qT[:, h, 0:NS], nsm[:, h, :],
                                        start=True, stop=True)
                    ins.then_inc(att_b, 1)
                    pe.wait_ge(bt_copied, 1)
                    for h in range(H):
                        ins = pe.transpose(pB[0:NS, h * 128:(h + 1) * 128], BT[:, h, :], ident[:, :])
                    ins.then_inc(bt_back, 1)
                else:
                    for h in range(H):
                        pe.matmul(pB[:, h * 128:(h + 1) * 128], qT[:, h, span], Cp[:, h, :], start=True, stop=True)
                    pe.wait_ge(att_e, t + 1)
                    for h in range(H):
                        ins = pe.matmul(pS[:, DB + h:DB + h + 1], qT[:, h, span], npr[:, h:h + 1], start=True, stop=True)
                    ins.then_inc(att_b, 1)
                p = job(("kTr", t))
                for h in range(H):
                    ins = pe.transpose(p[0:rows, h * 128:(h + 1) * 128], kT[:, h, span], ident[:, :])
                ins.then_inc(pp_full, 1)
                pe.wait_ge(att_p, t + 1)
                for h in range(H):
                    pe.matmul(pA[0:rows, h * 128:(h + 1) * 128], att[0:rows, h, 0:rows], v[0:rows, slot, h, :],
                              start=True, stop=True)
                for h in range(H):
                    ins = pe.matmul(pS[0:rows, DA + h:DA + h + 1], att[0:rows, h, 0:rows], ones[0:rows, :],
                                    start=True, stop=True)
                ins.then_inc(att_a, 1)
                evacuated(pe, ("kTr", t))
                pe.wait_ge(den_read, t + 1)
                if t:
                    for h in range(H):
                        pe.matmul(pC[:, h * 128:(h + 1) * 128], kw[:, h, :], v[:, slot, h, :], start=True, stop=True)
                    for h in range(H):
                        ins = pe.matmul(pS[:, DN + h:DN + h + 1], kw[:, h, :], ones[:, :], start=True, stop=True)
                    ins.then_inc(att_c, 1)
                pe.wait_ge(hs_ready, t + 1)
                transposes(("hT", t), num, rows, lambda s, h, rows=rows: s[0:rows, h, :], H)

            def outputs(g):
                pe.wait_ge(mix_c, CC * (g + 1))
                for t in GROUPS[g]:
                    evacuated(pe, ("hT", t))
                for j in range(N_OUT):
                    project(("out", g, j), g, g * N_W + N_IN + j, mixT, True)

            def sample_states(h):
                pe.wait_ge(vm_ready, h + 1)
                if h:
                    pe.wait_ge(cs_added, h)
                for half in range(2):
                    pe.matmul(yps[:, half * 512:(half + 1) * 512], kwS[:, h, :],
                              vm[h % 2][0:NS, 4 * half:4 * half + 4, :].rearrange("p b e -> p (b e)"),
                              start=True, stop=True)
                pe.matmul(pS[:, DN + h * NB:DN + (h + 1) * NB], kwS[:, h, :], bmask[:, :],
                          start=True, stop=True).then_inc(cs_new, 1)

            def queries(g):
                for t in GROUPS[g]:
                    rows = TILES[t][0]
                    pe.wait_ge(xn_ready, t + 1)
                    for half in range(2):
                        transposes(("x2T", t, half), xn, rows,
                                   lambda s, i, t=t, half=half, rows=rows:
                                   s[0:rows, XN_SLOT[t], (4 * half + i) * 128:(4 * half + i + 1) * 128], 4)
                for t in GROUPS[g]:
                    for half in range(2):
                        evacuated(pe, ("x2T", t, half))
                if g == 0:
                    pe.wait_ge(ld_keys, 16)
                for c in range(QC):
                    project(("query", g, c), g, g * N_W + N_IN + N_OUT + c, xnT, False)
                    p = job(("score", g, c))
                    evacuated(pe, ("query", g, c))
                    for i, t in enumerate(GROUPS[g]):
                        rows, col, _ = TILES[t]
                        low = c // 4 * NS if t == 0 else 0
                        ins = pe.matmul(p[low:low + rows, i * 128:(i + 1) * 128], qry[:, c % 2, col:col + rows], keys[:, c, :],
                                        start=True, stop=True)
                    ins.then_inc(pp_full, 1)
                    if g == 0 and 2 <= c < 2 + 2 * H and c % 2 == 0:
                        sample_states(c // 2 - 1)

            def experts(t):
                rows, _, g = TILES[t]
                if t:
                    pe.wait_ge(y_ready, t)
                for half in range(2):
                    pe.matmul(yps[0:rows, half * 512:(half + 1) * 512], ident[0:rows, 0:rows],
                              x[0:rows, t, half * 512:(half + 1) * 512], start=True, stop=True, skip_group_check=True)
                first = FIRST_PICK[t]
                with pe.Fori(0, N_PICK[t] // BLOCK) as i:
                    for r in range(BLOCK):
                        s = r % V_SLOTS
                        pe.wait_ge(v_land[s], i * (16 * BLOCK // V_SLOTS) + 16 * (first // V_SLOTS + r // V_SLOTS + 1))
                        pe.wait_ge(diag_ready, i * BLOCK + (first + r + 1))
                        for half in range(2):
                            ins = pe.matmul(yps[0:rows, half * 512:(half + 1) * 512], diag[:, s, 0:rows],
                                            V[s][:, half * 512:(half + 1) * 512], start=False, stop=True,
                                            skip_group_check=True)
                        ins.then_inc(v_done, 1)

            pe.wait_ge(consts, N_CONST)
            inputs(0)
            project_inputs(0, range(PAUSE, N_IN))
            evacuated(pe, ("in", 0, N_IN - 1))
            evacuated(pe, ("in", 0, N_IN - 2))
            conv_stats(0)
            attention(0)
            attention(1)
            outputs(0)
            queries(0)
            inputs(1)
            experts(0)
            project_inputs(1, range(PAUSE, N_IN))
            evacuated(pe, ("in", 1, N_IN - 1))
            evacuated(pe, ("in", 1, N_IN - 2))
            conv_stats(1)
            for t in GROUPS[1]:
                attention(t)
            outputs(1)
            queries(1)
            for t in range(1, 5):
                experts(t)

        @block.scalar
        def _(act):
            step = Steps(act, s_act)
            A = act.activation

            def norm1(g):
                for t in GROUPS[g]:
                    rows = TILES[t][0]
                    act.wait_ge(ld_x[t], 16)
                    step.done()
                    step(A(xn[0:rows, XN_SLOT[t] if g == 0 else 2, :], x[0:rows, t, :], ACT.Square, accum_out=ss[0:rows, 0, t:t + 1]))
                step.done()
                lo, hi = GROUPS[g][0], GROUPS[g][-1] + 1
                A(ss[:, 0, lo:hi], ss[:, 0, lo:hi], ACT.Sqrt, bias=eps[:, :], scale=1.0 / D).then_inc(sumsq1, 1)

            def scale_x(g):
                act.wait_ge(rstd1, g + 1)
                for t in GROUPS[g]:
                    rows = TILES[t][0]
                    dst = x4n if t == 4 else xn[0:rows, XN_SLOT[t], :]
                    if t == 4:
                        act.wait_ge(vm_ready, H)
                    A(dst, x[0:rows, t, :], ACT.Copy, scale=rstd[0:rows, 0, t:t + 1]).then_inc(xs_ready, 1)

            def spread_T(name, t, half, gain):
                rows, col, _ = TILES[t]
                job = (name, t, half)
                filled(act, job)
                if gain:
                    for i in range(4):
                        k = 4 * half + i
                        ins = A(xnT[:, k, col:col + rows], bank(job)[:, i * 128:i * 128 + rows], ACT.Copy, scale=gmix[:, k:k + 1])
                else:
                    ins = A(xnT[:, 4 * half:4 * half + 4, col:col + rows],
                            bank(job)[:, :].rearrange("p (i n) -> p i n", i=4)[:, :, 0:rows], ACT.Copy)
                ins.then_inc(free(job), 1)

            def inputs(g):
                n = WIDTH[g]
                scale_x(g)
                if g == 0:
                    act.wait_ge(ld_small, 16 * 11)
                for t in GROUPS[g]:
                    for half in range(2):
                        spread_T("xT", t, half, True)
                for at, (kind, bias) in enumerate((("gate_i", bi), ("gate_f", bf))):
                    job = (kind, g)
                    filled(act, job)
                    A(rowsIF[:, at, 0:n], bank(job)[0:H, 0:n], ACT.Identity, bias=bias[:, :]).then_inc(free(job), 1)
                if g == 0:
                    log_rows(0)
                if g == 1:
                    act.wait_ge(hist_ready, 1)
                input_chunks(g, range(PAUSE))

            def log_rows(g):
                n = WIDTH[g]
                act.wait_ge(neg_f, g + 1)
                step(A(lf[:, 0:n], lf[:, 0:n], ACT.Exp))
                step.done()
                A(lf[:, 0:n], lf[:, 0:n], ACT.Ln, bias=1.0).then_inc(log_f, 1)

            def input_chunks(g, chunks):
                n = WIDTH[g]
                for i in chunks:
                    kind, c = KINDS_IN[i]
                    if g == 1 and kind == "k" and c == 0:
                        act.wait_ge(scores_read, 2)
                    job = ("in", g, i)
                    p = bank(job)
                    filled(act, job)
                    if kind == "g":
                        ins = A(ct[:, c, 0:n], p[:, 0:n], ACT.Sigmoid)
                    elif kind == "a" and g == 0:
                        step(A(us[:, c, :, HIST:], p[:, 0:NS].rearrange("p (b t) -> p b t", t=NT), ACT.Copy))
                        ins = A(up[:, c, HIST:HIST + 128], p[:, NS:n], ACT.Copy)
                    elif kind == "a":
                        ins = A(up[:, c, HIST:HIST + n], p[:, 0:n], ACT.Copy)
                    elif kind == "k":
                        ins = A(kT[:, c, 0:n], p[:, 0:n], ACT.Copy, scale=128 ** -0.5)
                    elif kind == "q":
                        ins = A(qT[:, c, 0:n], p[:, 0:n], ACT.Copy)
                    else:
                        dst, f = (v, ACT.Copy) if kind == "v" else (sigo, ACT.Sigmoid)
                        if g == 0:
                            step(A(dst[0:NS, 0, c, :], p[0:NS, 0:128], f))
                            ins = A(dst[:, 1, c, :], p[:, 128:256], f)
                        else:
                            ins = A(dst[:, 0:3, c, :], p[:, 0:384].rearrange("p (t e) -> p t e", t=3), f)
                    ins.then_inc(free(job), 1)

            def exp_rows(t):
                rows = TILES[t][0]
                nb = NB if t == 0 else 1
                act.wait_ge(rows_set, t + 1)
                step(A(R[:, 3:6, 0:rows], R[:, 3:6, 0:rows], ACT.Exp))
                A(decR[:, 0:nb], decR[:, 0:nb], ACT.Exp).then_inc(rows_exp, 1)

            def mixer(g):
                n = WIDTH[g]
                for c in range(CC):
                    act.wait_ge(centred, CC * g + c + 1)
                    A(ct[:, c, 0:n], cv[:, c, 0:n], ACT.Square).then_inc(squared, 1)
                for c in range(CC):
                    job = ("var", g, c)
                    filled(act, job)
                    A(ct[:, c, 0:n], bank(job)[:, 0:n], ACT.Sqrt, bias=eps[:, :]).then_inc(free(job), 1)
                for c in range(CC):
                    act.wait_ge(normed, CC * g + c + 1)
                    A(mixT[:, CC + c, 0:n], cv[:, c, 0:n], ACT.Silu, bias=gnb[:, c:c + 1], scale=gng[:, c:c + 1]).then_inc(mix_c, 1)
                for t in GROUPS[g]:
                    rows, col, _ = TILES[t]
                    if t == 0:
                        act.wait_ge(att_b, 1)
                        A(BT, pB[:, 0:H * NS].rearrange("p (h n) -> p h n", h=H), ACT.Copy).then_inc(bt_copied, 1)
                    act.wait_ge(att_e, t + 1)
                    for h in range(H):
                        ins = A(att[0:rows, h, 0:rows], att[0:rows, h, 0:rows], ACT.Exp, bias=cols[0:rows, 0, h:h + 1])
                    ins.then_inc(att_w, 1)
                    if t + 1 in GROUPS[g]:
                        exp_rows(t + 1)
                    job = ("hT", t)
                    filled(act, job)
                    A(mixT[:, 0:H, col:col + rows], bank(job)[:, :].rearrange("p (h n) -> p h n", h=H)[:, :, 0:rows],
                      ACT.Copy).then_inc(free(job), 1)
                for t in GROUPS[g]:
                    rows = TILES[t][0]
                    evacuated(act, ("out", g, N_OUT - 1))
                    evacuated(act, ("out", g, N_OUT - 2))
                    if t == 4:
                        act.wait_ge(u_free, U_SLOTS + N_PICK[0])
                    step(A(xn[0:rows, XN_SLOT[t], :], x[0:rows, t, :], ACT.Square, accum_out=ss[0:rows, 1, t:t + 1]))
                    step.done()
                    A(ss[0:rows, 1, t:t + 1], ss[0:rows, 1, t:t + 1], ACT.Sqrt, bias=eps[0:rows, :], scale=1.0 / D).then_inc(sumsq2, 1)

            def queries(g):
                n = WIDTH[g]
                for t in GROUPS[g]:
                    for half in range(2):
                        spread_T("x2T", t, half, False)
                for c in range(QC):
                    job = ("query", g, c)
                    filled(act, job)
                    A(qry[:, c % 2, 0:n], bank(job)[:, 0:n], ACT.Copy).then_inc(free(job), 1)
                    job = ("score", g, c)
                    filled(act, job)
                    if g == 0:
                        part = slice(c // 4 * NS, (c // 4 + 1) * NS)
                        step(A(score[part, 0, c % 4, :], bank(job)[part, 0:128], ACT.Copy))
                        ins = A(score[:, 1, c, :], bank(job)[:, 128:256], ACT.Copy)
                    else:
                        ins = A(score[:, 0:3, c, :], bank(job)[:, 0:384].rearrange("p (t k) -> p t k", t=3), ACT.Copy)
                    ins.then_inc(free(job), 1)

            def gates(t):
                n = N_PICK[t]
                s = sub[:, t % 2, 0:n]
                act.wait_ge(u_free, U_SLOTS + FIRST_PICK[t] + n)
                step(A(s, s, ACT.Exp))
                A(dots[:, t % 2, 0:n], dots[:, t % 2, 0:n], ACT.Gelu).then_inc(z_act, 1)

            def diagonals(t):
                src = fold if t == 0 else ident
                w = NS if t == 0 else 128
                first = FIRST_PICK[t]
                act.wait_ge(z_ready, t + 1)
                with act.Fori(0, N_PICK[t] // BLOCK) as i:
                    for r in range(BLOCK):
                        act.wait_ge(v_done, i * BLOCK + (first + r + 1))
                        A(diag[:, r % V_SLOTS, 0:w], src[:, 0:w], ACT.Copy,
                          scale=z[:, t % 2, ds(i * BLOCK + r, 1)]).then_inc(diag_ready, 1)

            def final(t):
                rows = TILES[t][0]
                act.wait_ge(v_done, V_SLOTS + FIRST_PICK[t] + N_PICK[t])
                step(A(x[0:rows, t, :], yps[0:rows, :], ACT.Square, accum_out=ss[0:rows, 2, t:t + 1]))
                step.done()
                A(ss[0:rows, 2, t:t + 1], ss[0:rows, 2, t:t + 1], ACT.Sqrt, bias=eps[0:rows, :], scale=1.0 / D).then_inc(sumsq3, 1)

            act.wait_ge(consts, N_CONST)
            norm1(0)
            inputs(0)
            exp_rows(0)
            input_chunks(0, range(PAUSE, N_IN))
            norm1(1)
            mixer(0)
            queries(0)
            inputs(1)
            gates(0)
            log_rows(1)
            diagonals(0)
            final(0)
            exp_rows(2)
            input_chunks(1, range(PAUSE, N_IN))
            mixer(1)
            queries(1)
            gates(1)
            for t in range(1, 5):
                diagonals(t)
                if t < 4:
                    gates(t + 1)
                final(t)

        @block.vector
        def _(dve):
            step = Steps(dve, s_dve)

            def bc(ap, axis, shape):
                return ap.unsqueeze(axis).broadcast_to(shape)

            def conv(g, pair):
                if g == 0:
                    parts = [(us, slice(0, NS), True), (up, slice(NS, WIDTH[0]), False)]
                else:
                    parts = [(up, slice(0, GMAX), False)]
                for j in range(TAPS):
                    for c in (2 * pair, 2 * pair + 1):
                        for src, span, sample in parts:
                            out = cv[:, c, span]
                            if sample:
                                win = src[:, c, :, j:j + NT]
                                out = out.rearrange("p (b t) -> p b t", t=NT)
                            else:
                                win = src[:, c, j:j + span.stop - span.start]
                            if j == 0:
                                step(dve.tensor_scalar(out, win, wdw[:, c, 0:1], bdw[:, c:c + 1], ALU.mult, ALU.add))
                            else:
                                step.done(but=len(parts) * 2 - 1)
                                step(dve.scalar_tensor_tensor(out=out, in0=win, scalar=wdw[:, c, j:j + 1], in1=out,
                                                              op0=ALU.mult, op1=ALU.add))
                if pair == 1:
                    step.done()
                    dve.nop(nofuse=True).then_inc(conv_done, 1)

            def root1(g):
                dve.wait_ge(sumsq1, g + 1)
                lo, hi = GROUPS[g][0], GROUPS[g][-1] + 1
                dve.reciprocal(rstd[:, 0, lo:hi], ss[:, 0, lo:hi]).then_inc(rstd1, 1)

            def mixer_first(g):
                n = WIDTH[g]
                evacuated(dve, ("gate_f", g))
                evacuated(dve, ("gate_i", g))
                dve.scalar_tensor_tensor(out=lf[:, 0:n], in0=rowsIF[:, 1, 0:n], scalar=-1.0, in1=rowsIF[:, 1, 0:n],
                                         op0=ALU.mult, op1=ALU.min).then_inc(neg_f, 1)
                dve.wait_ge(log_f, g + 1)
                step(dve.scalar_tensor_tensor(out=rowsIF[:, 1, 0:n], in0=rowsIF[:, 1, 0:n], scalar=0.0, in1=lf[:, 0:n],
                                              op0=ALU.min, op1=ALU.subtract))
                step.done()
                rows_of(GROUPS[g][0])
                for pair in range(2):
                    two = slice(2 * pair, 2 * pair + 2)
                    last = 4 * pair + 3
                    evacuated(dve, ("in", g, last))
                    evacuated(dve, ("in", g, last - 1))
                    if g == 0:
                        step(dve.tensor_tensor(us[:, two, :, HIST:], us[:, two, :, HIST:],
                                               ct[:, two, 0:NS].rearrange("p c (b t) -> p c b t", t=NT), ALU.mult))
                        dve.tensor_tensor(up[:, two, HIST:HIST + 128], up[:, two, HIST:HIST + 128], ct[:, two, NS:n],
                                          ALU.mult).then_inc(u_ready, 1)
                    else:
                        dve.tensor_tensor(up[:, two, HIST:HIST + n], up[:, two, HIST:HIST + n], ct[:, two, 0:n],
                                          ALU.mult).then_inc(u_ready, 1)
                    dve.wait_ge(u_ready, 2 * g + pair + 1)
                    step.done()
                    conv(g, pair)

            def group_norm(g):
                n = WIDTH[g]
                for c in range(CC):
                    job = ("mean", g, c)
                    filled(dve, job)
                    step(dve.tensor_tensor(cv[:, c, 0:n], cv[:, c, 0:n], bank(job)[:, 0:n], ALU.subtract))
                    step.done()
                    dve.nop(nofuse=True).then_inc(centred, 1)
                    dve.nop(nofuse=True).then_inc(free(job), 1)
                for c in range(CC):
                    evacuated(dve, ("var", g, c))
                    step(dve.reciprocal(ct[:, c, 0:n], ct[:, c, 0:n]))
                    step.done()
                    dve.tensor_tensor(cv[:, c, 0:n], cv[:, c, 0:n], ct[:, c, 0:n], ALU.mult).then_inc(normed, 1)

            def rows_of(t):
                rows, col, g = TILES[t]
                b, gg, M, gx = (R[:, i, 0:rows] for i in (0, 1, 2, 6))
                span = slice(col, col + rows)
                sample = t == 0
                bt = (lambda ap: ap.rearrange("p (b t) -> p b t", t=NT))
                step(dve.tensor_tensor_scan(b, keepS[:, :] if sample else ones[0:4, :].broadcast_to([4, rows]), rowsIF[:, 1, span], 0.0,
                                            ALU.mult, ALU.add))
                step.done()
                step(dve.tensor_tensor(gg, rowsIF[:, 0, span], b, ALU.subtract))
                step.done()
                if sample:
                    step(dve.tensor_copy(gx, gg))
                    step.done()
                    first = bt(gx)[:, :, 0:1]
                    step(dve.tensor_tensor(first, first, m0[:, :].unsqueeze(2), ALU.max))
                    step.done()
                    step(dve.tensor_tensor_scan(M, dropS[:, :], gx, NEG, ALU.add, ALU.max))
                    step.done()
                    last = bt(M)[:, :, NT - 1:NT]
                    lastb = bt(b)[:, :, NT - 1:NT]
                    step(dve.tensor_copy(mlast[:, :].unsqueeze(2), last))
                    step.done()
                    carried = bc(m0[:, :], 2, [4, NB, NT])
                    step(dve.tensor_tensor(bt(R[:, 3, 0:rows]), carried, bt(M), ALU.subtract))
                    step(dve.tensor_tensor(bt(R[:, 5, 0:rows]), bt(gg), bc(mlast[:, :], 2, [4, NB, NT]), ALU.subtract))
                    step(dve.tensor_tensor(decR[:, :], m0[:, :], mlast[:, :], ALU.subtract))
                    step.done()
                    step(dve.tensor_tensor(m0[:, :].unsqueeze(2), last, lastb, ALU.add))
                else:
                    step(dve.tensor_tensor_scan(M, zero[:, :].broadcast_to([4, rows]), gg, mprev[:, :], ALU.add, ALU.max))
                    step.done()
                    step(dve.tensor_scalar(R[:, 3, 0:rows], M, -1.0, mprev[:, :], ALU.mult, ALU.add))
                    step(dve.tensor_scalar(R[:, 5, 0:rows], gg, M[:, rows - 1:rows], None, ALU.subtract))
                    step(dve.tensor_tensor(decR[:, 0:1], mprev[:, :], M[:, rows - 1:rows], ALU.subtract))
                    step.done()
                    step(dve.tensor_tensor(mprev[:, :], M[:, rows - 1:rows], b[:, rows - 1:rows], ALU.add))
                dve.scalar_tensor_tensor(out=R[:, 4, 0:rows], in0=M, scalar=-1.0, in1=b, op0=ALU.mult,
                                         op1=ALU.subtract).then_inc(rows_set, 1)

            def attention(t):
                rows, col, g = TILES[t]
                nb = NB if t == 0 else 1
                slot = t - GROUPS[g][0]
                full = [rows, H, 128]
                if t >= 1:
                    evacuated(dve, ("hT", t - 1))
                dve.wait_ge(att_in, t + 1)
                step(dve.tensor_copy(cols[0:rows, :, :], pS[0:rows, 0:16].rearrange("p (k h) -> p k h", h=H)))
                step(dve.tensor_copy((decS if t == 0 else dec)[:, :], pS[:, DEC:DEC + H * nb]))
                step.done()
                neg = negS if t == 0 else negP
                dve.tensor_tensor(att[0:rows, :, 0:rows], bc(neg[:, :], 1, [rows, H, rows]),
                                  pM[:, :].rearrange("p (h n) -> p h n", h=H)[0:rows, :, 0:rows], ALU.subtract).then_inc(att_e, 1)
                job = ("kTr", t)
                filled(dve, job)
                dve.tensor_tensor(kwS if t == 0 else kw[0:rows, :, :], bank(job)[0:rows, :].rearrange("p (h e) -> p h e", h=H),
                                  bc(cols[0:rows, 3, :], 2, full), ALU.mult).then_inc(free(job), 1)
                dve.wait_ge(att_w, t + 1)
                dve.tensor_tensor(att[0:rows, :, 0:rows], att[0:rows, :, 0:rows],
                                  pK[:, :].rearrange("p (h n) -> p h n", h=H)[0:rows, :, 0:rows], ALU.mult).then_inc(att_p, 1)
                if t + 1 in GROUPS[g]:
                    rows_of(t + 1)
                dve.wait_ge(att_b, t + 1)
                if t == 0:
                    dve.wait_ge(bt_back, 1)
                wi = cols[0:rows, 1, :]
                step(dve.tensor_tensor(num[0:rows, :, :], pB[0:rows, :].rearrange("p (h e) -> p h e", h=H),
                                       bc(wi, 2, full), ALU.mult))
                dve.wait_ge(att_a, t + 1)
                if t == 0:
                    step(dve.tensor_tensor(dtmp[0:rows, :, :], pS[0:rows, DB:DB + H * NB].rearrange("p (h b) -> p h b", h=H),
                                           bc(bmask[:, :], 1, [rows, H, NB]), ALU.mult))
                    step.done()
                    step(dve.tensor_reduce(den[0:rows, :], dtmp[0:rows, :, :], AX.X, ALU.add))
                    step.done()
                    step(dve.tensor_tensor(den[0:rows, :], den[0:rows, :], wi, ALU.mult))
                else:
                    step(dve.tensor_tensor(den[:, :], pS[:, DB:DB + H], wi, ALU.mult))
                step.done()
                dve.tensor_tensor(den[0:rows, :], den[0:rows, :], pS[0:rows, DA:DA + H], ALU.add).then_inc(den_read, 1)
                step(dve.tensor_tensor(num[0:rows, :, :], num[0:rows, :, :],
                                       pA[0:rows, :].rearrange("p (h e) -> p h e", h=H), ALU.add))
                dve.wait_ge(den_read, t + 1)
                step.done()
                step(dve.scalar_tensor_tensor(out=den[0:rows, :], in0=den[0:rows, :], scalar=-1.0, in1=den[0:rows, :],
                                              op0=ALU.mult, op1=ALU.max))
                step.done()
                step(dve.tensor_tensor(den[0:rows, :], den[0:rows, :], cols[0:rows, 2, :], ALU.max))
                step.done()
                step(dve.reciprocal(den[0:rows, :], den[0:rows, :]))
                step.done()
                step(dve.tensor_tensor(num[0:rows, :, :], num[0:rows, :, :], bc(den[0:rows, :], 2, full), ALU.mult))
                step.done()
                dve.tensor_tensor(num[0:rows, :, :], num[0:rows, :, :], sigo[0:rows, slot, :, :], ALU.mult).then_inc(hs_ready, 1)
                if t == 0:
                    step.done()
                    dve.nop(nofuse=True).then_inc(att_done, 1)
                    return
                step(dve.tensor_tensor(npr[:, :], npr[:, :], dec[:, :], ALU.mult))
                step.done()
                dve.wait_ge(att_c, t)
                step(dve.tensor_tensor(npr[:, :], npr[:, :], pS[:, DN:DN + H], ALU.add))
                for h in range(H):
                    step(dve.scalar_tensor_tensor(out=Cp[:, h, :], in0=Cp[:, h, :], scalar=dec[:, h:h + 1],
                                                  in1=pC[:, h * 128:(h + 1) * 128], op0=ALU.mult, op1=ALU.add))
                step.done()
                dve.nop(nofuse=True).then_inc(att_done, 1)

            def sample_states():
                def masked(h):
                    dve.tensor_tensor(vm[h % 2][0:NS], bc(v[0:NS, 0, h, :], 1, [NS, NB, 128]),
                                      bc(bmask[:, :], 2, [NS, NB, 128]), ALU.mult).then_inc(vm_ready, 1)
                masked(0)
                for h in range(H):
                    if h + 1 < H:
                        if h >= 1:
                            dve.wait_ge(cs_new, h)
                        masked(h + 1)
                    dh = decS[:, h * NB:(h + 1) * NB]
                    step(dve.tensor_tensor(Cs[:, h, :, :], Cs[:, h, :, :], bc(dh, 2, [128, NB, 128]), ALU.mult))
                    step(dve.tensor_tensor(nsm[:, h, :], nsm[:, h, :], dh, ALU.mult))
                    step.done()
                    dve.wait_ge(cs_new, h + 1)
                    step(dve.tensor_tensor(nsm[:, h, :], nsm[:, h, :], pS[:, DN + h * NB:DN + (h + 1) * NB], ALU.add))
                    dve.tensor_tensor(Cs[:, h, :, :].rearrange("p b e -> p (b e)"),
                                      Cs[:, h, :, :].rearrange("p b e -> p (b e)"), yps[:, :], ALU.add).then_inc(cs_added, 1)

            def residual(g, j):
                job = ("out", g, j)
                filled(dve, job)
                span = slice(j * 128, (j + 1) * 128)
                if g == 0:
                    step(dve.tensor_tensor(x[0:NS, 0, span], x[0:NS, 0, span], bank(job)[0:NS, 0:128], ALU.add))
                    ins = dve.tensor_tensor(x[:, 1, span], x[:, 1, span], bank(job)[:, 128:256], ALU.add)
                else:
                    ins = dve.tensor_tensor(x[:, 2:5, span], x[:, 2:5, span],
                                            bank(job)[:, 0:384].rearrange("p (t e) -> p t e", t=3), ALU.add)
                ins.then_inc(free(job), 1)

            def norm2(t):
                rows = TILES[t][0]
                dve.wait_ge(sumsq2, t + 1)
                step(dve.reciprocal(rstd[0:rows, 1, t:t + 1], ss[0:rows, 1, t:t + 1]))
                step.done()
                if t == 0:
                    dve.wait_ge(ld_gains, 16)
                dve.scalar_tensor_tensor(out=xn[0:rows, XN_SLOT[t], :], in0=x[0:rows, t, :], scalar=rstd[0:rows, 1, t:t + 1],
                                         in1=gain[0:rows, :], op0=ALU.mult, op1=ALU.mult).then_inc(xn_ready, 1)

            def top_lists(t, part):
                g = TILES[t][2]
                s = score[:, t - GROUPS[g][0]]
                chunks = range(4 * part, 4 * part + 4)
                last = chunks[-1] if t else QC - 1
                evacuated(dve, ("score", g, last))
                evacuated(dve, ("score", g, last - 1))
                topu = topi.bitcast(u32)
                for half in range(2):
                    k = slice(8 * half, 8 * half + 8)
                    for c in chunks:
                        step(dve.max(topv[:, c, k], s[:, c, :]))
                    step.done()
                    for c in chunks:
                        step(dve.max_index(topu[:, c, k], topv[:, c, k], s[:, c, :]))
                    if half == 0:
                        step.done()
                        for c in chunks:
                            step(dve.match_replace(s[:, c, :], topv[:, c, k], s[:, c, :], LOW))
                        step.done()
                if part == 3 or t == 0:
                    step.done()
                    dve.tensor_copy(topf[:, 0:chunks[-1] + 1], topu[:, 0:chunks[-1] + 1]).then_inc(scores_read, 1)
                    dve.wait_ge(scores_read, t + 1)

            def candidates(t):
                nh = N_PICK[t] // TOPK
                first = topf.rearrange("p (h s) k -> p h s k", s=2)[:, 0:nh]
                vals = topv.rearrange("p (h s) k -> p h s k", s=2)[:, 0:nh]
                step(dve.tensor_single_scalar(first[:, :, 0, :], first[:, :, 0, :], 128.0, ALU.mult))
                step.done()
                for out, src in ((cand, vals), (ceid, first)):
                    for i, ni, nj, at in PAIRS:
                        shape = [128, nh, ni, nj]
                        dst = out[:, 0:nh, at:at + ni * nj]
                        if ni == 1:
                            step(dve.tensor_tensor(dst, src[:, :, 0, i:i + 1].broadcast_to([128, nh, nj]), src[:, :, 1, 0:nj], ALU.add))
                        elif nj == 1:
                            step(dve.tensor_tensor(dst, src[:, :, 0, i:i + ni], src[:, :, 1, 0:1].broadcast_to([128, nh, ni]), ALU.add))
                        else:
                            step(dve.tensor_tensor(dst.rearrange("p h (i j) -> p h i j", i=ni),
                                                   src[:, :, 0, i:i + ni].unsqueeze(3).broadcast_to(shape),
                                                   src[:, :, 1, 0:nj].unsqueeze(2).broadcast_to(shape), ALU.add))
                step.done()
                posu = pos.bitcast(u32)
                for half in range(2):
                    k = slice(8 * half, 8 * half + 8)
                    for h in range(nh):
                        step(dve.max(best[:, h, k], cand[:, h, :]))
                    step.done()
                    for h in range(nh):
                        step(dve.max_index(posu[:, h, k], best[:, h, k], cand[:, h, :]))
                    if half == 0:
                        step.done()
                        for h in range(nh):
                            step(dve.match_replace(cand[:, h, :], best[:, h, k], cand[:, h, :], LOW))
                        step.done()
                step.done()
                step(dve.tensor_copy(posf[:, 0:nh], posu[:, 0:nh]))
                step(dve.tensor_tensor(sub[:, t % 2, 0:N_PICK[t]].rearrange("p (h k) -> p h k", h=nh), best[:, 0:nh],
                                       best[:, 0:nh, 0:1].broadcast_to([128, nh, TOPK]), ALU.subtract))
                step.done()

            def experts_of(t, part):
                half = N_PICK[t] // TOPK // 2
                for h in range(half * part, half * (part + 1)):
                    for k in range(TOPK):
                        if h or k >= HITS:
                            step.done(but=HITS - 1)
                        step(dve.scalar_tensor_tensor(out=hit[:, k % HITS, :], in0=iota[:, :], scalar=posf[:, h, k:k + 1],
                                                      in1=ceid[:, h, :], op0=ALU.is_equal, op1=ALU.mult,
                                                      accum_out=eid[:, h * TOPK + k:h * TOPK + k + 1]))
                step.done()
                if part == 1:
                    dve.tensor_copy(idx[:, t % 3, 0:N_PICK[t]], eid[:, 0:N_PICK[t]]).then_inc(picked, 1)
                    dve.wait_ge(picked, t + 1)

            def routing(t):
                return ([lambda p=p: top_lists(t, p) for p in range(4 if t else 1)] + [lambda: candidates(t)] +
                        [lambda p=p: experts_of(t, p) for p in range(2)])

            def dot_products(t, lo, hi):
                first = FIRST_PICK[t]
                if t == 0:
                    dve.wait_ge(spread_x, 48)
                    dve.wait_ge(xn_ready, 1)
                with dve.Fori(lo, hi) as i:
                    for r in range(BLOCK):
                        dve.wait_ge(u_land[r], i * 16 + 16 * (first // BLOCK + 1))
                        dve.scalar_tensor_tensor(out=U[r], in0=U[r], scalar=1.0, in1=xn[:, XN_SLOT[t], :],
                                                 op0=ALU.mult, op1=ALU.mult,
                                                 accum_out=dots[:, t % 2, ds(i * BLOCK + r, 1)]).then_inc(u_free, 1)

            def half_block(t, block, half):
                first = FIRST_PICK[t] + block * BLOCK
                for r in range(4 * half, 4 * half + 4):
                    pick = block * BLOCK + r
                    dve.wait_ge(u_land[r], 16 * (first // BLOCK + 1))
                    dve.scalar_tensor_tensor(out=U[r], in0=U[r], scalar=1.0, in1=xn[:, XN_SLOT[t], :],
                                             op0=ALU.mult, op1=ALU.mult,
                                             accum_out=dots[:, t % 2, pick:pick + 1]).then_inc(u_free, 1)

            def gates(t):
                n = N_PICK[t]
                nh = n // TOPK
                s = sub[:, t % 2, 0:n].rearrange("p (h k) -> p h k", k=TOPK)
                zt = z[:, t % 2, 0:n]
                dve.wait_ge(z_act, t + 1)
                if t >= 2:
                    dve.wait_ge(diag_ready, FIRST_PICK[t - 1])
                step(dve.tensor_reduce(zsum[:, 0:nh], s, AX.X, ALU.add))
                step.done()
                step(dve.reciprocal(zsum[:, 0:nh], zsum[:, 0:nh]))
                step.done()
                step(dve.tensor_tensor(zt.rearrange("p (h k) -> p h k", k=TOPK), s, bc(zsum[:, 0:nh], 2, [128, nh, TOPK]), ALU.mult))
                step.done()
                dve.tensor_tensor(zt, zt, dots[:, t % 2, 0:n], ALU.mult).then_inc(z_ready, 1)

            def final(t):
                rows = TILES[t][0]
                dve.wait_ge(sumsq3, t + 1)
                if t == 0:
                    dve.wait_ge(ld_gains, 32)
                step(dve.reciprocal(rstd[0:rows, 2, t:t + 1], ss[0:rows, 2, t:t + 1]))
                step.done()
                dve.scalar_tensor_tensor(out=x[0:rows, t, :], in0=yps[0:rows, :], scalar=rstd[0:rows, 2, t:t + 1],
                                         in1=gain[0:rows, :], op0=ALU.mult, op1=ALU.mult).then_inc(y_ready, 1)

            dve.wait_ge(consts, N_CONST)
            dve.memset(credit[:, 0:1], 0.0).then_inc(u_free, U_SLOTS)
            dve.memset(credit[:, 1:2], 0.0).then_inc(v_done, V_SLOTS)
            root1(0)
            dve.wait_ge(ld_small, 16 * 11)
            mixer_first(0)
            root1(1)
            dve.tensor_copy(up[:, :, 0:HIST], up[:, :, 128:128 + HIST]).then_inc(hist_ready, 1)
            group_norm(0)
            for t in GROUPS[0]:
                attention(t)
            for j in range(N_OUT):
                residual(0, j)
            for t in GROUPS[0]:
                norm2(t)
            sample_states()
            for part in routing(0):
                part()
            lists, rest = routing(1)[0:4], routing(1)[4:]
            for part in lists:
                part()
            dot_products(0, 0, N_PICK[0] // BLOCK)
            for part in rest:
                part()
            gates(0)
            mixer_first(1)
            group_norm(1)
            for i, t in enumerate(GROUPS[1]):
                attention(t)
                dot_products(1, i, i + 1)
            for j in range(N_OUT):
                residual(1, j)
                if j % 2:
                    half_block(1, 3 + j // 4, j // 2 % 2)
            for t in GROUPS[1]:
                norm2(t)
            final(0)
            lists, rest = routing(2)[0:4], routing(2)[4:]
            dot_products(1, 5, 9)
            lists[0]()
            dot_products(1, 9, 12)
            lists[1]()
            dot_products(1, 12, 15)
            lists[2]()
            dot_products(1, 15, 16)
            gates(1)
            for part in lists[3:] + rest:
                part()
            for t in range(2, 5):
                parts = routing(t + 1) if t < 4 else []
                for i in range(8):
                    dot_products(t, 2 * i, 2 * i + 2)
                    if i < len(parts):
                        parts[i]()
                gates(t)
                final(t - 1)
            final(4)


def kernel(x_prompt, x_sample, state_C, state_n, state_m, state_conv, norm_mix, w_in, b_gates, w_dw, b_dw,
           gn_gain, gn_bias, w_out, norm_ffn, w_query, keys1, keys2, u_experts, v_experts, norm_final):
    import numpy as np
    import concourse.bacc as bacc
    from concourse.bass_utils import run_bass_kernel_spmd

    def chunks(w):
        k, n = w.shape
        return w.reshape(k // 128, 128, n // 128, 128).transpose(2, 1, 0, 3)

    w = H * 128
    wi = w_in[0]
    part = {"q": wi[:, 0:w], "k": wi[:, w:2 * w], "v": wi[:, 2 * w:3 * w], "o": wi[:, 3 * w:4 * w],
            "a": wi[:, 4 * w + 2 * H:4 * w + 2 * H + w], "g": wi[:, 4 * w + 2 * H + w:]}
    part = {name: chunks(p) for name, p in part.items()}
    w_all = np.concatenate([np.stack([part[kind][c] for kind, c in KINDS_IN]), chunks(w_out[0]), chunks(w_query[0])])
    chan = lambda p: p.reshape(CC, 128).T
    ins = {
        "x_sample": x_sample.reshape(NS, D), "x_prompt": x_prompt[0],
        "w_all": w_all,
        "w_gates": wi[:, 4 * w:4 * w + 2 * H].reshape(KC, 128, 2 * H).transpose(1, 0, 2),
        "b_gates": b_gates[0].reshape(2 * H, 1),
        "gain_mix": norm_mix[0].reshape(KC, 128).T,
        "w_dw": w_dw[0].reshape(TAPS, CC, 128).transpose(2, 1, 0),
        "b_dw": chan(b_dw[0]), "gn_gain": chan(gn_gain[0]), "gn_bias": chan(gn_bias[0]),
        "state_C": state_C[0].transpose(2, 1, 0, 3), "state_n": state_n[0].transpose(2, 1, 0), "state_m": state_m[0].T,
        "conv_hist": state_conv[0].reshape(NB, HIST, CC, 128).transpose(3, 2, 0, 1),
        "keys_T": np.stack([keys1[0], keys2[0]], axis=1).reshape(QC, 128, 128).transpose(2, 0, 1),
        "norm_ffn": norm_ffn[0:1], "norm_final": norm_final.reshape(1, D),
        "u_experts": u_experts[0], "v_experts": v_experts[0],
    }
    outs = {"y_p": (SEQ, D), "y_s": (NS, D), "C_p": (128, H, 128), "n_p": (128, H), "m_p": (H, 1),
            "conv_p": (128, CC, HIST), "C_s": (128, H, NB, 128), "n_s": (128, H, NB), "m_s": (H, NB),
            "conv_s": (128, CC, NB, HIST)}
    nc = bacc.Bacc("TRN2", target_bir_lowering=False, num_devices=1)
    ins = {name: np.ascontiguousarray(p) for name, p in ins.items()}
    a = {name: nc.dram_tensor(f"in_{name}", p.shape, mybir.dt.from_np(p.dtype), kind="ExternalInput").ap()
         for name, p in ins.items()}
    o = {name: nc.dram_tensor(f"out_{name}", shape, mybir.dt.float32, kind="ExternalOutput").ap()
         for name, shape in outs.items()}
    build(nc, a, o)
    res = run_bass_kernel_spmd(nc, [{f"in_{name}": p for name, p in ins.items()}], core_ids=[0]).results[0]
    r = {name: np.asarray(res[f"out_{name}"]) for name in outs}
    return (r["y_p"].reshape(1, SEQ, D), r["y_s"].reshape(NB, NT, D),
            np.ascontiguousarray(r["C_p"].transpose(1, 0, 2))[None, None],
            np.ascontiguousarray(r["n_p"].T)[None, None],
            r["m_p"].reshape(1, 1, H),
            np.ascontiguousarray(r["conv_p"].transpose(2, 1, 0)).reshape(1, 1, HIST, CC * 128),
            np.ascontiguousarray(r["C_s"].transpose(2, 1, 0, 3))[None],
            np.ascontiguousarray(r["n_s"].transpose(2, 1, 0))[None],
            np.ascontiguousarray(r["m_s"].T)[None],
            np.ascontiguousarray(r["conv_s"].transpose(2, 3, 1, 0)).reshape(1, NB, HIST, CC * 128))
```

```python
import concourse.bass as bass
from concourse import mybir
from contextlib import ExitStack

D = 1024
KC = D // 128
SEQ, NB, NT = 512, 8, 4
NS = NB * NT
H = 4
CC = 4
TAPS = 31
HIST = TAPS - 1
QC = 16
PH = 8
TOPK = 16
PICKS = PH * TOPK
EPS = 1e-6
NEG = -1e30
LOW = -3e38

PAIRS = [(0, 1, 16, 0), (1, 1, 8, 16), (2, 1, 5, 24), (3, 1, 4, 29), (4, 1, 3, 33), (5, 3, 2, 36), (8, 8, 1, 42)]
CAND = 50
HITS = 8

TILES = [(NS, 0, 0), (128, NS, 0), (128, 0, 1), (128, 128, 1), (128, 256, 1)]
GROUPS = [(0, 1), (2, 3, 4)]
WIDTH = [NS + 128, 384]
GMAX = 384
XN_SLOT = [0, 1, 2, 3, 0]

N_IN, N_OUT = 24, 8
N_W = N_IN + N_OUT + QC
W_SLOTS = 4
KINDS_IN = [("g", c) if h == 0 else ("a", c) for c in range(CC) for h in range(2)] + \
           [(kind, c) for kind in "kqvo" for c in range(H)]
CONV_RUNS = [((0,), (1,), (2, 3)), ((0, 1), (2, 3))]
PAUSE = 18

U_SLOTS, V_SLOTS = 8, 4
N_PICK = [PICKS * NS // 128] + [PICKS] * 4
FIRST_PICK = [sum(N_PICK[:t]) for t in range(5)]
BLOCK = 8
LAST_PE, LAST_DVE = 12, 4
LEAD = 4


def pe_picks(t):
    return N_PICK[t] * LAST_PE // 16 if t == 4 else N_PICK[t]


def pp_jobs():
    jobs = []
    for g, tiles in enumerate(GROUPS):
        jobs += [("xT", t, half) for t in tiles for half in range(2)]
        jobs += [("gate_i", g), ("gate_f", g)]
        jobs += [("in", g, i) for i in range(N_IN)]
        jobs += [("mean", g, c) for c in range(CC)] + [("var", g, c) for c in range(CC)]
        for t in tiles:
            jobs += [("kTr", t), ("hT", t)]
        jobs += [("out", g, j) for j in range(N_OUT)]
        jobs += [("x2T", t, half) for t in tiles for half in range(2)]
        for c in range(0, QC, 2):
            jobs += [("query", g, c), ("query", g, c + 1), ("score", g, c), ("score", g, c + 1)]
    return {name: n for n, name in enumerate(jobs)}


class Steps:

    def __init__(self, engine, sem):
        self.engine, self.sem, self.n = engine, sem, 0

    def __call__(self, ins):
        self.n += 1
        ins.then_inc(self.sem, 1)

    def done(self, but=0):
        if self.n - but > 0:
            self.engine.wait_ge(self.sem, self.n - but)


def build(nc, a, o):
    f32, u32 = mybir.dt.float32, mybir.dt.uint32
    ALU, ACT, AX = mybir.AluOpType, mybir.ActivationFunctionType, mybir.AxisListType
    ds = bass.ds
    J = pp_jobs()

    with ExitStack() as ctx:
        def sb(name, shape, dt=f32):
            return ctx.enter_context(nc.sbuf_tensor(name, shape, dt))

        def sem(name):
            return ctx.enter_context(nc.semaphore(name))

        def view(region_, at, **dims):
            n = 1
            for d in dims.values():
                n *= d
            flat = region_[:, at:at + n]
            if len(dims) == 1:
                return flat
            names = " ".join(dims)
            return flat.rearrange(f"p ({names}) -> p {names}", **dims)

        W = sb("w_ring", [128, W_SLOTS, KC, 128])
        x = sb("x_res", [128, 5, D])
        xn = sb("x_normed", [128, 4, D])
        xnT = sb("x_normed_T", [128, KC, GMAX])
        v = sb("v_rows", [128, 3, H, 128])
        x4n = v[:, 0:2, :, :].rearrange("p t h e -> p (t h e)")
        sigo = sb("sig_o_T", [128, H, GMAX])
        up = sb("u_prompt", [128, CC, HIST + GMAX])
        mixT = sb("mix_T", [128, KC, GMAX])
        region = sb("region", [128, 3 * QC * 128])
        qT = view(region, 0, h=H, n=GMAX)
        kT = view(region, H * GMAX, h=H, n=GMAX)
        cv = view(region, 2 * H * GMAX, c=CC, n=GMAX)
        ct = view(region, 3 * H * GMAX, c=CC, n=GMAX)
        score = view(region, 0, t=3, c=QC, k=128)
        qry = mixT[:, 0:2, :]
        u_ring = sb("u_ring", [128, U_SLOTS * D])
        v_ring = sb("v_ring", [128, V_SLOTS * D])
        U = [u_ring[:, s * D:(s + 1) * D] for s in range(U_SLOTS)]
        V = [v_ring[:, s * D:(s + 1) * D] for s in range(V_SLOTS)]
        Cs = view(u_ring, 0, h=H, b=NB, e=128)
        us = view(v_ring, 0, c=CC, b=NB, w=HIST + NT)
        AFTER_US = CC * NB * (HIST + NT)
        vm = [view(v_ring, AFTER_US + 1024 * i, b=NB, e=128) for i in range(2)]
        qm = [view(v_ring, AFTER_US + h * NB * (NS + NT), n=NB * (NS + NT)) for h in range(H)]
        Cp = sb("C_prompt", [128, H, 128])
        keys = sb("keys_T", [128, QC, 128])
        gain = sb("gain", [128, D])
        rowsIF = sb("rows_if", [4, 2, GMAX])
        scratch = sb("scratch", [128, 2480])
        att = view(scratch, 0, h=H, n=128)
        num = view(scratch, 512, h=H, e=128)
        kw = view(scratch, 1024, h=H, e=128)
        kwS = sigo[0:NS, :, 256:384]
        R = view(scratch, 1536, k=7, n=128)[0:4]
        lf = scratch[0:4, 1536:1536 + GMAX]
        topv = view(scratch, 0, c=QC, k=TOPK)
        topi = view(scratch, 256, c=QC, k=TOPK)
        topf = view(scratch, 512, c=QC, k=TOPK)
        cand = view(scratch, 768, h=PH, c=CAND)
        ceid = view(scratch, 1168, h=PH, c=CAND)
        best = view(scratch, 1568, h=PH, k=TOPK)
        pos = view(scratch, 1696, h=PH, k=TOPK)
        posf = view(scratch, 1824, h=PH, k=TOPK)
        hit = view(scratch, 1952, k=HITS, c=CAND)
        eid = scratch[:, 2352:2480]
        idx = sb("expert_idx", [128, 3, PICKS], u32)
        sub = sb("score_minus_max", [128, 2, PICKS])
        dots = sb("dots", [128, 2, PICKS])
        z = sb("z", [128, 2, PICKS])
        acc = xn[:, 1, :]
        u_idx = sb("u_idx_now", [128, 2, BLOCK], u32)
        v_idx = sb("v_idx_now", [128, 2, BLOCK], u32)
        last_idx = sb("v_idx_last", [128, 2 * BLOCK], u32)
        diag = sb("diag", [128, V_SLOTS, 128])
        ident = sb("ident", [128, 128])
        fold = sb("fold", [128, NS])
        halves = sb("halves", [128, 128])
        negP = sb("neg_prompt", [128, 128])
        negS = sb("neg_sample", [NS, NS])
        sel = sb("sel", [4, H, 128])
        bmask = sb("batch_mask", [NS, NB])
        ones = sb("ones", [128, 1])
        iota_i = sb("iota_i", [128, CAND], mybir.dt.int32)
        iota = sb("iota", [128, CAND])
        zero = sb("zero", [4, 1])
        keepS = sb("keep_sample", [4, NS])
        dropS = sb("drop_sample", [4, NS])
        eps = sb("eps", [128, 1])
        gmix = sb("gain_mix", [128, KC])
        wg = sb("w_gates", [128, KC, 2 * H])
        bi = sb("b_i", [4, 1])
        bf = sb("b_f", [4, 1])
        wdw = sb("w_dw", [128, CC, TAPS])
        bdw = sb("b_dw", [128, CC])
        gng = sb("gn_gain", [128, CC])
        gnb = sb("gn_bias", [128, CC])
        npr = sb("n_prompt", [128, H])
        nsm = sb("n_sample", [128, H, NB])
        m0 = sb("m_sample", [4, NB])
        mprev = sb("m_prompt", [4, 1])
        mlast = sb("M_last", [4, NB])
        decR = sb("decay_rows", [4, NB])
        cols = sb("cols", [128, 4, H])
        dec = sb("decay", [128, H])
        decS = sb("decay_sample", [128, H * NB])
        dtmp = sb("den_tmp", [128, H, NB])
        den = sb("den", [128, H])
        ss = sb("sum_squares", [128, 3, 5])
        rstd = sb("rstd", [128, 3, 5])
        zsum = sb("z_sum", [128, PH])
        credit = sb("credit", [128, 2])

        pp = [ctx.enter_context(nc.psum_tensor(f"pp{i}", [128, 512], f32)) for i in range(2)]
        pa = [ctx.enter_context(nc.psum_tensor(f"pa{i}", [128, 512], f32)) for i in range(4)]
        yps = ctx.enter_context(nc.psum_tensor("y", [128, D], f32))
        pM, pA = pa[0], pa[0]
        pK, pC = pa[1], pa[1]
        pB, pS = pa[2], pa[3]
        DEC, DA, DB, DN = 16, 48, 52, 84

        ld_x = [sem(f"ld_x{t}") for t in range(5)]
        ld_small, ld_keys, ld_state, ld_gains = sem("ld_small"), sem("ld_keys"), sem("ld_state"), sem("ld_gains")
        w_land = [sem(f"w_land{s}") for s in range(W_SLOTS)]
        consts = sem("consts")
        pp_full, pp_free = sem("pp_full"), [sem(f"pp_free{i}") for i in range(2)]
        sumsq1, rstd1, xs_ready = sem("sumsq1"), sem("rstd1"), sem("xs_ready")
        neg_f, log_f = sem("neg_f"), sem("log_f")
        u_ready, centred, squared, normed = sem("u_ready"), sem("centred"), sem("squared"), sem("normed")
        mix_c, conv_done, hist_ready = sem("mix_c"), sem("conv_done"), sem("hist_ready")
        rows_set, rows_exp = sem("rows_set"), sem("rows_exp")
        att_in, att_e, att_w, att_p = sem("att_in"), sem("att_e"), sem("att_w"), sem("att_p")
        att_b, att_a, att_c, att_done = sem("att_b"), sem("att_a"), sem("att_c"), sem("att_done")
        vm_ready, cs_new, cs_added = sem("vm_ready"), sem("cs_new"), sem("cs_added")
        hs_ready, den_read = sem("hs_ready"), sem("den_read")
        sumsq2, xn_ready = sem("sumsq2"), sem("xn_ready")
        spread_x = sem("spread_x")
        scores_read, picked = sem("scores_read"), sem("picked")
        u_land = [sem(f"u_land{s}") for s in range(U_SLOTS)]
        v_land = [sem(f"v_land{s}") for s in range(V_SLOTS)]
        u_free, v_done, diag_ready = sem("u_free"), sem("v_done"), sem("diag_ready")
        staged, last_sum = sem("staged"), sem("last_sum")
        z_act, z_ready = sem("z_act"), sem("z_ready")
        sumsq3, y_ready = sem("sumsq3"), sem("y_ready")
        out_s, out_p, out_y = sem("out_s"), sem("out_p"), sem("out_y")
        share = sem("share")
        s_act, s_dve, s_pool = sem("s_act"), sem("s_dve"), sem("s_pool")
        N_CONST = 22

        def filled(eng, job):
            eng.wait_ge(pp_full, J[job] + 1)

        def evacuated(eng, job):
            eng.wait_ge(pp_free[J[job] % 2], J[job] // 2 + 1)

        def bank(job):
            return pp[J[job] % 2]

        def free(job):
            return pp_free[J[job] % 2]

        def weight_job(n):
            g, i = divmod(n, N_W)
            if i < N_IN:
                return "in", g, i
            return ("out", g, i - N_IN) if i < N_IN + N_OUT else ("query", g, i - N_IN - N_OUT)

        block = ctx.enter_context(nc.Block())

        @block.sync
        def _(sp):
            def load_x(t):
                rows = TILES[t][0]
                src = a["x_sample"] if t == 0 else a["x_prompt"][(t - 1) * 128:t * 128, :]
                sp.dma_start(x[0:rows, t, :], src).then_inc(ld_x[t], 16)

            def load_w(n):
                if n >= W_SLOTS:
                    sp.wait_ge(pp_full, J[weight_job(n - W_SLOTS)] + 1)
                sp.dma_start(W[:, n % W_SLOTS, :, :], a["w_all"][n % N_W]).then_inc(w_land[n % W_SLOTS], 16)

            load_x(0)
            load_x(1)
            sp.dma_start(gmix[:, :], a["gain_mix"]).then_inc(ld_small, 16)
            sp.dma_start(wg[:, :, :], a["w_gates"]).then_inc(ld_small, 16)
            sp.dma_start(bi[:, :], a["b_gates"][0:H, :]).then_inc(ld_small, 16)
            sp.dma_start(bf[:, :], a["b_gates"][H:2 * H, :]).then_inc(ld_small, 16)
            for n in range(W_SLOTS):
                load_w(n)
            for dst, name in ((wdw[:, :, :], "w_dw"), (bdw[:, :], "b_dw"), (gng[:, :], "gn_gain"),
                              (gnb[:, :], "gn_bias"), (m0[:, :], "state_m"), (nsm[:, :, :], "state_n"),
                              (us[:, :, :, 0:HIST], "conv_hist")):
                sp.dma_start(dst, a[name]).then_inc(ld_small, 16)
            for t in (2, 3, 4):
                load_x(t)
            sp.dma_start(Cs, a["state_C"]).then_inc(ld_state, 16)
            sp.dma_start(keys[:, :, :], a["keys_T"]).then_inc(ld_keys, 16)
            sp.dma_start(gain[:, :], a["norm_ffn"].broadcast_to([128, D])).then_inc(ld_gains, 16)
            for n in range(W_SLOTS, N_W):
                load_w(n)
            sp.wait_ge(u_ready, len(CONV_RUNS[0]))
            sp.dma_start(o["conv_s"], us[:, :, :, NT:NT + HIST]).then_inc(out_s, 16)
            sp.wait_ge(cs_added, H)
            sp.dma_start(o["C_s"], Cs).then_inc(out_s, 16)
            sp.dma_start(o["n_s"], nsm[:, :, :]).then_inc(out_s, 16)
            sp.dma_start(o["m_s"], m0[:, :]).then_inc(out_s, 16)
            sp.wait_ge(xn_ready, 1)
            for s in range(1, 4):
                sp.dma_start(xn[NS * s:NS * (s + 1), 0, :], xn[0:NS, 0, :]).then_inc(spread_x, 16)
            for n in range(N_W, 2 * N_W - QC + W_SLOTS):
                load_w(n)
            sp.wait_ge(u_ready, len(CONV_RUNS[0]) + len(CONV_RUNS[1]))
            sp.dma_start(o["conv_p"], up[:, :, GMAX:GMAX + HIST]).then_inc(out_p, 16)
            sp.wait_ge(att_done, 5)
            sp.dma_start(o["C_p"], Cp[:, :, :]).then_inc(out_p, 16)
            sp.dma_start(o["n_p"], npr[:, :]).then_inc(out_p, 16)
            sp.dma_start(o["m_p"], mprev[:, :]).then_inc(out_p, 16)
            sp.wait_ge(xn_ready, 5)
            sp.dma_start(gain[:, :], a["norm_final"].broadcast_to([128, D])).then_inc(ld_gains, 16)
            for n in range(2 * N_W - QC + W_SLOTS, 2 * N_W):
                load_w(n)
            for t in range(5):
                sp.wait_ge(y_ready, t + 1)
                dst = o["y_s"] if t == 0 else o["y_p"][(t - 1) * 128:t * 128, :]
                sp.dma_start(dst, x[0:TILES[t][0], t, :]).then_inc(out_y, 16)
            sp.wait_ge(out_y, 16 * 5)
            sp.wait_ge(out_s, 16 * 4)
            sp.wait_ge(out_p, 16 * 4)

        @block.gpsimd
        def _(pool):
            step = Steps(pool, s_pool)
            for t, value in ((ident, 0.0), (fold, 0.0), (halves, 1.0 / 64), (negP, 0.0), (negS, 0.0),
                             (bmask, 1.0), (dropS, 0.0), (keepS, 1.0)):
                step(pool.memset(t[:, :], value))
            step(pool.memset(sel[:, :, :], 0.0))
            step.done()
            n_const = [0]

            def const(ins):
                n_const[0] += 1
                ins.then_inc(consts, 1)

            const(pool.affine_select(out=ident[:, :], in_=ident[:, :], compare_op=ALU.not_equal, fill=1.0,
                                     base=0, pattern=[[-1, 128]], channel_multiplier=1))
            step(pool.affine_select(out=negS[:, :], in_=negS[:, :], compare_op=ALU.is_ge, fill=NEG,
                                    base=0, pattern=[[-4, NB], [0, NT]], channel_multiplier=1))
            step(pool.affine_select(out=bmask[:, :], in_=bmask[:, :], compare_op=ALU.is_ge, fill=0.0,
                                    base=0, pattern=[[-4, NB]], channel_multiplier=1))
            step(pool.iota(iota_i[:, :], [[1, CAND]], base=0, channel_multiplier=0))
            const(pool.affine_select(out=negP[:, :], in_=negP[:, :], compare_op=ALU.is_ge, fill=NEG,
                                     base=0, pattern=[[1, 128]], channel_multiplier=-1))
            const(pool.affine_select(out=sel[:, :, :], in_=sel[:, :, :], compare_op=ALU.not_equal, fill=1.0,
                                     base=0, pattern=[[-1, H], [0, 128]], channel_multiplier=1))
            for at, base, mul in ((0, 63, -1), (64, -64, 1)):
                const(pool.affine_select(out=halves[:, at:at + 64], in_=halves[:, at:at + 64], compare_op=ALU.is_ge,
                                         fill=0.0, base=base, pattern=[[0, 64]], channel_multiplier=mul))
            const(pool.memset(keepS[:, :].rearrange("p (b t) -> p b t", t=NT)[:, :, 0:1], 0.0))
            const(pool.memset(dropS[:, :].rearrange("p (b t) -> p b t", t=NT)[:, :, 0:1], NEG))
            const(pool.memset(ones[:, :], 1.0))
            const(pool.memset(eps[:, :], EPS))
            const(pool.memset(up[:, :, 0:HIST], 0.0))
            const(pool.memset(zero[:, :], 0.0))
            const(pool.memset(view(v_ring, AFTER_US, n=H * NB * (NS + NT)), 0.0))
            const(pool.memset(npr[:, :], 0.0))
            const(pool.memset(mprev[:, :], 0.0))
            const(pool.memset(Cp[:, :, :], 0.0))
            for i in range(3):
                const(pool.memset(ss[:, i, :], 1.0))
            step.done()
            const(pool.affine_select(out=negS[:, :], in_=negS[:, :], compare_op=ALU.is_ge, fill=NEG,
                                     base=0, pattern=[[4, NB], [1, NT]], channel_multiplier=-1))
            const(pool.affine_select(out=bmask[:, :], in_=bmask[:, :], compare_op=ALU.is_ge, fill=0.0,
                                     base=NT - 1, pattern=[[4, NB]], channel_multiplier=-1))
            const(pool.tensor_copy(iota[:, :], iota_i[:, :]))
            for s in range(4):
                ins = pool.affine_select(out=fold[:, :], in_=fold[:, :], compare_op=ALU.not_equal, fill=1.0,
                                         base=-NS * s, pattern=[[-1, NS]], channel_multiplier=1)
                if s < 3:
                    step(ins)
                    step.done()
                else:
                    const(ins)
            assert n_const[0] == N_CONST
            pool.wait_ge(consts, N_CONST)

            turns = [0]
            rings = {"u": (a["u_experts"], u_idx, U, U_SLOTS, u_land, u_free),
                     "v": (a["v_experts"], v_idx, V, V_SLOTS, v_land, v_done)}

            def gathers(*streams):
                n = len(streams)
                base = turns[0]
                blocks = streams[0][3] - streams[0][2]
                with pool.Fori(0, blocks // 2) as i:
                    for h in range(2):
                        for kind, t, lo, _ in streams:
                            src = idx[:, t % 3, :]
                            pool.tensor_copy(rings[kind][1][:, h, :],
                                             src[:, ds(i * 2 * BLOCK + (lo + h) * BLOCK, BLOCK)]).then_inc(staged, 1)
                        pool.wait_ge(staged, i * 2 * n + (base + (h + 1) * n))
                        for r in range(BLOCK):
                            for kind, t, lo, _ in streams:
                                table, now, ring, slots, land, freed = rings[kind]
                                s = r % slots
                                pool.wait_ge(freed, i * 2 * BLOCK + ((lo + h) * BLOCK + r + FIRST_PICK[t] + 1))
                                pool.nop(nofuse=True)
                                pool.indirect_dma_start(
                                    out=ring[s], out_offset=None, in_=table,
                                    in_offset=bass.IndirectOffsetOnAxis(ap=now[:, h, r:r + 1], axis=0)
                                ).then_inc(land[s], 16)
                turns[0] += n * blocks

            pool.wait_ge(out_s, 16 * 4)
            pool.wait_ge(picked, 1)
            gathers(("u", 0, 0, 4))
            gathers(("v", 0, 0, 4))
            pool.wait_ge(picked, 2)
            gathers(("u", 1, 0, 16))
            gathers(("v", 1, 0, LEAD))
            pool.wait_ge(picked, 3)
            gathers(("u", 2, 0, 16 - LEAD), ("v", 1, LEAD, 16))
            gathers(("u", 2, 16 - LEAD, 16))
            for t in range(2, 4):
                pool.wait_ge(picked, t + 2)
                gathers(("u", t + 1, 0, 16), ("v", t, 0, 16))
            v_first, u_first = FIRST_PICK[4], FIRST_PICK[4] + N_PICK[4]
            src = idx[:, 4 % 3, :]
            with pool.Fori(0, N_PICK[4] // 16) as i:
                n_pe, n_dve = 0, 0
                for r in range(16):
                    if r % BLOCK == 0:
                        pool.wait_ge(u_free, i * LAST_DVE + (u_first + U_SLOTS - LAST_DVE // 2 + n_dve))
                        pool.tensor_copy(last_idx[:, r:r + BLOCK], src[:, ds(i * 16 + r, BLOCK)]).then_inc(staged, 1)
                        pool.wait_ge(staged, i * 2 + (turns[0] + r // BLOCK + 1))
                    if r % 4 == 3:
                        pool.wait_ge(u_free, i * LAST_DVE + (u_first + n_dve + 1 + U_SLOTS - LAST_DVE))
                        out, land = U[n_dve], u_land[n_dve]
                        n_dve += 1
                    else:
                        s = n_pe % V_SLOTS
                        pool.wait_ge(v_done, i * LAST_PE + (v_first + n_pe + 1))
                        out, land = V[s], v_land[s]
                        n_pe += 1
                    pool.nop(nofuse=True)
                    pool.indirect_dma_start(
                        out=out, out_offset=None, in_=a["v_experts"],
                        in_offset=bass.IndirectOffsetOnAxis(ap=last_idx[:, r:r + 1], axis=0)).then_inc(land, 16)

        @block.tensor
        def _(pe):
            def job(name):
                n = J[name]
                if n >= 2:
                    pe.wait_ge(pp_free[n % 2], n // 2)
                return pp[n % 2]

            def transposes(name, src, rows, cols_of, count):
                p = job(name)
                for i in range(count):
                    ins = pe.transpose(p[:, i * 128:i * 128 + rows], cols_of(src, i), ident[0:rows, 0:rows])
                ins.then_inc(pp_full, 1)

            def weights(n):
                pe.wait_ge(w_land[n % W_SLOTS], 16 * (n // W_SLOTS + 1))
                return W[:, n % W_SLOTS, :, :]

            def project(name, g, n, actT, rows_out):
                w = weights(n)
                p = job(name)
                if rows_out:
                    parts = [(i, TILES[t][0], TILES[t][1]) for i, t in enumerate(GROUPS[g])]
                else:
                    parts = [(0, 128, 0)]
                for i, rows, col in parts:
                    for k in range(KC):
                        if rows_out:
                            ins = pe.matmul(p[0:rows, i * 128:(i + 1) * 128], actT[:, k, col:col + rows], w[:, k, :],
                                            start=(k == 0), stop=(k == KC - 1))
                        else:
                            ins = pe.matmul(p[:, 0:WIDTH[g]], w[:, k, :], actT[:, k, 0:WIDTH[g]],
                                            start=(k == 0), stop=(k == KC - 1))
                ins.then_inc(pp_full, 1)

            def inputs(g):
                for t in GROUPS[g]:
                    rows = TILES[t][0]
                    pe.wait_ge(xs_ready, t + 1)
                    for half in range(2):
                        transposes(("xT", t, half), x4n if t == 4 else xn[0:rows, XN_SLOT[t], :], rows,
                                   lambda s, i, half=half: s[:, (4 * half + i) * 128:(4 * half + i + 1) * 128], 4)
                for t in GROUPS[g]:
                    for half in range(2):
                        evacuated(pe, ("xT", t, half))
                if g == 0:
                    pe.wait_ge(ld_small, 16 * 11)
                for kind, at in (("gate_i", 0), ("gate_f", H)):
                    p = job((kind, g))
                    for k in range(KC):
                        ins = pe.matmul(p[0:H, 0:WIDTH[g]], wg[:, k, at:at + H], xnT[:, k, 0:WIDTH[g]],
                                        start=(k == 0), stop=(k == KC - 1))
                    ins.then_inc(pp_full, 1)
                project_inputs(g, range(PAUSE))

            def project_inputs(g, chunks):
                for i in chunks:
                    project(("in", g, i), g, g * N_W + i, xnT, KINDS_IN[i][0] == "v")

            def conv_statistics(g):
                n = WIDTH[g]
                pe.wait_ge(conv_done, g + 1)
                for c in range(CC):
                    p = job(("mean", g, c))
                    pe.matmul(p[:, 0:n], halves[:, :], cv[:, c, 0:n], start=True, stop=True).then_inc(pp_full, 1)
                for c in range(CC):
                    pe.wait_ge(squared, CC * g + c + 1)
                    p = job(("var", g, c))
                    pe.matmul(p[:, 0:n], halves[:, :], ct[:, c, 0:n], start=True, stop=True).then_inc(pp_full, 1)

            def attention(t):
                rows, col, g = TILES[t]
                nb = NB if t == 0 else 1
                slot = t - GROUPS[g][0]
                span = slice(col, col + rows)
                pe.wait_ge(rows_exp, t + 1)
                if t >= 1:
                    pe.wait_ge(att_done, t)
                for kind, k in enumerate((1, 3, 4, 5)):
                    pe.transpose(pS[0:rows, 4 * kind:4 * kind + 4], R[:, k, 0:rows], ident[0:4, 0:4])
                for h in range(H):
                    pe.matmul(pS[:, DEC + h * nb:DEC + (h + 1) * nb], sel[:, h, :], decR[:, 0:nb], start=True, stop=True)
                for h in range(H):
                    pe.matmul(pM[0:rows, h * 128:h * 128 + rows], sel[:, h, 0:rows], R[:, 2, 0:rows], start=True, stop=True)
                for h in range(H):
                    ins = pe.matmul(pK[0:rows, h * 128:h * 128 + rows], kT[:, h, span], qT[:, h, span], start=True, stop=True)
                ins.then_inc(att_in, 1)
                if t == 0:
                    pe.wait_ge(ld_state, 16)
                    for h in range(H):
                        for b in range(NB):
                            pe.matmul(pB[0:NS, h * 128:(h + 1) * 128], qm[h][:, b * NS:(b + 1) * NS], Cs[:, h, b, :],
                                      start=(b == 0), stop=(b == NB - 1))
                    pe.wait_ge(att_e, t + 1)
                    for h in range(H):
                        ins = pe.matmul(pS[0:rows, DB + h * NB:DB + (h + 1) * NB], qT[:, h, 0:NS], nsm[:, h, :],
                                        start=True, stop=True)
                    ins.then_inc(att_b, 1)
                else:
                    for h in range(H):
                        pe.matmul(pB[:, h * 128:(h + 1) * 128], qT[:, h, span], Cp[:, h, :], start=True, stop=True)
                    pe.wait_ge(att_e, t + 1)
                    for h in range(H):
                        ins = pe.matmul(pS[:, DB + h:DB + h + 1], qT[:, h, span], npr[:, h:h + 1], start=True, stop=True)
                    ins.then_inc(att_b, 1)
                p = job(("kTr", t))
                for h in range(H):
                    ins = pe.transpose(p[0:rows, h * 128:(h + 1) * 128], kT[:, h, span], ident[:, :])
                ins.then_inc(pp_full, 1)
                pe.wait_ge(att_p, t + 1)
                for h in range(H):
                    pe.matmul(pA[0:rows, h * 128:(h + 1) * 128], att[0:rows, h, 0:rows], v[0:rows, slot, h, :],
                              start=True, stop=True)
                for h in range(H):
                    ins = pe.matmul(pS[0:rows, DA + h:DA + h + 1], att[0:rows, h, 0:rows], ones[0:rows, :],
                                    start=True, stop=True)
                ins.then_inc(att_a, 1)
                evacuated(pe, ("kTr", t))
                pe.wait_ge(den_read, t + 1)
                if t:
                    for h in range(H):
                        pe.matmul(pC[:, h * 128:(h + 1) * 128], kw[:, h, :], v[:, slot, h, :], start=True, stop=True)
                    for h in range(H):
                        ins = pe.matmul(pS[:, DN + h:DN + h + 1], kw[:, h, :], ones[:, :], start=True, stop=True)
                    ins.then_inc(att_c, 1)
                pe.wait_ge(hs_ready, t + 1)
                transposes(("hT", t), num, rows, lambda s, h, rows=rows: s[0:rows, h, :], H)

            def outputs(g):
                pe.wait_ge(mix_c, CC * (g + 1))
                for t in GROUPS[g]:
                    evacuated(pe, ("hT", t))
                for j in range(N_OUT):
                    project(("out", g, j), g, g * N_W + N_IN + j, mixT, True)

            def sample_states(h):
                pe.wait_ge(vm_ready, h + 1)
                if h:
                    pe.wait_ge(cs_added, h)
                for half in range(2):
                    pe.matmul(yps[:, half * 512:(half + 1) * 512], kwS[:, h, :],
                              vm[h % 2][0:NS, 4 * half:4 * half + 4, :].rearrange("p b e -> p (b e)"),
                              start=True, stop=True)
                pe.matmul(pS[:, DN + h * NB:DN + (h + 1) * NB], kwS[:, h, :], bmask[:, :],
                          start=True, stop=True).then_inc(cs_new, 1)

            def queries(g):
                for t in GROUPS[g]:
                    rows = TILES[t][0]
                    pe.wait_ge(xn_ready, t + 1)
                    for half in range(2):
                        transposes(("x2T", t, half), xn, rows,
                                   lambda s, i, t=t, half=half, rows=rows:
                                   s[0:rows, XN_SLOT[t], (4 * half + i) * 128:(4 * half + i + 1) * 128], 4)
                for t in GROUPS[g]:
                    for half in range(2):
                        evacuated(pe, ("x2T", t, half))
                if g == 0:
                    pe.wait_ge(ld_keys, 16)
                for pair in range(0, QC, 2):
                    for c in (pair, pair + 1):
                        project(("query", g, c), g, g * N_W + N_IN + N_OUT + c, xnT, False)
                    for c in (pair, pair + 1):
                        p = job(("score", g, c))
                        evacuated(pe, ("query", g, c))
                        for i, t in enumerate(GROUPS[g]):
                            rows, col, _ = TILES[t]
                            low = c // 4 * NS if t == 0 else 0
                            ins = pe.matmul(p[low:low + rows, i * 128:(i + 1) * 128], qry[:, c % 2, col:col + rows],
                                            keys[:, c, :], start=True, stop=True)
                        ins.then_inc(pp_full, 1)
                    if g == 0 and 2 <= pair < 2 + 2 * H:
                        sample_states(pair // 2 - 1)

            def experts(t):
                rows = TILES[t][0]
                if t:
                    pe.wait_ge(y_ready, t)
                for half in range(2):
                    pe.matmul(yps[0:rows, half * 512:(half + 1) * 512], ident[0:rows, 0:rows],
                              x[0:rows, t, half * 512:(half + 1) * 512], start=True, stop=True, skip_group_check=True)
                first = FIRST_PICK[t]
                turn = LAST_PE if t == 4 else BLOCK
                with pe.Fori(0, pe_picks(t) // turn) as i:
                    for r in range(turn):
                        s = r % V_SLOTS
                        pe.wait_ge(v_land[s], i * (16 * turn // V_SLOTS) + 16 * (first // V_SLOTS + r // V_SLOTS + 1))
                        pe.wait_ge(diag_ready, i * turn + (first + r + 1))
                        for half in range(2):
                            ins = pe.matmul(yps[0:rows, half * 512:(half + 1) * 512], diag[:, s, 0:rows],
                                            V[s][:, half * 512:(half + 1) * 512], start=False, stop=True,
                                            skip_group_check=True)
                        ins.then_inc(v_done, 1)

            pe.wait_ge(consts, N_CONST)
            inputs(0)
            project_inputs(0, range(PAUSE, N_IN))
            evacuated(pe, ("in", 0, N_IN - 1))
            evacuated(pe, ("in", 0, N_IN - 2))
            conv_statistics(0)
            attention(0)
            attention(1)
            outputs(0)
            queries(0)
            inputs(1)
            experts(0)
            project_inputs(1, range(PAUSE, N_IN))
            evacuated(pe, ("in", 1, N_IN - 1))
            evacuated(pe, ("in", 1, N_IN - 2))
            conv_statistics(1)
            for t in GROUPS[1]:
                attention(t)
            outputs(1)
            queries(1)
            for t in range(1, 5):
                experts(t)

        @block.scalar
        def _(act):
            step = Steps(act, s_act)
            A = act.activation

            def norm1(g):
                for t in GROUPS[g]:
                    rows = TILES[t][0]
                    act.wait_ge(ld_x[t], 16)
                    step.done()
                    step(A(xn[0:rows, XN_SLOT[t] if g == 0 else 2, :], x[0:rows, t, :], ACT.Square, accum_out=ss[0:rows, 0, t:t + 1]))
                step.done()
                lo, hi = GROUPS[g][0], GROUPS[g][-1] + 1
                A(ss[:, 0, lo:hi], ss[:, 0, lo:hi], ACT.Sqrt, bias=eps[:, :], scale=1.0 / D).then_inc(sumsq1, 1)

            def scale_x(g):
                act.wait_ge(rstd1, g + 1)
                for t in GROUPS[g]:
                    rows = TILES[t][0]
                    dst = x4n if t == 4 else xn[0:rows, XN_SLOT[t], :]
                    if t == 4:
                        act.wait_ge(vm_ready, H)
                    A(dst, x[0:rows, t, :], ACT.Copy, scale=rstd[0:rows, 0, t:t + 1]).then_inc(xs_ready, 1)

            def spread_T(name, t, half, gain):
                rows, col, _ = TILES[t]
                job = (name, t, half)
                filled(act, job)
                if gain:
                    for i in range(4):
                        k = 4 * half + i
                        ins = A(xnT[:, k, col:col + rows], bank(job)[:, i * 128:i * 128 + rows], ACT.Copy, scale=gmix[:, k:k + 1])
                else:
                    ins = A(xnT[:, 4 * half:4 * half + 4, col:col + rows],
                            bank(job)[:, :].rearrange("p (i n) -> p i n", i=4)[:, :, 0:rows], ACT.Copy)
                ins.then_inc(free(job), 1)

            def inputs(g):
                n = WIDTH[g]
                scale_x(g)
                if g == 0:
                    act.wait_ge(ld_small, 16 * 11)
                for t in GROUPS[g]:
                    for half in range(2):
                        spread_T("xT", t, half, True)
                for at, (kind, bias) in enumerate((("gate_i", bi), ("gate_f", bf))):
                    job = (kind, g)
                    filled(act, job)
                    A(rowsIF[:, at, 0:n], bank(job)[0:H, 0:n], ACT.Identity, bias=bias[:, :]).then_inc(free(job), 1)
                if g == 0:
                    log_rows(0)
                if g == 1:
                    act.wait_ge(hist_ready, 1)
                input_chunks(g, range(PAUSE))

            def log_rows(g):
                n = WIDTH[g]
                act.wait_ge(neg_f, g + 1)
                step(A(lf[:, 0:n], lf[:, 0:n], ACT.Exp))
                step.done()
                A(lf[:, 0:n], lf[:, 0:n], ACT.Ln, bias=1.0).then_inc(log_f, 1)

            def input_chunks(g, chunks):
                n = WIDTH[g]
                for i in chunks:
                    kind, c = KINDS_IN[i]
                    if g == 1 and kind == "k" and c == 0:
                        act.wait_ge(scores_read, 2)
                    job = ("in", g, i)
                    p = bank(job)
                    filled(act, job)
                    if kind == "g":
                        ins = A(ct[:, c, 0:n], p[:, 0:n], ACT.Sigmoid)
                    elif kind == "a" and g == 0:
                        step(A(us[:, c, :, HIST:], p[:, 0:NS].rearrange("p (b t) -> p b t", t=NT), ACT.Copy))
                        ins = A(up[:, c, HIST:HIST + 128], p[:, NS:n], ACT.Copy)
                    elif kind == "a":
                        ins = A(up[:, c, HIST:HIST + n], p[:, 0:n], ACT.Copy)
                    elif kind == "k":
                        ins = A(kT[:, c, 0:n], p[:, 0:n], ACT.Copy, scale=128 ** -0.5)
                    elif kind == "q" and g == 0:
                        step(A(qm[c].rearrange("p (b w) -> p b w", b=NB)[:, :, 0:NT],
                               p[:, 0:NS].rearrange("p (b t) -> p b t", t=NT), ACT.Copy))
                        ins = A(qT[:, c, 0:n], p[:, 0:n], ACT.Copy)
                    elif kind == "q":
                        ins = A(qT[:, c, 0:n], p[:, 0:n], ACT.Copy)
                    elif kind == "o":
                        ins = A(sigo[:, c, 0:n], p[:, 0:n], ACT.Sigmoid)
                    elif g == 0:
                        step(A(v[0:NS, 0, c, :], p[0:NS, 0:128], ACT.Copy))
                        ins = A(v[:, 1, c, :], p[:, 128:256], ACT.Copy)
                    else:
                        ins = A(v[:, 0:3, c, :], p[:, 0:384].rearrange("p (t e) -> p t e", t=3), ACT.Copy)
                    ins.then_inc(free(job), 1)

            def exp_rows(t):
                rows = TILES[t][0]
                nb = NB if t == 0 else 1
                act.wait_ge(rows_set, t + 1)
                step(A(R[:, 3:6, 0:rows], R[:, 3:6, 0:rows], ACT.Exp))
                A(decR[:, 0:nb], decR[:, 0:nb], ACT.Exp).then_inc(rows_exp, 1)

            def mixer(g):
                n = WIDTH[g]
                for c in range(CC):
                    act.wait_ge(centred, CC * g + c + 1)
                    A(ct[:, c, 0:n], cv[:, c, 0:n], ACT.Square).then_inc(squared, 1)
                for c in range(CC):
                    job = ("var", g, c)
                    filled(act, job)
                    A(ct[:, c, 0:n], bank(job)[:, 0:n], ACT.Sqrt, bias=eps[:, :]).then_inc(free(job), 1)
                for c in range(CC):
                    act.wait_ge(normed, CC * g + c + 1)
                    A(mixT[:, CC + c, 0:n], cv[:, c, 0:n], ACT.Silu, bias=gnb[:, c:c + 1], scale=gng[:, c:c + 1]).then_inc(mix_c, 1)
                for t in GROUPS[g]:
                    rows = TILES[t][0]
                    act.wait_ge(att_e, t + 1)
                    for h in range(H):
                        ins = A(att[0:rows, h, 0:rows], att[0:rows, h, 0:rows], ACT.Exp, bias=cols[0:rows, 0, h:h + 1])
                    ins.then_inc(att_w, 1)
                    if t + 1 in GROUPS[g]:
                        exp_rows(t + 1)
                for t in GROUPS[g]:
                    rows = TILES[t][0]
                    evacuated(act, ("out", g, N_OUT - 1))
                    evacuated(act, ("out", g, N_OUT - 2))
                    if t == 4:
                        act.wait_ge(u_free, U_SLOTS + N_PICK[0])
                    step(A(xn[0:rows, XN_SLOT[t], :], x[0:rows, t, :], ACT.Square, accum_out=ss[0:rows, 1, t:t + 1]))
                    step.done()
                    A(ss[0:rows, 1, t:t + 1], ss[0:rows, 1, t:t + 1], ACT.Sqrt, bias=eps[0:rows, :], scale=1.0 / D).then_inc(sumsq2, 1)

            def queries(g):
                n = WIDTH[g]
                for t in GROUPS[g]:
                    for half in range(2):
                        spread_T("x2T", t, half, False)
                for pair in range(0, QC, 2):
                    for c in (pair, pair + 1):
                        job = ("query", g, c)
                        filled(act, job)
                        A(qry[:, c % 2, 0:n], bank(job)[:, 0:n], ACT.Copy).then_inc(free(job), 1)
                    for c in (pair, pair + 1):
                        job = ("score", g, c)
                        filled(act, job)
                        if g == 0:
                            part = slice(c // 4 * NS, (c // 4 + 1) * NS)
                            step(A(score[part, 0, c % 4, :], bank(job)[part, 0:128], ACT.Copy))
                            ins = A(score[:, 1, c, :], bank(job)[:, 128:256], ACT.Copy)
                        else:
                            ins = A(score[:, 0:3, c, :], bank(job)[:, 0:384].rearrange("p (t k) -> p t k", t=3), ACT.Copy)
                        ins.then_inc(free(job), 1)

            def gates(t):
                n = N_PICK[t]
                s = sub[:, t % 2, 0:n]
                act.wait_ge(u_free, U_SLOTS + FIRST_PICK[t] + n)
                step(A(s, s, ACT.Exp))
                A(dots[:, t % 2, 0:n], dots[:, t % 2, 0:n], ACT.Gelu).then_inc(z_act, 1)

            def diagonals(t):
                src = fold if t == 0 else ident
                w = NS if t == 0 else 128
                first = FIRST_PICK[t]
                act.wait_ge(z_ready, t + 1)
                turn = LAST_PE if t == 4 else BLOCK
                with act.Fori(0, pe_picks(t) // turn) as i:
                    for r in range(turn):
                        pick = r + r // 3 if t == 4 else r
                        act.wait_ge(v_done, i * turn + (first + r + 1))
                        A(diag[:, r % V_SLOTS, 0:w], src[:, 0:w], ACT.Copy,
                          scale=z[:, t % 2, ds(i * (16 if t == 4 else BLOCK) + pick, 1)]).then_inc(diag_ready, 1)

            def final(t):
                rows = TILES[t][0]
                act.wait_ge(v_done, V_SLOTS + FIRST_PICK[t] + pe_picks(t))
                if t == 4:
                    act.wait_ge(last_sum, 1)
                src = acc if t == 4 else yps
                step(A(x[0:rows, t, :], src[0:rows, :], ACT.Square, accum_out=ss[0:rows, 2, t:t + 1]))
                step.done()
                A(ss[0:rows, 2, t:t + 1], ss[0:rows, 2, t:t + 1], ACT.Sqrt, bias=eps[0:rows, :], scale=1.0 / D).then_inc(sumsq3, 1)

            act.wait_ge(consts, N_CONST)
            norm1(0)
            inputs(0)
            exp_rows(0)
            input_chunks(0, range(PAUSE, N_IN))
            mixer(0)
            norm1(1)
            queries(0)
            inputs(1)
            gates(0)
            log_rows(1)
            diagonals(0)
            final(0)
            exp_rows(2)
            input_chunks(1, range(PAUSE, N_IN))
            mixer(1)
            queries(1)
            gates(1)
            for t in range(1, 5):
                diagonals(t)
                if t < 4:
                    gates(t + 1)
                final(t)

        @block.vector
        def _(dve):
            step = Steps(dve, s_dve)

            def bc(ap, axis, shape):
                return ap.unsqueeze(axis).broadcast_to(shape)

            def conv(g, chunks):
                if g == 0:
                    parts = [(us, slice(0, NS), True), (up, slice(NS, WIDTH[0]), False)]
                else:
                    parts = [(up, slice(0, GMAX), False)]
                for j in range(TAPS):
                    for c in chunks:
                        for src, span, sample in parts:
                            out = cv[:, c, span]
                            if sample:
                                win = src[:, c, :, j:j + NT]
                                out = out.rearrange("p (b t) -> p b t", t=NT)
                            else:
                                win = src[:, c, j:j + span.stop - span.start]
                            if j == 0:
                                step(dve.tensor_scalar(out, win, wdw[:, c, 0:1], bdw[:, c:c + 1], ALU.mult, ALU.add))
                            else:
                                step.done(but=len(parts) * len(chunks) - 1)
                                step(dve.scalar_tensor_tensor(out=out, in0=win, scalar=wdw[:, c, j:j + 1], in1=out,
                                                              op0=ALU.mult, op1=ALU.add))
                if chunks[-1] == CC - 1:
                    step.done()
                    dve.nop(nofuse=True).then_inc(conv_done, 1)

            def root1(g):
                dve.wait_ge(sumsq1, g + 1)
                lo, hi = GROUPS[g][0], GROUPS[g][-1] + 1
                dve.reciprocal(rstd[:, 0, lo:hi], ss[:, 0, lo:hi]).then_inc(rstd1, 1)

            def mixer_first(g):
                n = WIDTH[g]
                evacuated(dve, ("gate_f", g))
                evacuated(dve, ("gate_i", g))
                dve.scalar_tensor_tensor(out=lf[:, 0:n], in0=rowsIF[:, 1, 0:n], scalar=-1.0, in1=rowsIF[:, 1, 0:n],
                                         op0=ALU.mult, op1=ALU.min).then_inc(neg_f, 1)
                dve.wait_ge(log_f, g + 1)
                step(dve.scalar_tensor_tensor(out=rowsIF[:, 1, 0:n], in0=rowsIF[:, 1, 0:n], scalar=0.0, in1=lf[:, 0:n],
                                              op0=ALU.min, op1=ALU.subtract))
                step.done()
                rows_of(GROUPS[g][0])
                for i, chunks in enumerate(CONV_RUNS[g]):
                    run = slice(chunks[0], chunks[-1] + 1)
                    last = 2 * chunks[-1] + 1
                    evacuated(dve, ("in", g, last))
                    evacuated(dve, ("in", g, last - 1))
                    if g == 0:
                        step(dve.tensor_tensor(us[:, run, :, HIST:], us[:, run, :, HIST:],
                                               ct[:, run, 0:NS].rearrange("p c (b t) -> p c b t", t=NT), ALU.mult))
                        dve.tensor_tensor(up[:, run, HIST:HIST + 128], up[:, run, HIST:HIST + 128], ct[:, run, NS:n],
                                          ALU.mult).then_inc(u_ready, 1)
                    else:
                        dve.tensor_tensor(up[:, run, HIST:HIST + n], up[:, run, HIST:HIST + n], ct[:, run, 0:n],
                                          ALU.mult).then_inc(u_ready, 1)
                    dve.wait_ge(u_ready, len(CONV_RUNS[0]) * g + i + 1)
                    step.done()
                    conv(g, chunks)

            def group_norm(g):
                n = WIDTH[g]
                for c in range(CC):
                    job = ("mean", g, c)
                    filled(dve, job)
                    step(dve.tensor_tensor(cv[:, c, 0:n], cv[:, c, 0:n], bank(job)[:, 0:n], ALU.subtract))
                    step.done()
                    dve.nop(nofuse=True).then_inc(centred, 1)
                    dve.nop(nofuse=True).then_inc(free(job), 1)
                for c in range(CC):
                    evacuated(dve, ("var", g, c))
                    step(dve.reciprocal(ct[:, c, 0:n], ct[:, c, 0:n]))
                    step.done()
                    dve.tensor_tensor(cv[:, c, 0:n], cv[:, c, 0:n], ct[:, c, 0:n], ALU.mult).then_inc(normed, 1)

            def rows_of(t):
                rows, col, g = TILES[t]
                b, gg, M, gx = (R[:, i, 0:rows] for i in (0, 1, 2, 6))
                span = slice(col, col + rows)
                sample = t == 0
                bt = (lambda ap: ap.rearrange("p (b t) -> p b t", t=NT))
                step(dve.tensor_tensor_scan(b, keepS[:, :] if sample else ones[0:4, :].broadcast_to([4, rows]), rowsIF[:, 1, span], 0.0,
                                            ALU.mult, ALU.add))
                step.done()
                step(dve.tensor_tensor(gg, rowsIF[:, 0, span], b, ALU.subtract))
                step.done()
                if sample:
                    step(dve.tensor_copy(gx, gg))
                    step.done()
                    first = bt(gx)[:, :, 0:1]
                    step(dve.tensor_tensor(first, first, m0[:, :].unsqueeze(2), ALU.max))
                    step.done()
                    step(dve.tensor_tensor_scan(M, dropS[:, :], gx, NEG, ALU.add, ALU.max))
                    step.done()
                    last = bt(M)[:, :, NT - 1:NT]
                    lastb = bt(b)[:, :, NT - 1:NT]
                    step(dve.tensor_copy(mlast[:, :].unsqueeze(2), last))
                    step.done()
                    carried = bc(m0[:, :], 2, [4, NB, NT])
                    step(dve.tensor_tensor(bt(R[:, 3, 0:rows]), carried, bt(M), ALU.subtract))
                    step(dve.tensor_tensor(bt(R[:, 5, 0:rows]), bt(gg), bc(mlast[:, :], 2, [4, NB, NT]), ALU.subtract))
                    step(dve.tensor_tensor(decR[:, :], m0[:, :], mlast[:, :], ALU.subtract))
                    step.done()
                    step(dve.tensor_tensor(m0[:, :].unsqueeze(2), last, lastb, ALU.add))
                else:
                    step(dve.tensor_tensor_scan(M, zero[:, :].broadcast_to([4, rows]), gg, mprev[:, :], ALU.add, ALU.max))
                    step.done()
                    step(dve.tensor_scalar(R[:, 3, 0:rows], M, -1.0, mprev[:, :], ALU.mult, ALU.add))
                    step(dve.tensor_scalar(R[:, 5, 0:rows], gg, M[:, rows - 1:rows], None, ALU.subtract))
                    step(dve.tensor_tensor(decR[:, 0:1], mprev[:, :], M[:, rows - 1:rows], ALU.subtract))
                    step.done()
                    step(dve.tensor_tensor(mprev[:, :], M[:, rows - 1:rows], b[:, rows - 1:rows], ALU.add))
                dve.scalar_tensor_tensor(out=R[:, 4, 0:rows], in0=M, scalar=-1.0, in1=b, op0=ALU.mult,
                                         op1=ALU.subtract).then_inc(rows_set, 1)

            def attention(t):
                rows, _, g = TILES[t]
                nb = NB if t == 0 else 1
                full = [rows, H, 128]
                if t >= 1:
                    evacuated(dve, ("hT", t - 1))
                dve.wait_ge(att_in, t + 1)
                step(dve.tensor_copy(cols[0:rows, :, :], pS[0:rows, 0:16].rearrange("p (k h) -> p k h", h=H)))
                step(dve.tensor_copy((decS if t == 0 else dec)[:, :], pS[:, DEC:DEC + H * nb]))
                step.done()
                neg = negS if t == 0 else negP
                dve.tensor_tensor(att[0:rows, :, 0:rows], bc(neg[:, :], 1, [rows, H, rows]),
                                  pM[:, :].rearrange("p (h n) -> p h n", h=H)[0:rows, :, 0:rows], ALU.subtract).then_inc(att_e, 1)
                job = ("kTr", t)
                filled(dve, job)
                dve.tensor_tensor(kwS if t == 0 else kw[0:rows, :, :], bank(job)[0:rows, :].rearrange("p (h e) -> p h e", h=H),
                                  bc(cols[0:rows, 3, :], 2, full), ALU.mult).then_inc(free(job), 1)
                dve.wait_ge(att_w, t + 1)
                dve.tensor_tensor(att[0:rows, :, 0:rows], att[0:rows, :, 0:rows],
                                  pK[:, :].rearrange("p (h n) -> p h n", h=H)[0:rows, :, 0:rows], ALU.mult).then_inc(att_p, 1)
                if t + 1 in GROUPS[g]:
                    rows_of(t + 1)
                dve.wait_ge(att_b, t + 1)
                wi = cols[0:rows, 1, :]
                step(dve.tensor_tensor(num[0:rows, :, :], pB[0:rows, :].rearrange("p (h e) -> p h e", h=H),
                                       bc(wi, 2, full), ALU.mult))
                dve.wait_ge(att_a, t + 1)
                if t == 0:
                    step(dve.tensor_tensor(dtmp[0:rows, :, :], pS[0:rows, DB:DB + H * NB].rearrange("p (h b) -> p h b", h=H),
                                           bc(bmask[:, :], 1, [rows, H, NB]), ALU.mult))
                    step.done()
                    step(dve.tensor_reduce(den[0:rows, :], dtmp[0:rows, :, :], AX.X, ALU.add))
                    step.done()
                    step(dve.tensor_tensor(den[0:rows, :], den[0:rows, :], wi, ALU.mult))
                else:
                    step(dve.tensor_tensor(den[:, :], pS[:, DB:DB + H], wi, ALU.mult))
                step.done()
                dve.tensor_tensor(den[0:rows, :], den[0:rows, :], pS[0:rows, DA:DA + H], ALU.add).then_inc(den_read, 1)
                step(dve.tensor_tensor(num[0:rows, :, :], num[0:rows, :, :],
                                       pA[0:rows, :].rearrange("p (h e) -> p h e", h=H), ALU.add))
                dve.wait_ge(den_read, t + 1)
                step.done()
                step(dve.scalar_tensor_tensor(out=den[0:rows, :], in0=den[0:rows, :], scalar=-1.0, in1=den[0:rows, :],
                                              op0=ALU.mult, op1=ALU.max))
                step.done()
                step(dve.tensor_tensor(den[0:rows, :], den[0:rows, :], cols[0:rows, 2, :], ALU.max))
                step.done()
                step(dve.reciprocal(den[0:rows, :], den[0:rows, :]))
                step.done()
                dve.tensor_tensor(num[0:rows, :, :], num[0:rows, :, :], bc(den[0:rows, :], 2, full), ALU.mult).then_inc(hs_ready, 1)
                if t == 0:
                    gate_heads(t)
                    step.done()
                    dve.nop(nofuse=True).then_inc(att_done, 1)
                    return
                step(dve.tensor_tensor(npr[:, :], npr[:, :], dec[:, :], ALU.mult))
                step.done()
                dve.wait_ge(att_c, t)
                step(dve.tensor_tensor(npr[:, :], npr[:, :], pS[:, DN:DN + H], ALU.add))
                for h in range(H):
                    step(dve.scalar_tensor_tensor(out=Cp[:, h, :], in0=Cp[:, h, :], scalar=dec[:, h:h + 1],
                                                  in1=pC[:, h * 128:(h + 1) * 128], op0=ALU.mult, op1=ALU.add))
                gate_heads(t)
                step.done()
                dve.nop(nofuse=True).then_inc(att_done, 1)

            def gate_heads(t):
                rows, col, _ = TILES[t]
                job = ("hT", t)
                filled(dve, job)
                dve.tensor_tensor(mixT[:, 0:H, col:col + rows], bank(job)[:, :].rearrange("p (h n) -> p h n", h=H)[:, :, 0:rows],
                                  sigo[:, :, col:col + rows], ALU.mult).then_inc(free(job), 1)

            def sample_states():
                def masked(h):
                    dve.tensor_tensor(vm[h % 2][0:NS], bc(v[0:NS, 0, h, :], 1, [NS, NB, 128]),
                                      bc(bmask[:, :], 2, [NS, NB, 128]), ALU.mult).then_inc(vm_ready, 1)
                masked(0)
                for h in range(H):
                    if h + 1 < H:
                        if h >= 1:
                            dve.wait_ge(cs_new, h)
                        masked(h + 1)
                    dh = decS[:, h * NB:(h + 1) * NB]
                    step(dve.tensor_tensor(Cs[:, h, :, :], Cs[:, h, :, :], bc(dh, 2, [128, NB, 128]), ALU.mult))
                    step(dve.tensor_tensor(nsm[:, h, :], nsm[:, h, :], dh, ALU.mult))
                    step.done()
                    dve.wait_ge(cs_new, h + 1)
                    step(dve.tensor_tensor(nsm[:, h, :], nsm[:, h, :], pS[:, DN + h * NB:DN + (h + 1) * NB], ALU.add))
                    dve.tensor_tensor(Cs[:, h, :, :].rearrange("p b e -> p (b e)"),
                                      Cs[:, h, :, :].rearrange("p b e -> p (b e)"), yps[:, :], ALU.add).then_inc(cs_added, 1)

            def residual(g, j):
                job = ("out", g, j)
                filled(dve, job)
                span = slice(j * 128, (j + 1) * 128)
                if g == 0:
                    step(dve.tensor_tensor(x[0:NS, 0, span], x[0:NS, 0, span], bank(job)[0:NS, 0:128], ALU.add))
                    ins = dve.tensor_tensor(x[:, 1, span], x[:, 1, span], bank(job)[:, 128:256], ALU.add)
                else:
                    ins = dve.tensor_tensor(x[:, 2:5, span], x[:, 2:5, span],
                                            bank(job)[:, 0:384].rearrange("p (t e) -> p t e", t=3), ALU.add)
                ins.then_inc(free(job), 1)

            def norm2(t):
                rows = TILES[t][0]
                dve.wait_ge(sumsq2, t + 1)
                step(dve.reciprocal(rstd[0:rows, 1, t:t + 1], ss[0:rows, 1, t:t + 1]))
                step.done()
                if t == 0:
                    dve.wait_ge(ld_gains, 16)
                dve.scalar_tensor_tensor(out=xn[0:rows, XN_SLOT[t], :], in0=x[0:rows, t, :], scalar=rstd[0:rows, 1, t:t + 1],
                                         in1=gain[0:rows, :], op0=ALU.mult, op1=ALU.mult).then_inc(xn_ready, 1)

            def top_lists(t, part):
                g = TILES[t][2]
                s = score[:, t - GROUPS[g][0]]
                chunks = range(4 * part, 4 * part + 4)
                last = chunks[-1] if t else QC - 1
                evacuated(dve, ("score", g, last))
                evacuated(dve, ("score", g, last - 1))
                topu = topi.bitcast(u32)
                for half in range(2):
                    k = slice(8 * half, 8 * half + 8)
                    for c in chunks:
                        step(dve.max(topv[:, c, k], s[:, c, :]))
                    step.done()
                    for c in chunks:
                        step(dve.max_index(topu[:, c, k], topv[:, c, k], s[:, c, :]))
                    if half == 0:
                        step.done()
                        for c in chunks:
                            step(dve.match_replace(s[:, c, :], topv[:, c, k], s[:, c, :], LOW))
                        step.done()
                if part == 3 or t == 0:
                    step.done()
                    dve.tensor_copy(topf[:, 0:chunks[-1] + 1], topu[:, 0:chunks[-1] + 1]).then_inc(scores_read, 1)
                    dve.wait_ge(scores_read, t + 1)

            def candidates(t):
                nh = N_PICK[t] // TOPK
                first = topf.rearrange("p (h s) k -> p h s k", s=2)[:, 0:nh]
                vals = topv.rearrange("p (h s) k -> p h s k", s=2)[:, 0:nh]
                step(dve.tensor_single_scalar(first[:, :, 0, :], first[:, :, 0, :], 128.0, ALU.mult))
                step.done()
                for out, src in ((cand, vals), (ceid, first)):
                    for i, ni, nj, at in PAIRS:
                        shape = [128, nh, ni, nj]
                        dst = out[:, 0:nh, at:at + ni * nj]
                        if ni == 1:
                            step(dve.tensor_tensor(dst, src[:, :, 0, i:i + 1].broadcast_to([128, nh, nj]), src[:, :, 1, 0:nj], ALU.add))
                        elif nj == 1:
                            step(dve.tensor_tensor(dst, src[:, :, 0, i:i + ni], src[:, :, 1, 0:1].broadcast_to([128, nh, ni]), ALU.add))
                        else:
                            step(dve.tensor_tensor(dst.rearrange("p h (i j) -> p h i j", i=ni),
                                                   src[:, :, 0, i:i + ni].unsqueeze(3).broadcast_to(shape),
                                                   src[:, :, 1, 0:nj].unsqueeze(2).broadcast_to(shape), ALU.add))
                step.done()
                posu = pos.bitcast(u32)
                for half in range(2):
                    k = slice(8 * half, 8 * half + 8)
                    for h in range(nh):
                        step(dve.max(best[:, h, k], cand[:, h, :]))
                    step.done()
                    for h in range(nh):
                        step(dve.max_index(posu[:, h, k], best[:, h, k], cand[:, h, :]))
                    if half == 0:
                        step.done()
                        for h in range(nh):
                            step(dve.match_replace(cand[:, h, :], best[:, h, k], cand[:, h, :], LOW))
                        step.done()
                step.done()
                step(dve.tensor_copy(posf[:, 0:nh], posu[:, 0:nh]))
                step(dve.tensor_tensor(sub[:, t % 2, 0:N_PICK[t]].rearrange("p (h k) -> p h k", h=nh), best[:, 0:nh],
                                       best[:, 0:nh, 0:1].broadcast_to([128, nh, TOPK]), ALU.subtract))
                step.done()

            def experts_of(t, part):
                half = N_PICK[t] // TOPK // 2
                for h in range(half * part, half * (part + 1)):
                    for k in range(TOPK):
                        if h or k >= HITS:
                            step.done(but=HITS - 1)
                        step(dve.scalar_tensor_tensor(out=hit[:, k % HITS, :], in0=iota[:, :], scalar=posf[:, h, k:k + 1],
                                                      in1=ceid[:, h, :], op0=ALU.is_equal, op1=ALU.mult,
                                                      accum_out=eid[:, h * TOPK + k:h * TOPK + k + 1]))
                step.done()
                if part == 1:
                    dve.tensor_copy(idx[:, t % 3, 0:N_PICK[t]], eid[:, 0:N_PICK[t]]).then_inc(picked, 1)
                    dve.wait_ge(picked, t + 1)

            def routing(t, part):
                if part < 4:
                    top_lists(t, part)
                elif part == 4:
                    candidates(t)
                else:
                    experts_of(t, part - 5)

            def dot_products(t, lo, hi):
                first = FIRST_PICK[t]
                if t == 0:
                    dve.wait_ge(spread_x, 48)
                    dve.wait_ge(xn_ready, 1)
                with dve.Fori(lo, hi) as i:
                    for r in range(BLOCK):
                        dve.wait_ge(u_land[r], i * 16 + 16 * (first // BLOCK + 1))
                        dve.scalar_tensor_tensor(out=U[r], in0=U[r], scalar=1.0, in1=xn[:, XN_SLOT[t], :],
                                                 op0=ALU.mult, op1=ALU.mult,
                                                 accum_out=dots[:, t % 2, ds(i * BLOCK + r, 1)]).then_inc(u_free, 1)

            def half_block(t, block, half):
                first = FIRST_PICK[t] + block * BLOCK
                for r in range(4 * half, 4 * half + 4):
                    pick = block * BLOCK + r
                    dve.wait_ge(u_land[r], 16 * (first // BLOCK + 1))
                    dve.scalar_tensor_tensor(out=U[r], in0=U[r], scalar=1.0, in1=xn[:, XN_SLOT[t], :],
                                             op0=ALU.mult, op1=ALU.mult,
                                             accum_out=dots[:, t % 2, pick:pick + 1]).then_inc(u_free, 1)

            def gates(t):
                n = N_PICK[t]
                nh = n // TOPK
                s = sub[:, t % 2, 0:n].rearrange("p (h k) -> p h k", k=TOPK)
                zt = z[:, t % 2, 0:n]
                dve.wait_ge(z_act, t + 1)
                if t >= 2:
                    dve.wait_ge(diag_ready, FIRST_PICK[t - 1])
                step(dve.tensor_reduce(zsum[:, 0:nh], s, AX.X, ALU.add))
                step.done()
                step(dve.reciprocal(zsum[:, 0:nh], zsum[:, 0:nh]))
                step.done()
                step(dve.tensor_tensor(zt.rearrange("p (h k) -> p h k", k=TOPK), s, bc(zsum[:, 0:nh], 2, [128, nh, TOPK]), ALU.mult))
                step.done()
                dve.tensor_tensor(zt, zt, dots[:, t % 2, 0:n], ALU.mult).then_inc(z_ready, 1)

            def last_rows():
                dve.memset(acc, 0.0).then_inc(share, 1)
                dve.wait_ge(z_ready, 5)
                land = (FIRST_PICK[4] + N_PICK[4]) // U_SLOTS
                with dve.Fori(0, N_PICK[4] // 16) as i:
                    for r in range(LAST_DVE):
                        dve.wait_ge(u_land[r], i * 16 + 16 * (land + 1))
                        dve.wait_ge(share, i * LAST_DVE + (r + 1))
                        dve.scalar_tensor_tensor(out=acc, in0=U[r], scalar=z[:, 0, ds(i * 16 + 4 * r + 3, 1)],
                                                 in1=acc, op0=ALU.mult, op1=ALU.add).then_inc(share, 1)
                        dve.wait_ge(share, i * LAST_DVE + (r + 2))
                        dve.nop(nofuse=True).then_inc(u_free, 1)
                dve.wait_ge(v_done, V_SLOTS + FIRST_PICK[4] + pe_picks(4))
                dve.wait_ge(share, 1 + N_PICK[4] * LAST_DVE // 16)
                dve.tensor_tensor(acc, acc, yps[:, :], ALU.add).then_inc(last_sum, 1)

            def final(t):
                rows = TILES[t][0]
                dve.wait_ge(sumsq3, t + 1)
                if t == 0:
                    dve.wait_ge(ld_gains, 32)
                step(dve.reciprocal(rstd[0:rows, 2, t:t + 1], ss[0:rows, 2, t:t + 1]))
                step.done()
                src = acc if t == 4 else yps
                dve.scalar_tensor_tensor(out=x[0:rows, t, :], in0=src[0:rows, :], scalar=rstd[0:rows, 2, t:t + 1],
                                         in1=gain[0:rows, :], op0=ALU.mult, op1=ALU.mult).then_inc(y_ready, 1)

            dve.wait_ge(consts, N_CONST)
            dve.memset(credit[:, 0:1], 0.0).then_inc(u_free, U_SLOTS)
            dve.memset(credit[:, 1:2], 0.0).then_inc(v_done, V_SLOTS)
            root1(0)
            dve.wait_ge(ld_small, 16 * 11)
            mixer_first(0)
            dve.tensor_copy(up[:, :, 0:HIST], up[:, :, 128:128 + HIST]).then_inc(hist_ready, 1)
            group_norm(0)
            for t in GROUPS[0]:
                attention(t)
            for j in range(N_OUT):
                residual(0, j)
            for t in GROUPS[0]:
                norm2(t)
            sample_states()
            root1(1)
            for part in (0, 4, 5, 6):
                routing(0, part)
            for part in range(4):
                routing(1, part)
            dot_products(0, 0, N_PICK[0] // BLOCK)
            for part in range(4, 7):
                routing(1, part)
            gates(0)
            mixer_first(1)
            dot_products(1, 0, 2)
            group_norm(1)
            for i, t in enumerate(GROUPS[1]):
                attention(t)
                dot_products(1, 2 + i, 3 + i)
            for j in range(N_OUT):
                residual(1, j)
                half_block(1, 5 + j // 2, j % 2)
            for t in GROUPS[1]:
                norm2(t)
            final(0)
            dot_products(1, 9, 12)
            routing(2, 0)
            dot_products(1, 12, 14)
            routing(2, 1)
            dot_products(1, 14, 16)
            gates(1)
            for part in range(2, 7):
                routing(2, part)
            for t in range(2, 5):
                if t < 4:
                    ends = (0, 2, 3, 5, 7, 8, 10, 11)
                    for part in range(7):
                        dot_products(t, ends[part], ends[part + 1])
                        routing(t + 1, part)
                    dot_products(t, ends[-1], N_PICK[t] // BLOCK)
                else:
                    dot_products(t, 0, N_PICK[t] // BLOCK)
                gates(t)
                final(t - 1)
            last_rows()
            final(4)


def kernel(x_prompt, x_sample, state_C, state_n, state_m, state_conv, norm_mix, w_in, b_gates, w_dw, b_dw,
           gn_gain, gn_bias, w_out, norm_ffn, w_query, keys1, keys2, u_experts, v_experts, norm_final):
    import numpy as np
    import concourse.bacc as bacc
    from concourse.bass_utils import run_bass_kernel_spmd

    def chunks(w):
        k, n = w.shape
        return w.reshape(k // 128, 128, n // 128, 128).transpose(2, 1, 0, 3)

    w = H * 128
    wi = w_in[0]
    part = {"q": wi[:, 0:w], "k": wi[:, w:2 * w], "v": wi[:, 2 * w:3 * w], "o": wi[:, 3 * w:4 * w],
            "a": wi[:, 4 * w + 2 * H:4 * w + 2 * H + w], "g": wi[:, 4 * w + 2 * H + w:]}
    part = {name: chunks(p) for name, p in part.items()}
    w_all = np.concatenate([np.stack([part[kind][c] for kind, c in KINDS_IN]), chunks(w_out[0]), chunks(w_query[0])])
    chan = lambda p: p.reshape(CC, 128).T
    ins = {
        "x_sample": x_sample.reshape(NS, D), "x_prompt": x_prompt[0],
        "w_all": w_all,
        "w_gates": wi[:, 4 * w:4 * w + 2 * H].reshape(KC, 128, 2 * H).transpose(1, 0, 2),
        "b_gates": b_gates[0].reshape(2 * H, 1),
        "gain_mix": norm_mix[0].reshape(KC, 128).T,
        "w_dw": w_dw[0].reshape(TAPS, CC, 128).transpose(2, 1, 0),
        "b_dw": chan(b_dw[0]), "gn_gain": chan(gn_gain[0]), "gn_bias": chan(gn_bias[0]),
        "state_C": state_C[0].transpose(2, 1, 0, 3), "state_n": state_n[0].transpose(2, 1, 0), "state_m": state_m[0].T,
        "conv_hist": state_conv[0].reshape(NB, HIST, CC, 128).transpose(3, 2, 0, 1),
        "keys_T": np.stack([keys1[0], keys2[0]], axis=1).reshape(QC, 128, 128).transpose(2, 0, 1),
        "norm_ffn": norm_ffn[0:1], "norm_final": norm_final.reshape(1, D),
        "u_experts": u_experts[0], "v_experts": v_experts[0],
    }
    outs = {"y_p": (SEQ, D), "y_s": (NS, D), "C_p": (128, H, 128), "n_p": (128, H), "m_p": (H, 1),
            "conv_p": (128, CC, HIST), "C_s": (128, H, NB, 128), "n_s": (128, H, NB), "m_s": (H, NB),
            "conv_s": (128, CC, NB, HIST)}
    nc = bacc.Bacc("TRN2", target_bir_lowering=False, num_devices=1)
    ins = {name: np.ascontiguousarray(p) for name, p in ins.items()}
    a = {name: nc.dram_tensor(f"in_{name}", p.shape, mybir.dt.from_np(p.dtype), kind="ExternalInput").ap()
         for name, p in ins.items()}
    o = {name: nc.dram_tensor(f"out_{name}", shape, mybir.dt.float32, kind="ExternalOutput").ap()
         for name, shape in outs.items()}
    build(nc, a, o)
    res = run_bass_kernel_spmd(nc, [{f"in_{name}": p for name, p in ins.items()}], core_ids=[0]).results[0]
    r = {name: np.asarray(res[f"out_{name}"]) for name in outs}
    return (r["y_p"].reshape(1, SEQ, D), r["y_s"].reshape(NB, NT, D),
            np.ascontiguousarray(r["C_p"].transpose(1, 0, 2))[None, None],
            np.ascontiguousarray(r["n_p"].T)[None, None],
            r["m_p"].reshape(1, 1, H),
            np.ascontiguousarray(r["conv_p"].transpose(2, 1, 0)).reshape(1, 1, HIST, CC * 128),
            np.ascontiguousarray(r["C_s"].transpose(2, 1, 0, 3))[None],
            np.ascontiguousarray(r["n_s"].transpose(2, 1, 0))[None],
            np.ascontiguousarray(r["m_s"].T)[None],
            np.ascontiguousarray(r["conv_s"].transpose(2, 3, 1, 0)).reshape(1, NB, HIST, CC * 128))
```
